# Optimizing a Trainium2 kernel written in Bass

```python
import math
import jax, jax.numpy as jnp
from jax import lax
import numpy as np

D_MODEL = 2048
BATCH = 1
SEQ = 256
DEPTH = 2

CHUNK = 64
N_LEFT_CHUNKS = 8
BAND = (N_LEFT_CHUNKS + 1) * CHUNK

A_HEADS = 16
A_HEAD_DIM = 64
A_WIDTH = A_HEADS * A_HEAD_DIM
MAX_REL = 128
N_REL = 2 * MAX_REL + 1

S5_WIDTH = D_MODEL // 2
S5_GROUP = 16
S5_GROUPS = S5_WIDTH // S5_GROUP
S5_STATE = 64
DT_MIN = 0.001
DT_MAX = 0.1

C_HEADS = 16
C_HEAD_DIM = 128
C_WIDTH = C_HEADS * C_HEAD_DIM
Q_BLOCK = 128

EVEN_MIX = A_WIDTH + S5_WIDTH
W_IN_EVEN = 3 * A_WIDTH + S5_WIDTH + A_WIDTH + S5_WIDTH
W_IN_ODD = 3 * C_WIDTH + C_WIDTH + C_HEADS
N_EVEN = (DEPTH + 1) // 2
N_ODD = DEPTH // 2
EPS = 1e-6


def rmsnorm(x, g):
    xf = x.astype(jnp.float32)
    y = xf * lax.rsqrt(jnp.mean(xf * xf, axis=-1, keepdims=True) + EPS)
    return (y * g.astype(jnp.float32)).astype(x.dtype)

def chunked_relpos_attention(q, k, v, rel_bias):
    b, l, h, dh = q.shape
    nc = l // CHUNK
    qc = q.reshape(b, nc, CHUNK, h, dh)
    pad = ((0, 0), (N_LEFT_CHUNKS, 0), (0, 0), (0, 0), (0, 0))
    kc = jnp.pad(k.reshape(b, nc, CHUNK, h, dh), pad)
    vc = jnp.pad(v.reshape(b, nc, CHUNK, h, dh), pad)
    band_idx = jnp.arange(nc)[:, None] + jnp.arange(N_LEFT_CHUNKS + 1)[None, :]
    kb = jnp.take(kc, band_idx, axis=1).reshape(b, nc, BAND, h, dh)
    vb = jnp.take(vc, band_idx, axis=1).reshape(b, nc, BAND, h, dh)
    scale = 1.0 / math.sqrt(dh)
    s = jnp.einsum('bcqhd,bckhd->bhcqk', qc, kb).astype(jnp.float32) * scale
    rel = jnp.arange(CHUNK)[:, None] + N_LEFT_CHUNKS * CHUNK - jnp.arange(BAND)[None, :]
    rel_idx = jnp.clip(rel, -MAX_REL, MAX_REL) + MAX_REL
    bias = rel_bias.astype(jnp.float32)[:, rel_idx]
    key_chunk = jnp.arange(nc)[:, None] - N_LEFT_CHUNKS + jnp.arange(BAND)[None, :] // CHUNK
    valid = key_chunk >= 0
    s = s + bias[None, :, None]
    s = jnp.where(valid[None, None, :, None, :], s, -jnp.inf)
    p = jax.nn.softmax(s, axis=-1).astype(v.dtype)
    o = jnp.einsum('bhcqk,bckhd->bcqhd', p, vb)
    return o.reshape(b, l, h * dh)

def s5_ssm(u, lam_re, lam_im, log_dt, b_re, b_im, c_re, c_im, d_skip):
    bsz, l, _ = u.shape
    uf = u.astype(jnp.float32).reshape(bsz, l, S5_GROUPS, S5_GROUP)
    lr = lam_re.astype(jnp.float32)
    li = lam_im.astype(jnp.float32)
    dt = jnp.exp(log_dt.astype(jnp.float32))[:, None]
    mag = jnp.exp(lr * dt)
    ang = li * dt
    a_re = mag * jnp.cos(ang)
    a_im = mag * jnp.sin(ang)
    den = lr * lr + li * li
    nr = a_re - 1.0
    ni = a_im
    coef_re = (nr * lr + ni * li) / den
    coef_im = (ni * lr - nr * li) / den
    br = b_re.astype(jnp.float32)
    bi = b_im.astype(jnp.float32)
    bb_re = coef_re[..., None] * br - coef_im[..., None] * bi
    bb_im = coef_re[..., None] * bi + coef_im[..., None] * br
    bu_re = jnp.einsum('blgc,gpc->blgp', uf, bb_re)
    bu_im = jnp.einsum('blgc,gpc->blgp', uf, bb_im)
    a_re_t = jnp.broadcast_to(a_re, (1, l, S5_GROUPS, S5_STATE))
    a_im_t = jnp.broadcast_to(a_im, (1, l, S5_GROUPS, S5_STATE))

    def combine(e1, e2):
        ar1, ai1, xr1, xi1 = e1
        ar2, ai2, xr2, xi2 = e2
        return (ar2 * ar1 - ai2 * ai1,
                ar2 * ai1 + ai2 * ar1,
                ar2 * xr1 - ai2 * xi1 + xr2,
                ar2 * xi1 + ai2 * xr1 + xi2)

    _, _, xr, xi = lax.associative_scan(combine, (a_re_t, a_im_t, bu_re, bu_im), axis=1)
    y = (jnp.einsum('blgp,gcp->blgc', xr, c_re.astype(jnp.float32))
         - jnp.einsum('blgp,gcp->blgc', xi, c_im.astype(jnp.float32))
         + d_skip.astype(jnp.float32) * uf)
    return y.reshape(bsz, l, S5_WIDTH)

def forgetting_attention(q, k, v, log_f):
    b, l, h, dh = q.shape
    nqb = l // Q_BLOCK
    cum = jnp.cumsum(log_f, axis=1).transpose(0, 2, 1)
    qb = q.reshape(b, nqb, Q_BLOCK, h, dh).transpose(1, 0, 3, 2, 4)
    cq = cum.reshape(b, h, nqb, Q_BLOCK).transpose(2, 0, 1, 3)
    kpos = jnp.arange(l)
    scale = 1.0 / math.sqrt(dh)

    def block(args):
        qi, cqi, bi = args
        s = jnp.einsum('bhqd,bkhd->bhqk', qi, k).astype(jnp.float32) * scale
        s = s + cqi[..., None] - cum[:, :, None, :]
        qpos = bi * Q_BLOCK + jnp.arange(Q_BLOCK)
        s = jnp.where(kpos[None, :] <= qpos[:, None], s, -jnp.inf)
        p = jax.nn.softmax(s, axis=-1).astype(v.dtype)
        return jnp.einsum('bhqk,bkhd->bqhd', p, v)

    o = lax.map(block, (qb, cq, jnp.arange(nqb)))
    return o.transpose(1, 0, 2, 3, 4).reshape(b, l, h * dh)

def even_layer(x, norm_g, w_in, rel_bias, lam_re, lam_im, log_dt, b_re, b_im,
               c_re, c_im, d_skip, w_glu, b_glu, w_out):
    bsz, l, _ = x.shape
    hn = rmsnorm(x, norm_g)
    proj = hn @ w_in
    cuts = [A_WIDTH, 2 * A_WIDTH, 3 * A_WIDTH, 3 * A_WIDTH + S5_WIDTH,
            4 * A_WIDTH + S5_WIDTH]
    q, k, v, u, z_a, z_b = jnp.split(proj, cuts, axis=-1)
    shp = (bsz, l, A_HEADS, A_HEAD_DIM)
    o_a = chunked_relpos_attention(q.reshape(shp), k.reshape(shp), v.reshape(shp), rel_bias)
    o_a = o_a * jax.nn.silu(z_a)
    y = jax.nn.gelu(s5_ssm(u, lam_re, lam_im, log_dt, b_re, b_im, c_re, c_im, d_skip).astype(x.dtype))
    o_b = y * jax.nn.sigmoid(y @ w_glu + b_glu)
    o_b = o_b * jax.nn.silu(z_b)
    return x + jnp.concatenate([o_a, o_b], axis=-1) @ w_out

def odd_layer(x, norm_g, w_in, b_forget, w_out):
    bsz, l, _ = x.shape
    hn = rmsnorm(x, norm_g)
    proj = hn @ w_in
    cuts = [C_WIDTH, 2 * C_WIDTH, 3 * C_WIDTH, 4 * C_WIDTH]
    q, k, v, z, f_logit = jnp.split(proj, cuts, axis=-1)
    log_f = jax.nn.log_sigmoid((f_logit + b_forget).astype(jnp.float32))
    shp = (bsz, l, C_HEADS, C_HEAD_DIM)
    o = forgetting_attention(q.reshape(shp), k.reshape(shp), v.reshape(shp), log_f)
    o = o * jax.nn.silu(z)
    return x + o @ w_out

def first_inputs(seed: int = 0) -> dict:
    key = jax.random.key(seed)
    ks = jax.random.split(key, 20)
    f32 = jnp.float32
    x = jax.random.normal(ks[0], (BATCH, SEQ, D_MODEL), f32)
    norm_even_g = 1.0 + 0.05 * jax.random.normal(ks[1], (N_EVEN, D_MODEL), f32)
    w_in_even = jax.random.normal(ks[2], (N_EVEN, D_MODEL, W_IN_EVEN), f32) * D_MODEL ** -0.5
    rel_bias = 0.2 * jax.random.normal(ks[3], (N_EVEN, A_HEADS, N_REL), f32)
    n = jnp.arange(S5_STATE, dtype=f32)
    s5_lambda_re = -0.5 + 0.01 * jax.random.normal(ks[4], (N_EVEN, S5_GROUPS, S5_STATE), f32)
    s5_lambda_im = math.pi * n + 0.01 * jax.random.normal(ks[5], (N_EVEN, S5_GROUPS, S5_STATE), f32)
    s5_log_dt = jax.random.uniform(ks[6], (N_EVEN, S5_GROUPS), f32,
                                   math.log(DT_MIN), math.log(DT_MAX))
    s5_b_re = jax.random.normal(ks[7], (N_EVEN, S5_GROUPS, S5_STATE, S5_GROUP), f32) * (2 * S5_GROUP) ** -0.5
    s5_b_im = jax.random.normal(ks[8], (N_EVEN, S5_GROUPS, S5_STATE, S5_GROUP), f32) * (2 * S5_GROUP) ** -0.5
    s5_c_re = jax.random.normal(ks[9], (N_EVEN, S5_GROUPS, S5_GROUP, S5_STATE), f32) * (2 * S5_STATE) ** -0.5
    s5_c_im = jax.random.normal(ks[10], (N_EVEN, S5_GROUPS, S5_GROUP, S5_STATE), f32) * (2 * S5_STATE) ** -0.5
    s5_d = 0.5 * jax.random.normal(ks[11], (N_EVEN, S5_GROUPS, S5_GROUP), f32)
    w_glu = jax.random.normal(ks[12], (N_EVEN, S5_WIDTH, S5_WIDTH), f32) * S5_WIDTH ** -0.5
    b_glu = 0.02 * jax.random.normal(ks[13], (N_EVEN, S5_WIDTH), f32)
    w_out_even = jax.random.normal(ks[14], (N_EVEN, EVEN_MIX, D_MODEL), f32) * EVEN_MIX ** -0.5
    norm_odd_g = 1.0 + 0.05 * jax.random.normal(ks[15], (N_ODD, D_MODEL), f32)
    w_in_odd = jax.random.normal(ks[16], (N_ODD, D_MODEL, W_IN_ODD), f32) * D_MODEL ** -0.5
    b_forget = jax.random.uniform(ks[17], (N_ODD, C_HEADS), f32, 1.0, 4.0)
    w_out_odd = jax.random.normal(ks[18], (N_ODD, C_WIDTH, D_MODEL), f32) * C_WIDTH ** -0.5
    final_norm_g = 1.0 + 0.05 * jax.random.normal(ks[19], (D_MODEL,), f32)
    return {"x": x, "norm_even_g": norm_even_g, "w_in_even": w_in_even, "rel_bias": rel_bias,
            "s5_lambda_re": s5_lambda_re, "s5_lambda_im": s5_lambda_im, "s5_log_dt": s5_log_dt,
            "s5_b_re": s5_b_re, "s5_b_im": s5_b_im, "s5_c_re": s5_c_re, "s5_c_im": s5_c_im,
            "s5_d": s5_d, "w_glu": w_glu, "b_glu": b_glu, "w_out_even": w_out_even,
            "norm_odd_g": norm_odd_g, "w_in_odd": w_in_odd, "b_forget": b_forget,
            "w_out_odd": w_out_odd, "final_norm_g": final_norm_g}

def first_block(x, norm_even_g, w_in_even, rel_bias, s5_lambda_re, s5_lambda_im, s5_log_dt,
              s5_b_re, s5_b_im, s5_c_re, s5_c_im, s5_d, w_glu, b_glu, w_out_even,
              norm_odd_g, w_in_odd, b_forget, w_out_odd, final_norm_g):
    for layer in range(DEPTH):
        i = layer // 2
        if layer % 2 == 0:
            x = even_layer(x, norm_even_g[i], w_in_even[i], rel_bias[i], s5_lambda_re[i],
                           s5_lambda_im[i], s5_log_dt[i], s5_b_re[i], s5_b_im[i], s5_c_re[i],
                           s5_c_im[i], s5_d[i], w_glu[i], b_glu[i], w_out_even[i])
        else:
            x = odd_layer(x, norm_odd_g[i], w_in_odd[i], b_forget[i], w_out_odd[i])
    return rmsnorm(x, final_norm_g)


N_EVEN_2 = (DEPTH + 1) // 2
N_ODD_2 = DEPTH // 2
NORM_EPS = 1e-6
NEG_INF = -1e30
FORCE_SCORE = 1e30
TINY = 1e-30

D_A = D_MODEL
A_DK = 128
A_HEADS_2 = D_A // 128
A_DV = D_A // A_HEADS_2
A_QK = A_HEADS_2 * A_DK
A_CHUNK = 64

D_B = D_MODEL
B_HEADS = 16
B_DH = D_B // B_HEADS
B_KV = 4
B_HPG = B_HEADS // B_KV
B_KVW = B_KV * B_DH
CMP_LEN = 32
CMP_STRIDE = 16
SEL_LEN = 64
SEL_TOPK = 16
WIN = 512
WIN_QB = 128
SEL_QB = 32

D_RNN = 2560
RG_BLOCKS = 10
RG_BS = D_RNN // RG_BLOCKS
CONV_W = 4
RG_C = 8.0

EVEN_SIZES = (A_QK, A_QK, D_A, D_A, D_B, B_KVW, B_KVW, B_KVW, B_KVW, B_KVW, B_KVW, 3 * B_HEADS, D_B)
EVEN_IN = sum(EVEN_SIZES)
EVEN_SPLIT_AT = tuple(int(v) for v in np.cumsum(EVEN_SIZES)[:-1])
EVEN_MIX_2 = D_A + D_B


def rms_norm(x, w):
    xf = x.astype(jnp.float32)
    y = xf * lax.rsqrt(jnp.mean(xf * xf, axis=-1, keepdims=True) + NORM_EPS)
    return (y * w.astype(jnp.float32)).astype(x.dtype)

def alibi_slopes(n):
    return jnp.asarray(2.0 ** (-8.0 * np.arange(1, n + 1) / n), dtype=jnp.float32)

def hgrn2(q, fz, v, lb, gain):
    bsz, T, _ = q.shape
    f32 = jnp.float32
    qf = jax.nn.silu(q.astype(f32))
    fz = fz.astype(f32)
    f = lb + (1.0 - lb) * jax.nn.sigmoid(fz)
    logf = jnp.log(jnp.maximum(f, TINY))
    k = (1.0 - lb) * jax.nn.sigmoid(-fz)
    vf = v.astype(f32)
    nc = T // A_CHUNK

    def to_chunks(a, d):
        return a.reshape(bsz, nc, A_CHUNK, A_HEADS_2, d).transpose(1, 0, 3, 2, 4)

    qc, kc, gc, vc = to_chunks(qf, A_DK), to_chunks(k, A_DK), to_chunks(logf, A_DK), to_chunks(vf, A_DV)
    causal = jnp.tril(jnp.ones((A_CHUNK, A_CHUNK), dtype=bool))[None, None, :, :, None]

    def step(S, inp):
        qt, kt, gt, vt = inp
        b = jnp.cumsum(gt, axis=2)
        o_inter = jnp.einsum('bhtk,bhkv->bhtv', qt * jnp.exp(b), S)
        rel = b[:, :, :, None, :] - b[:, :, None, :, :]
        decay = jnp.exp(jnp.where(causal, rel, NEG_INF))
        att = jnp.einsum('bhtk,bhsk,bhtsk->bhts', qt, kt, decay)
        o = o_inter + jnp.einsum('bhts,bhsv->bhtv', att, vt)
        b_last = b[:, :, -1:, :]
        S = jnp.exp(b_last[:, :, 0, :])[..., None] * S + jnp.einsum('bhsk,bhsv->bhkv', kt * jnp.exp(b_last - b), vt)
        return S, o

    S0 = jnp.zeros((bsz, A_HEADS_2, A_DK, A_DV), f32)
    _, o = lax.scan(step, S0, (qc, kc, gc, vc))
    o = o.transpose(1, 0, 3, 2, 4).reshape(bsz, T, A_HEADS_2, A_DV)
    o = o * lax.rsqrt(jnp.mean(o * o, axis=-1, keepdims=True) + NORM_EPS)
    return (o.reshape(bsz, T, D_A) * gain.astype(f32)).astype(q.dtype)

def nsa(q, kc, vc, ks, vs, kw, vw, gate_logits, pe_k, w1_k, w2_k, pe_v, w1_v, w2_v):
    bsz, T, _ = q.shape
    f32 = jnp.float32
    dt = q.dtype
    scale = B_DH ** -0.5
    slopes = alibi_slopes(B_HEADS).reshape(B_KV, B_HPG)

    def heads(a, n):
        return a.reshape(bsz, T, n, B_DH).transpose(0, 2, 1, 3)

    qh = heads(q, B_HEADS).reshape(bsz, B_KV, B_HPG, T, B_DH)
    pos = np.arange(T)

    n_cmp = (T - CMP_LEN) // CMP_STRIDE + 1
    cmp_idx = np.arange(n_cmp)[:, None] * CMP_STRIDE + np.arange(CMP_LEN)[None, :]

    def compress(a, pe, w1, w2):
        blk = heads(a, B_KV)[:, :, cmp_idx] + pe
        hid = jax.nn.silu(blk.reshape(bsz, B_KV, n_cmp, CMP_LEN * B_DH) @ w1)
        return hid @ w2

    Kc = compress(kc, pe_k, w1_k, w2_k)
    Vc = compress(vc, pe_v, w1_v, w2_v)
    dist_c = pos[:, None] - cmp_idx[None, :, -1]
    mask_c = dist_c >= 0
    s = jnp.einsum('bghtd,bgnd->bghtn', qh, Kc).astype(f32) * scale - slopes[..., None, None] * dist_c.astype(np.float32)
    p_cmp = jnp.where(mask_c, jax.nn.softmax(jnp.where(mask_c, s, NEG_INF), axis=-1), 0.0)
    o_cmp = jnp.einsum('bghtn,bgnd->bghtd', p_cmp.astype(dt), Vc)

    n_slc = T // SEL_LEN
    c_start = np.arange(n_cmp) * CMP_STRIDE
    s_start = np.arange(n_slc) * SEL_LEN
    overlap = ((c_start[:, None] <= s_start[None, :] + SEL_LEN - 1) &
               (c_start[:, None] + CMP_LEN - 1 >= s_start[None, :])).astype(np.float32)
    imp = jnp.einsum('bghtn,nj->bgtj', p_cmp, overlap)
    blk = np.arange(n_slc)[None, :]
    cur = (pos // SEL_LEN)[:, None]
    valid = blk <= cur
    forced = (blk == 0) | (blk == cur) | (blk == cur - 1)
    score = jnp.where(forced, FORCE_SCORE, jnp.where(valid, imp, NEG_INF))
    topk = min(SEL_TOPK, n_slc)
    _, idx = lax.top_k(score, topk)

    Ks = heads(ks, B_KV).reshape(bsz, B_KV, n_slc, SEL_LEN, B_DH)
    Vs = heads(vs, B_KV).reshape(bsz, B_KV, n_slc, SEL_LEN, B_DH)
    nqb = T // SEL_QB
    q_blocks = qh.reshape(bsz, B_KV, B_HPG, nqb, SEL_QB, B_DH).transpose(3, 0, 1, 2, 4, 5)
    idx_blocks = idx.reshape(bsz, B_KV, nqb, SEL_QB, topk).transpose(2, 0, 1, 3, 4)
    t_blocks = jnp.arange(T).reshape(nqb, SEL_QB)
    bi = jnp.arange(bsz)[:, None, None, None]
    gi = jnp.arange(B_KV)[None, :, None, None]
    offs = jnp.arange(SEL_LEN)

    def sel_block(args):
        qb, ib, tb = args
        kg = Ks[bi, gi, ib].reshape(bsz, B_KV, SEL_QB, topk * SEL_LEN, B_DH)
        vg = Vs[bi, gi, ib].reshape(bsz, B_KV, SEL_QB, topk * SEL_LEN, B_DH)
        kpos = (ib[..., None] * SEL_LEN + offs).reshape(bsz, B_KV, SEL_QB, topk * SEL_LEN)
        d = (tb[None, None, :, None] - kpos)[:, :, None]
        sb = jnp.einsum('bghqd,bgqsd->bghqs', qb, kg).astype(f32) * scale - slopes[:, :, None, None] * d.astype(f32)
        pb = jax.nn.softmax(jnp.where(d >= 0, sb, NEG_INF), axis=-1).astype(dt)
        return jnp.einsum('bghqs,bgqsd->bghqd', pb, vg)

    o_sel = lax.map(sel_block, (q_blocks, idx_blocks, t_blocks))
    o_sel = o_sel.transpose(1, 2, 3, 0, 4, 5).reshape(bsz, B_KV, B_HPG, T, B_DH)

    n_wb = T // WIN_QB
    span = WIN + WIN_QB
    kpos_w = np.arange(n_wb)[:, None] * WIN_QB - WIN + np.arange(span)[None, :]
    kidx = np.clip(kpos_w, 0, T - 1)
    Kw = heads(kw, B_KV)[:, :, kidx]
    Vw = heads(vw, B_KV)[:, :, kidx]
    qw = qh.reshape(bsz, B_KV, B_HPG, n_wb, WIN_QB, B_DH)
    d_w = pos.reshape(n_wb, WIN_QB)[:, :, None] - kpos_w[:, None, :]
    mask_w = (d_w >= 0) & (d_w < WIN) & (kpos_w[:, None, :] >= 0)
    sw = jnp.einsum('bghnqd,bgnkd->bghnqk', qw, Kw).astype(f32) * scale - slopes[:, :, None, None, None] * d_w.astype(np.float32)
    pw = jax.nn.softmax(jnp.where(mask_w, sw, NEG_INF), axis=-1).astype(dt)
    o_win = jnp.einsum('bghnqk,bgnkd->bghnqd', pw, Vw).reshape(bsz, B_KV, B_HPG, T, B_DH)

    g = jax.nn.sigmoid(gate_logits.astype(f32)).reshape(bsz, T, B_KV, B_HPG, 3).transpose(0, 2, 3, 1, 4)
    o = (g[..., 0:1] * o_cmp.astype(f32) + g[..., 1:2] * o_sel.astype(f32) + g[..., 2:3] * o_win.astype(f32))
    return o.transpose(0, 3, 1, 2, 4).reshape(bsz, T, D_B).astype(dt)

def rglru(xb, conv_w, conv_b, w_a, b_a, w_i, b_i, lam):
    bsz, T, _ = xb.shape
    f32 = jnp.float32
    xp = jnp.pad(xb, ((0, 0), (CONV_W - 1, 0), (0, 0)))
    xc = sum(xp[:, j:j + T] * conv_w[j] for j in range(CONV_W)) + conv_b
    xg = xc.reshape(bsz, T, RG_BLOCKS, RG_BS)
    r = jax.nn.sigmoid(jnp.einsum('btnd,nde->btne', xg, w_a).reshape(bsz, T, D_RNN).astype(f32) + b_a.astype(f32))
    i = jax.nn.sigmoid(jnp.einsum('btnd,nde->btne', xg, w_i).reshape(bsz, T, D_RNN).astype(f32) + b_i.astype(f32))
    log_a = -RG_C * jax.nn.softplus(-lam.astype(f32)) * r
    a = jnp.exp(log_a)
    u = jnp.sqrt(jnp.maximum(-jnp.expm1(2.0 * log_a), 0.0)) * (i * xc.astype(f32))

    def combine(c1, c2):
        a1, b1 = c1
        a2, b2 = c2
        return a1 * a2, a2 * b1 + b2

    _, h = lax.associative_scan(combine, (a, u), axis=1)
    return h.astype(xb.dtype)

def second_inputs(seed: int = 0) -> dict:
    key = jax.random.key(seed)
    ks = jax.random.split(key, 24)
    nrm = jax.random.normal
    f32 = jnp.float32
    lo, hi = 0.9 ** (1.0 / RG_C), 0.999 ** (1.0 / RG_C)
    u = jax.random.uniform(ks[21], (N_ODD_2, D_RNN), f32, minval=lo, maxval=hi)
    return {
        'x': nrm(ks[0], (BATCH, SEQ, D_MODEL), f32),
        'norm_w': 1.0 + 0.02 * nrm(ks[1], (DEPTH, D_MODEL), f32),
        'final_norm_w': 1.0 + 0.02 * nrm(ks[2], (D_MODEL,), f32),
        'even_w_in': nrm(ks[3], (N_EVEN_2, D_MODEL, EVEN_IN), f32) * D_MODEL ** -0.5,
        'even_w_out': nrm(ks[4], (N_EVEN_2, EVEN_MIX_2, D_MODEL), f32) * EVEN_MIX_2 ** -0.5,
        'hgrn_lb_logits': 0.5 * nrm(ks[5], (N_EVEN_2, A_QK), f32),
        'hgrn_norm_w': 1.0 + 0.02 * nrm(ks[6], (N_EVEN_2, D_A), f32),
        'cmp_pe_k': 0.02 * nrm(ks[7], (N_EVEN_2, CMP_LEN, B_DH), f32),
        'cmp_w1_k': nrm(ks[8], (N_EVEN_2, CMP_LEN * B_DH, B_DH), f32) * (CMP_LEN * B_DH) ** -0.5,
        'cmp_w2_k': nrm(ks[9], (N_EVEN_2, B_DH, B_DH), f32) * B_DH ** -0.5,
        'cmp_pe_v': 0.02 * nrm(ks[10], (N_EVEN_2, CMP_LEN, B_DH), f32),
        'cmp_w1_v': nrm(ks[11], (N_EVEN_2, CMP_LEN * B_DH, B_DH), f32) * (CMP_LEN * B_DH) ** -0.5,
        'cmp_w2_v': nrm(ks[12], (N_EVEN_2, B_DH, B_DH), f32) * B_DH ** -0.5,
        'odd_w_in': nrm(ks[13], (N_ODD_2, D_MODEL, 2 * D_RNN), f32) * D_MODEL ** -0.5,
        'odd_w_out': nrm(ks[14], (N_ODD_2, D_RNN, D_MODEL), f32) * D_RNN ** -0.5,
        'rg_conv_w': nrm(ks[15], (N_ODD_2, CONV_W, D_RNN), f32) * CONV_W ** -0.5,
        'rg_conv_b': 0.01 * nrm(ks[16], (N_ODD_2, D_RNN), f32),
        'rg_w_a': nrm(ks[17], (N_ODD_2, RG_BLOCKS, RG_BS, RG_BS), f32) * RG_BS ** -0.5,
        'rg_b_a': 0.01 * nrm(ks[18], (N_ODD_2, D_RNN), f32),
        'rg_w_i': nrm(ks[19], (N_ODD_2, RG_BLOCKS, RG_BS, RG_BS), f32) * RG_BS ** -0.5,
        'rg_b_i': 0.01 * nrm(ks[20], (N_ODD_2, D_RNN), f32),
        'rg_lambda': jnp.log(u) - jnp.log1p(-u),
    }

def second_block(x, norm_w, final_norm_w, even_w_in, even_w_out, hgrn_lb_logits, hgrn_norm_w,
              cmp_pe_k, cmp_w1_k, cmp_w2_k, cmp_pe_v, cmp_w1_v, cmp_w2_v,
              odd_w_in, odd_w_out, rg_conv_w, rg_conv_b, rg_w_a, rg_b_a, rg_w_i, rg_b_i, rg_lambda):
    lb_sm = jax.nn.softmax(hgrn_lb_logits.astype(jnp.float32), axis=0)
    lb_all = jnp.cumsum(lb_sm, axis=0) - lb_sm[0]
    for layer in range(DEPTH):
        h = rms_norm(x, norm_w[layer])
        if layer % 2 == 0:
            e = layer // 2
            (a_q, a_f, a_i, a_g, b_q, b_kc, b_vc, b_ks, b_vs, b_kw, b_vw, b_gate, b_g) = jnp.split(
                h @ even_w_in[e], EVEN_SPLIT_AT, axis=-1)
            ya = hgrn2(a_q, a_f, a_i, lb_all[e], hgrn_norm_w[e]) * jax.nn.silu(a_g)
            yb = nsa(b_q, b_kc, b_vc, b_ks, b_vs, b_kw, b_vw, b_gate,
                     cmp_pe_k[e], cmp_w1_k[e], cmp_w2_k[e], cmp_pe_v[e], cmp_w1_v[e], cmp_w2_v[e]) * jax.nn.silu(b_g)
            y = jnp.concatenate([ya, yb], axis=-1) @ even_w_out[e]
        else:
            o = layer // 2
            xb, g = jnp.split(h @ odd_w_in[o], [D_RNN], axis=-1)
            hr = rglru(xb, rg_conv_w[o], rg_conv_b[o], rg_w_a[o], rg_b_a[o], rg_w_i[o], rg_b_i[o], rg_lambda[o])
            y = (hr * jax.nn.silu(g)) @ odd_w_out[o]
        x = x + y.astype(x.dtype)
    return rms_norm(x, final_norm_w)


_first_inputs = second_inputs


def second_inputs(seed=0):
    import zlib

    import numpy as np

    out = dict(_first_inputs(seed))
    spreads = {}
    factors = {'norm_w': 3.636,
     'final_norm_w': 7.632,
     'hgrn_norm_w': 19.197,
     'cmp_pe_k': 8.0,
     'cmp_w1_k': 3.317,
     'cmp_w2_k': 3.271,
     'cmp_pe_v': 39.002,
     'rg_conv_b': 10.017,
     'rg_b_a': 64.0,
     'rg_b_i': 64.0}
    for name, (base, spread) in spreads.items():
        noise = np.random.default_rng([zlib.crc32(name.encode()), seed]).standard_normal(out[name].shape)
        drawn = base * np.exp(spread * noise) if base else spread * noise
        out[name] = __import__('jax').numpy.asarray(drawn.astype(out[name].dtype))
    for name, factor in factors.items():
        out[name] = (out[name] * factor).astype(out[name].dtype)
    return out


_narrow_inputs = second_inputs


def second_inputs(seed=0):

    out = dict(_narrow_inputs(seed))
    wider = {'final_norm_w': 3.1,
     'hgrn_norm_w': 3.13,
     'cmp_pe_k': 5.22,
     'cmp_pe_v': 3.43,
     'rg_b_a': 3.76}
    for name, times in wider.items():
        mean = out[name].mean()
        out[name] = (mean + times * (out[name] - mean)).astype(out[name].dtype)
    return out


def setup_inputs(seed=0):
    out = dict(first_inputs(seed))
    for name, value in second_inputs(seed + 1).items():
        if name != "x":
            out[name + "_2"] = value
    return out


def reference(
    x, norm_even_g, w_in_even, rel_bias, s5_lambda_re, s5_lambda_im, s5_log_dt, s5_b_re,
    s5_b_im, s5_c_re, s5_c_im, s5_d, w_glu, b_glu, w_out_even, norm_odd_g, w_in_odd, b_forget,
    w_out_odd, final_norm_g, norm_w_2, final_norm_w_2, even_w_in_2, even_w_out_2,
    hgrn_lb_logits_2, hgrn_norm_w_2, cmp_pe_k_2, cmp_w1_k_2, cmp_w2_k_2, cmp_pe_v_2, cmp_w1_v_2,
    cmp_w2_v_2, odd_w_in_2, odd_w_out_2, rg_conv_w_2, rg_conv_b_2, rg_w_a_2, rg_b_a_2, rg_w_i_2,
    rg_b_i_2, rg_lambda_2,
):
    x = first_block(
        x, norm_even_g, w_in_even, rel_bias, s5_lambda_re, s5_lambda_im, s5_log_dt, s5_b_re,
        s5_b_im, s5_c_re, s5_c_im, s5_d, w_glu, b_glu, w_out_even, norm_odd_g, w_in_odd,
        b_forget, w_out_odd, final_norm_g,
    )
    return second_block(
        x, norm_w_2, final_norm_w_2, even_w_in_2, even_w_out_2, hgrn_lb_logits_2, hgrn_norm_w_2,
        cmp_pe_k_2, cmp_w1_k_2, cmp_w2_k_2, cmp_pe_v_2, cmp_w1_v_2, cmp_w2_v_2, odd_w_in_2,
        odd_w_out_2, rg_conv_w_2, rg_conv_b_2, rg_w_a_2, rg_b_a_2, rg_w_i_2, rg_b_i_2,
        rg_lambda_2,
    )


_drawn_inputs = setup_inputs


def setup_inputs(seed=0):
    import zlib

    import numpy as np

    out = dict(_drawn_inputs(seed))
    spreads = {}
    factors = {'norm_even_g': 3.808,
     's5_lambda_re': 64.0,
     's5_lambda_im': 33.88,
     's5_log_dt': 34.128,
     's5_b_re': 47.48,
     's5_b_im': 48.336,
     's5_c_re': 47.368,
     's5_c_im': 48.808,
     'w_glu': 3.265,
     'b_glu': 33.26,
     'norm_odd_g': 8.0}
    for name, (base, spread) in spreads.items():
        noise = np.random.default_rng([zlib.crc32(name.encode()), seed]).standard_normal(out[name].shape)
        drawn = base * np.exp(spread * noise) if base else spread * noise
        out[name] = __import__('jax').numpy.asarray(drawn.astype(out[name].dtype))
    for name, factor in factors.items():
        out[name] = (out[name] * factor).astype(out[name].dtype)
    return out
```

```python
from contextlib import ExitStack
import math

import numpy as np
import concourse.bass as bass
from concourse import mybir

F32 = mybir.dt.float32
U32 = mybir.dt.uint32
ALU = mybir.AluOpType
ACT = mybir.ActivationFunctionType
AX_X = mybir.AxisListType.X

P = 128
T = 256
D = 2048
KT = D // P
HALF = P
SLOTS = 7
TILES = 16
SLOT = TILES * P
CREDIT = 2

PAIRS = 8
HEADS = 16
GROUPS = 4
HPG = 4
NCMP = 15
CMP_LEN, CMP_STRIDE = 32, 16
RGB = 10
CHUNK = 64
LEVELS = 7
LEVEL_BANKS = (2, 3, 6, 7)
LEVEL_ORDER = (LEVELS,) + tuple(range(LEVELS))
EPS = 1e-6
NEG = -1e30
FAR = -1e34
TINY = 1e-30
SPLIT = 2.0 ** -30
ROUND = 1.5 * 2.0 ** 23
TWO_PI = 2 * math.pi
TURN = 6.283185
TWO_PI_HI = 6.28125
TWO_PI_LO = TWO_PI - TWO_PI_HI
PI_IN = 3.1415925
GELU_C = 0.044715
GELU_S = math.sqrt(2.0 / math.pi)
ds = bass.ds


def columns(spec):
    out, at = {}, 0
    for name, width in spec:
        out[name] = (at, width)
        at += width
    return out, at


PARAMS, N_PARAMS = columns([
    ("g_even", KT), ("g_odd", KT), ("g_final", KT), ("g_even2", KT), ("g_odd2", KT), ("g_final2", KT),
    ("lam_re", 32), ("lam_im", 32), ("log_dt", 32), ("d_skip", PAIRS), ("b_glu", PAIRS),
    ("b_forget", 1), ("lb", HEADS), ("gain", HEADS), ("pe_k", CMP_LEN), ("pe_v", CMP_LEN),
    ("rg", RGB * 16)])
RG_COLS = dict(w=0, b=4, ba=5, bi=6, lam=7)
CONSTS, N_CONSTS = columns([
    ("ident", P), ("flip", P), ("ones", P), ("alibi", 384), ("causal", 384), ("alibi_c", 2 * NCMP),
    ("seen_c", 2 * NCMP), ("slopes", HEADS), ("time", T), ("level", (LEVELS + 1) * P),
    ("chunk", T), ("eps", 1)])


class Steps:

    def __init__(self, eng, sem):
        self.eng, self.sem = eng, sem
        self.base, self.n, self.i, self.per = 0, 0, 0, 0

    def mark(self, instruction):
        instruction.then_inc(self.sem, 1)
        self.n += 1
        return instruction

    def settle(self):
        self.eng.wait_ge(self.sem, self.base + self.i * self.per + self.n)

    def enter(self, i, per):
        self.base, self.n, self.i, self.per = self.base + self.n, 0, i, per

    def leave(self, times):
        assert self.n == self.per, f"{self.sem}: {self.n} steps per turn, not {self.per}"
        self.base, self.n, self.i, self.per = self.base + times * self.per, 0, 0, 0


class Load:

    def __init__(self, slot, src, width, freed, others=0):
        self.slot, self.src, self.width, self.freed, self.others = slot, src, width, freed, others


class Phase:

    def __init__(self, turns, units, loads):
        self.turns, self.units, self.loads = turns, units, loads


def plan(phases):
    units = 0
    landed = [0] * SLOTS
    last = [0] * SLOTS
    for ph in phases:
        ph.base = units
        per = [0] * SLOTS
        for ld in ph.loads:
            per[ld.slot] += 16 * (1 + ld.others)
        so_far = [0] * SLOTS
        prev = {}
        for ld in ph.loads:
            so_far[ld.slot] += 16 * (1 + ld.others)
            ld.land0 = landed[ld.slot] + so_far[ld.slot]
            ld.land_per = per[ld.slot]
            ld.free0 = ph.base + prev[ld.slot] if ld.slot in prev else last[ld.slot]
            final = [x for x in ph.loads if x.slot == ld.slot][-1].freed
            ld.free_later = (0, prev[ld.slot]) if ld.slot in prev else (-1, final)
            prev[ld.slot] = ld.freed
        for s in range(SLOTS):
            landed[s] += per[s] * ph.turns
            if s in prev:
                last[s] = ph.base + (ph.turns - 1) * ph.units + prev[s]
        units += ph.units * ph.turns
    return phases


def program(nc, a, out):
    with ExitStack() as ctx:
        def sb(name, shape, dt=F32):
            return ctx.enter_context(nc.sbuf_tensor(name, shape, dt))

        def signal(name):
            s = ctx.enter_context(nc.semaphore(name))
            signals.append(s)
            return s

        signals = []
        psum = ctx.enter_context(nc.psum_tensor("psum", [P, 8, 512], F32))
        bank = [psum[:, n, :] for n in range(8)]
        ring = sb("ring", [P, SLOTS, SLOT])
        x = sb("x", [P, KT, T])
        h = sb("h", [P, KT, T])
        mix = sb("mix", [P, 32, T])
        par = sb("par", [P, N_PARAMS])
        con = sb("con", [P, N_CONSTS])

        def pcol(name, a0=0, width=None):
            c, w = PARAMS[name]
            return par[:, c + a0:c + a0 + (w - a0 if width is None else width)]

        def ccol(name, a0=0, width=None):
            c, w = CONSTS[name]
            return con[:, c + a0:c + a0 + (w - a0 if width is None else width)]

        ident, flip, ones = ccol("ident"), ccol("flip"), ccol("ones")
        ssq = sb("ssq", [P, T])
        rstd = sb("rstd", [P, T])
        sq = sb("sq", [P, 2, T])
        uT = sb("uT", [P, T])
        qT = sb("qT", [P, T])
        kT = sb("kT", [P, T])
        kT2 = sb("kT2", [P, T])
        vN = sb("vN", [P, T])
        vN2 = sb("vN2", [P, T])
        prob = sb("prob", [P, 2, 384])
        probT = sb("probT", [P, 2, 384])
        score = sb("score", [P, 2, 384])
        near = sb("near", [P, 384])
        nmax = sb("nmax", [P, 2, 2])
        psums = sb("psums", [P, 2, 2])
        pinv = sb("pinv", [P, 2, 2])
        gate = sb("gate", [P, T])
        gz = sb("gz", [P, T])
        wide_a = sb("wide_a", [P, 8, T])
        wide_b = sb("wide_b", [P, 8, T])
        wide_c = sb("wide_c", [P, 8, T])
        w2 = sb("w2", [P, 2, T])
        w3 = sb("w3", [P, 2, T])
        w4 = sb("w4", [P, 2, T])
        w5 = sb("w5", [P, 2, T])
        w8 = sb("w8", [P, 2, T])
        w9 = sb("w9", [P, 2, T])
        nv, nt = w9[:, 0, :], w9[:, 1, :]
        w6 = sb("w6", [P, 2, 2, T])
        small = sb("small", [P, 256])
        cur = sb("cur", [P, 32])

        def tiles(name, n):
            return lambda i: a[name][ds(i, 1), n].rearrange("a p n -> (a p) n")

        even1 = Phase(PAIRS, 6, [Load(n, tiles("w_even1", n), SLOT, n + 1) for n in range(4)] +
                      [Load(6, None, 0, 6, 2)] +
                      [Load(n, tiles("w_even1", n), SLOT, n + 1) for n in range(4, 6)])
        glu = Phase(2, 4, [Load(n, tiles("w_glu", n), SLOT, 2 * n + 2) for n in range(2)])
        out1 = Phase(4, 4, [Load(2 + n, tiles("w_out1", n), SLOT, n + 1) for n in range(4)])
        forget = Phase(1, 1, [Load(6, tiles("w_forget", 0), KT * HEADS, 1)])
        odd1 = Phase(HEADS, 4, [Load(n, tiles("w_odd1", n), SLOT, n + 1) for n in range(4)])
        out2 = Phase(4, 4, [Load(3 + n, tiles("w_out2", n), SLOT, n + 1) for n in range(4)])
        hgrn = Phase(HEADS, 4, [Load(n, tiles("w_hgrn", n), SLOT, n + 1) for n in range(4)])
        gates = Phase(1, 1, [Load(4, tiles("w_gates", 0), KT * 3 * HEADS, 1)])
        cmp_in = Phase(GROUPS, 2, [Load(5 + n, tiles("w_cmp_in", n), SLOT, n + 1) for n in range(2)])
        cmp_w1 = Phase(1, 5, [Load(n, tiles("w_cmp1", n), SLOT, n + 1) for n in range(4)] +
                       [Load(4, tiles("w_cmp2", 0), 2 * P, 5)])
        nsa = Phase(GROUPS, 12, [Load(n % 6, tiles("w_nsa", n), SLOT, n + 1) for n in range(12)])
        out3 = Phase(4, 8, [Load(n % 7, tiles("w_out3", n), SLOT, n + 1) for n in range(8)])
        rg = Phase(RGB, 5, [Load(n, tiles("w_rg", n), SLOT, (1, 2, 3, 5)[n]) for n in range(4)] +
                   [Load(4, tiles("w_rgg", 0), 8 * P, 4)])
        out4 = Phase(4, 20, [Load((5 + n) % 7, tiles("w_out4", n), SLOT, 4 * n + 4) for n in range(5)])
        phases = plan([even1, glu, out1, forget, odd1, out2, hgrn, gates, cmp_in, cmp_w1, nsa, out3,
                       rg, out4])

        landed = [ctx.enter_context(nc.semaphore(f"landed{s}")) for s in range(SLOTS)]
        used = ctx.enter_context(nc.semaphore("used"))
        x_in = ctx.enter_context(nc.semaphore("x_in"))
        par_in = ctx.enter_context(nc.semaphore("par_in"))
        con_in = ctx.enter_context(nc.semaphore("con_in"))
        stored = ctx.enter_context(nc.semaphore("stored"))

        def done(ph, i, unit):
            return ph.base + i * ph.units + unit

        def wait_load(pe, ph, i, n):
            ld = ph.loads[n]
            pe.wait_ge(landed[ld.slot], ld.land0 + i * ld.land_per)

        def tile(ph, n, t):
            return ring[:, ph.loads[n].slot, t * P:(t + 1) * P]

        squares = signal("squares")
        ssq_ready = signal("ssq_ready")
        sum_ready = signal("sum_ready")
        rms_guess = signal("rms_guess")
        h_ready = signal("h_ready")
        x_added = signal("x_added")
        sq_ready = signal("sq_ready")
        x_final = signal("x_final")
        q_ready, k_ready, v_ready = signal("q_ready"), signal("k_ready"), signal("v_ready")
        s_ready = signal("s_ready")
        m_ready = signal("m_ready")
        e_ready = signal("e_ready")
        p_ready = signal("p_ready")
        pt_ready = signal("pt_ready")
        pt_used = signal("pt_used")
        o_ready, o_used = signal("o_ready"), signal("o_used")
        u_ready = signal("u_ready")
        za_tanh, za_used, zb_tanh, zb_used = (signal(n) for n in ("za_tanh", "za_used", "zb_tanh", "zb_used"))
        bias_masked = signal("bias_masked")
        s5_mid = signal("s5_mid")
        s5_act = signal("s5_act")
        s5_par = signal("s5_par")
        phase_ready, trig_ready, rot_ready = signal("phase_ready"), signal("trig_ready"), signal("rot_ready")
        rot_used = signal("rot_used")
        bu_ready, bu_used = signal("bu_ready"), signal("bu_used")
        xrot, state_ready = signal("xrot"), signal("state_ready")
        y_ready, y_used, gelu_in, gelu_t, y_mixed = (signal(n) for n in (
            "y_ready", "y_used", "gelu_in", "gelu_t", "y_mixed"))
        glu_t, glu_mixed = signal("glu_t"), signal("glu_mixed")
        f_in, f_exp, f_ln, f_cum, ck_ready = (signal(n) for n in ("f_in", "f_exp", "f_ln", "f_cum", "ck_ready"))
        z_tanh, z_used = signal("z_tanh"), signal("z_used")
        hf_in, hf_exp, hf_split, hf_ln, hb_ready = (signal(n) for n in (
            "hf_in", "hf_exp", "hf_split", "hf_ln", "hb_ready"))
        hq_tanh, hq_used, hv_ready, hg_tanh, hg_used = (signal(n) for n in (
            "hq_tanh", "hq_used", "hv_ready", "hg_tanh", "hg_used"))
        span_ready, decay_ready, w_low, w_high = (signal(n) for n in (
            "span_ready", "decay_ready", "w_low", "w_high"))
        lv_ready, lv_used, att_far, att_ready = (signal(n) for n in ("lv_ready", "lv_used", "att_far", "att_ready"))
        ho_ready, ho_sq, ho_guess, ho_norm, ht_ready, h_mixed = (signal(n) for n in (
            "ho_ready", "ho_sq", "ho_guess", "ho_norm", "ht_ready", "h_mixed"))
        gate_exp, gates_ready = signal("gate_exp"), signal("gates_ready")
        ckv_ready, cblk_ready, c_hid, c_tanh, c_silu, c_out, c_kept = (signal(n) for n in (
            "ckv_ready", "cblk_ready", "c_hid", "c_tanh", "c_silu", "c_out", "c_kept"))
        nkv_ready, near_ready, cur_kv = signal("nkv_ready"), signal("near_ready"), signal("cur_kv")
        xb_ready, xc_ready, rg_pre, rg_r, rg_a, rg_t, rg_v, rg_s, rgg_tanh, rgg_used, rg_mixed = (signal(n) for n in (
            "xb_ready", "xc_ready", "rg_pre", "rg_r", "rg_a", "rg_t", "rg_v", "rg_s", "rgg_tanh", "rgg_used",
            "rg_mixed"))
        sp_in, sp_exp = signal("sp_in"), signal("sp_exp")

        s5 = sb("s5", [P, 4, 32])
        s5t = prob[:, :, :].rearrange("p a n -> p (a n)")[:, 0:384].rearrange("p (a n) -> p a n", a=12)
        s5_pool = sb("s5_pool", [P, 4, 4])
        bgh = sb("bgh", [P, PAIRS])
        rgt = sb("rgt", [P, 6, 2 * RGB])
        nc_ = sb("neg_cum", [16, T])
        fl = wide_a[0:16, 0:4, :]
        ck = sb("ck", [16, T])
        lbt = sb("lbt", [P, 4, HEADS])
        gates_sb = sb("gates_sb", [P, 2, 3 * HEADS])
        gcur = sb("gcur", [P, 2, 3 * HPG])
        Kc = sb("Kc", [P, GROUPS * NCMP])
        Vc = sb("Vc", [16, GROUPS, P])
        kc_cur = sb("kc_cur", [P, 16])
        vc_cur = sb("vc_cur", [16, P])
        near_c = sb("near_c", [P, 2, NCMP])
        score_c = sb("score_c", [P, 2, NCMP])
        prob_c = sb("prob_c", [P, 2, NCMP])
        probT_c = sb("probT_c", [16, T])
        stat = sb("stat", [P, 4, 2, 3])
        xpad = score[:, :, 0:T + 4]

        apart_sem = ctx.enter_context(nc.semaphore("apart"))

        def apart(eng):
            eng.sem_inc(apart_sem, 1)

        step_sem = {n: ctx.enter_context(nc.semaphore(f"{n}_step")) for n in ("dve", "pool", "act")}
        block = ctx.enter_context(nc.Block())

        def after(n):
            return n + CREDIT
        @block.sync
        def _(sp):
            def fill(ph, ld, i, first):
                if ld.src is None:
                    sp.wait_ge(y_ready, after(4 * i))
                    sp.dma_start(ring[:, ld.slot, 0:512], a["s5_bc"][ds(i, 1)].rearrange("a p n -> (a p) n"))\
                        .then_inc(landed[ld.slot], 16)
                    for e in range(2):
                        rows = a["rel"][ds(2 * i + e, 1)].rearrange("a p n -> (a p) n")
                        sp.dma_start(ring[:, ld.slot, 512 + e * T:768 + e * T], rows)\
                            .then_inc(landed[ld.slot], 16)
                    return
                if first:
                    if ld.free0:
                        sp.wait_ge(used, ld.free0)
                else:
                    back, unit = ld.free_later
                    sp.wait_ge(used, ph.base + (i + back) * ph.units + unit)
                sp.dma_start(ring[:, ld.slot, 0:ld.width], ld.src(i)).then_inc(landed[ld.slot], 16)

            sp.dma_start(par[:, :], a["params"]).then_inc(par_in, 16)
            for c in range(4):
                sp.dma_start(x[:, 4 * c:4 * c + 4, :], a["xT"][4 * c:4 * c + 4].rearrange("k p t -> p k t"))\
                    .then_inc(x_in, 16)
            sp.dma_start(con[:, :], a["consts"]).then_inc(con_in, 16)
            for ph in phases:
                if ph is forget:
                    sp.wait_ge(y_ready, after(4 * PAIRS))
                for ld in ph.loads:
                    fill(ph, ld, 0, True)
                if ph.turns > 1:
                    with sp.Fori(1, ph.turns) as i:
                        for ld in ph.loads:
                            fill(ph, ld, i, False)
            for c in range(4):
                sp.wait_ge(x_final, after(4 * c + 4))
                sp.dma_start(out[4 * c:4 * c + 4].rearrange("k p t -> p k t"), x[:, 4 * c:4 * c + 4, :])\
                    .then_inc(stored, 16)
            sp.wait_ge(stored, 64)

        @block.tensor
        def _(pe):
            def product(ph, i, n, dst, k0=0, k1=KT):
                if k0 == 0:
                    wait_load(pe, ph, i, n)
                for k in range(k0, k1):
                    mm = pe.matmul(dst[:, 0:T], tile(ph, n, k), h[:, k, :], start=k == 0, stop=k == KT - 1)
                if k1 == KT:
                    mm.then_inc(used, 1)

            def values(ph, i, n, dst):
                wait_load(pe, ph, i, n)
                for tt in range(2):
                    for k in range(KT):
                        mm = pe.matmul(dst[:, tt * P:(tt + 1) * P], h[:, k, tt * P:(tt + 1) * P], tile(ph, n, k),
                                       start=k == 0, stop=k == KT - 1)
                mm.then_inc(used, 1)

            def norm(n):
                pe.wait_ge(ssq_ready, after(n + 1))
                pe.matmul(bank[7][:, 0:T], ones, ssq[:, :], start=True, stop=True).then_inc(sum_ready, 1)

            def out_proj(ph, ktiles, first_block, unit):
                with pe.Fori(0, 4) as i:
                    at = 0
                    for b in range(4):
                        pe.wait_ge(x_added, after(first_block + 4 * i + b - 1))
                        for k in range(ktiles):
                            if at % TILES == 0:
                                wait_load(pe, ph, i, at // TILES)
                            mm = pe.matmul(bank[b % 2][:, 0:T], tile(ph, at // TILES, at % TILES), mix[:, k, :],
                                           start=k == 0, stop=k == ktiles - 1)
                            at += 1
                            if at % unit == 0:
                                mm.then_inc(used, 1)

            def causal_scores(dst, keys, queries=qT):
                for c0, width, q0 in ((0, P, 0), (P, T, P)):
                    mm = pe.matmul(dst[:, c0:c0 + width], queries[:, q0:q0 + P], keys[:, 0:width],
                                   start=True, stop=True)
                return mm

            def turn_probs(dst, src):
                for c in range(3):
                    mm = pe.transpose(dst[:, c * P:(c + 1) * P], src[:, c * P:(c + 1) * P], ident)
                return mm

            pe.wait_ge(con_in, 16)
            norm(0)
            pe.wait_ge(h_ready, after(KT))
            with pe.Fori(0, PAIRS) as i:
                misc = ring[:, 6, :]

                def drive(t):
                    pe.wait_ge(bu_used, after(4 * i + t))
                    for c in range(2):
                        mm = pe.matmul(bank[6][:, c * T:(c + 1) * T], misc[32 * t:32 * t + 32, c * P:(c + 1) * P],
                                       uT[32 * t:32 * t + 32, :], start=True, stop=True)
                    mm.then_inc(bu_ready, 1)

                def read_out(t):
                    pe.wait_ge(state_ready, after(8 * i + 2 * t + 2))
                    if t == 0:
                        pe.wait_ge(y_used, after(i))
                    for c in range(2):
                        mm = pe.matmul(bank[7][32 * t:32 * t + 32, 0:T],
                                       misc[:, T + c * P + 32 * t:T + c * P + 32 * t + 32],
                                       w6[:, t % 2, c, :], start=c == 0, stop=c == 1)
                    mm.then_inc(y_ready, 1)

                def turn_head(e):
                    pe.wait_ge(p_ready, after(2 * i + e + 1))
                    pe.wait_ge(pt_used, after(2 * i + e))
                    turn_probs(bank[4], prob[:, e, :]).then_inc(pt_ready, 1)

                pe.wait_ge(za_used, after(i))
                product(even1, i, 0, bank[0])
                pe.wait_ge(zb_used, after(i))
                product(even1, i, 1, bank[1])
                pe.wait_ge(u_ready, after(i + 1))
                wait_load(pe, even1, i, 4)
                drive(0)
                product(even1, i, 2, bank[0])
                drive(1)
                pe.wait_ge(q_ready, after(i + 1))
                values(even1, i, 3, bank[1])
                pe.wait_ge(k_ready, after(i + 1))
                pe.wait_ge(bias_masked, after(i + 1))
                for e in range(2):
                    qk = slice(64 * e, 64 * e + 64)
                    bias = misc[:, 512 + e * T:768 + e * T]
                    for c0, width, q0 in ((0, P, 0), (P, T, P)):
                        dst = bank[2 + e][:, c0:c0 + width]
                        pe.matmul(dst, qT[qk, q0:q0 + P], kT[qk, 0:width], start=True, stop=False)
                        mm = pe.matmul(dst, flip, bias[:, T - width:T], start=False, stop=True)
                    mm.then_inc(s_ready, 1)
                drive(2)
                product(even1, i, 5, bank[0])
                read_out(0)
                drive(3)
                pe.wait_ge(v_ready, after(i + 1))
                product(even1, i, 6, bank[1], 0, 6)
                turn_head(0)
                read_out(1)
                product(even1, i, 6, bank[1], 6, 11)
                turn_head(1)
                product(even1, i, 6, bank[1], 11, KT)
                pe.wait_ge(o_used, after(i))
                for e in range(2):
                    pe.wait_ge(pt_used, after(2 * i + e + 1))
                    dst = bank[5][64 * e:64 * e + 64, 0:T]
                    pe.matmul(dst, vN[:, 64 * e:64 * e + 64], probT[:, e, 0:T], start=True, stop=False)
                    mm = pe.matmul(dst[:, P:T], vN[:, P + 64 * e:P + 64 * e + 64], probT[:, e, T:T + P],
                                   start=False, stop=True)
                mm.then_inc(o_ready, 1)
                read_out(2)
                read_out(3)
            pe.wait_ge(y_mixed, after(PAIRS))
            pe.wait_ge(za_used, after(PAIRS))
            pe.wait_ge(zb_used, after(PAIRS))
            with pe.Fori(0, 2) as i:
                for b in range(4):
                    pe.wait_ge(glu_t, after(4 * i + b - 1))
                    if b % 2 == 0:
                        wait_load(pe, glu, i, b // 2)
                    for k in range(8):
                        mm = pe.matmul(bank[b % 2][:, 0:T], tile(glu, b // 2, 8 * (b % 2) + k), mix[:, 16 + k, :],
                                       start=k == 0, stop=k == 7)
                    mm.then_inc(used, 1)
            pe.wait_ge(glu_mixed, after(PAIRS))
            pe.wait_ge(o_used, after(PAIRS))
            out_proj(out1, 16, 0, 16)
            norm(1)
            pe.wait_ge(h_ready, after(2 * KT))
            wait_load(pe, forget, 0, 0)
            for k in range(KT):
                mm = pe.matmul(bank[6][0:HEADS, 0:T], ring[:, 6, k * HEADS:(k + 1) * HEADS], h[:, k, :],
                               start=k == 0, stop=k == KT - 1)
            mm.then_inc(used, 1)
            with pe.Fori(0, HEADS) as i:
                pe.wait_ge(q_ready, after(PAIRS + i))
                pe.wait_ge(v_ready, after(PAIRS + i))
                product(odd1, i, 0, bank[0])
                pe.wait_ge(z_used, after(i))
                product(odd1, i, 1, bank[1])
                pe.wait_ge(q_ready, after(PAIRS + i + 1))
                values(odd1, i, 2, bank[0])
                pe.wait_ge(k_ready, after(PAIRS + i + 1))
                pe.wait_ge(ck_ready, after(i + 1))
                for c0, width, q0 in ((0, P, 0), (P, T, P)):
                    dst = bank[2][:, c0:c0 + width]
                    pe.matmul(dst, qT[:, q0:q0 + P], kT[:, 0:width], start=True, stop=False)
                    mm = pe.matmul(dst, ones[0:16, :], ck[:, 0:width], start=False, stop=True)
                mm.then_inc(s_ready, 1)
                product(odd1, i, 3, bank[1], 0, 9)
                pe.wait_ge(p_ready, after(2 * PAIRS + i + 1))
                turn_probs(bank[4], prob[:, 0, :]).then_inc(pt_ready, 1)
                product(odd1, i, 3, bank[1], 9, KT)
                pe.wait_ge(pt_used, after(2 * PAIRS + i + 1))
                pe.wait_ge(v_ready, after(PAIRS + i + 1))
                pe.wait_ge(o_used, after(PAIRS + i))
                pe.matmul(bank[5][:, 0:T], vN[:, 0:P], probT[:, 0, 0:T], start=True, stop=False)
                pe.matmul(bank[5][:, P:T], vN[:, P:T], probT[:, 0, T:T + P], start=False, stop=True)\
                    .then_inc(o_ready, 1)
            pe.wait_ge(o_used, after(PAIRS + HEADS))
            out_proj(out2, 16, 16, 16)
            norm(2)
            norm(3)
            pe.wait_ge(h_ready, after(4 * KT))
            with pe.Fori(0, HEADS) as i:
                kk, qs = w9[:, 0, :], w9[:, 1, :]

                def level(pos, lv):
                    pe.wait_ge(lv_used, after(8 * i + max(pos - 3, 0)))
                    dst = bank[LEVEL_BANKS[pos % 4]][:, 0:T]
                    for b in range(2):
                        cols = slice(b * P, (b + 1) * P)
                        if lv < LEVELS:
                            mm = pe.matmul(dst[:, cols], wide_b[:, lv, cols], wide_b[:, lv, cols],
                                           start=True, stop=True)
                        else:
                            mm = pe.matmul(dst[:, cols], kk[:, cols], qs[:, cols], start=True, stop=True)
                    mm.then_inc(lv_ready, 1)

                pe.wait_ge(hv_ready, after(i))
                product(hgrn, i, 0, bank[0])
                pe.wait_ge(hg_used, after(i))
                product(hgrn, i, 1, bank[1])
                pe.wait_ge(hf_in, after(i + 1))
                values(hgrn, i, 2, bank[0])
                pe.wait_ge(hq_used, after(i + 1))
                product(hgrn, i, 3, bank[1], 0, 4)
                pe.wait_ge(w_low, after(i + 1))
                for pos, lv in enumerate(LEVEL_ORDER[0:5]):
                    level(pos, lv)
                product(hgrn, i, 3, bank[1], 4, 8)
                pe.wait_ge(w_high, after(8 * i + 8))
                for pos in range(5, 8):
                    level(pos, LEVEL_ORDER[pos])
                pe.wait_ge(h_mixed, after(i))
                pe.matmul(bank[4][:, 0:P], wide_b[:, 7, 0:P], wide_b[:, 7, P:T], start=True, stop=True)\
                    .then_inc(att_far, 1)
                product(hgrn, i, 3, bank[1], 8, 12)
                pe.wait_ge(lv_used, after(8 * i + 8))
                pe.wait_ge(att_ready, after(i + 1))
                pe.wait_ge(hv_ready, after(i + 1))
                pe.matmul(bank[5][:, 0:P], small[:, 0:P], vN[:, 0:P], start=True, stop=True)
                pe.matmul(bank[5][:, P:T], small[:, P:T], vN[:, P:T], start=True, stop=False)
                pe.matmul(bank[5][:, P:T], near[:, 0:P], vN[:, 0:P], start=False, stop=True).then_inc(ho_ready, 1)
                product(hgrn, i, 3, bank[1], 12, KT)
                pe.wait_ge(ho_norm, after(i + 1))
                for tt in range(2):
                    mm = pe.transpose(bank[4][:, tt * P:(tt + 1) * P], w6[:, 0, 0, tt * P:(tt + 1) * P], ident)
                mm.then_inc(ht_ready, 1)
            pe.wait_ge(hg_used, after(HEADS))
            pe.wait_ge(h_mixed, after(HEADS))
            wait_load(pe, gates, 0, 0)
            for tt in range(2):
                for k in range(KT):
                    mm = pe.matmul(bank[6][:, tt * 48:(tt + 1) * 48], h[:, k, tt * P:(tt + 1) * P],
                                   ring[:, 4, k * 48:(k + 1) * 48], start=k == 0, stop=k == KT - 1)
            mm.then_inc(used, 1)
            with pe.Fori(0, GROUPS) as i:
                for n in range(2):
                    pe.wait_ge(ckv_ready, after(2 * i))
                    product(cmp_in, i, n, bank[n])
            for n in range(2):
                pe.wait_ge(cblk_ready, after(n + 1))
                blk = (wide_a, wide_c)[n].rearrange("p k t -> p (k t)")
                for l in range(CMP_LEN):
                    if l % TILES == 0:
                        wait_load(pe, cmp_w1, 0, 2 * n + l // TILES)
                    mm = pe.matmul(bank[2 + n][:, 0:GROUPS * NCMP], tile(cmp_w1, 2 * n + l // TILES, l % TILES),
                                   blk[:, l * GROUPS * NCMP:(l + 1) * GROUPS * NCMP], start=l == 0,
                                   stop=l == CMP_LEN - 1)
                    if l % TILES == TILES - 1:
                        mm.then_inc(used, 1)
            wait_load(pe, cmp_w1, 0, 4)
            pe.wait_ge(c_silu, after(1))
            pe.matmul(bank[4][:, 0:GROUPS * NCMP], ring[:, 4, 0:P], w2[:, 0, 0:GROUPS * NCMP], start=True, stop=True)\
                .then_inc(c_out, 1)
            pe.wait_ge(c_silu, after(2))
            for g in range(GROUPS):
                mm = pe.matmul(bank[5][0:NCMP, g * P:(g + 1) * P], w2[:, 1, g * NCMP:(g + 1) * NCMP],
                               ring[:, 4, P:2 * P], start=True, stop=True)
            mm.then_inc(used, 1)
            pe.wait_ge(c_kept, after(2))
            pe.wait_ge(ckv_ready, after(2 * GROUPS))
            q_base, o_base, g_base = PAIRS + HEADS, PAIRS + HEADS, HEADS
            s_base = 2 * PAIRS + HEADS
            with pe.Fori(0, GROUPS) as i:
                def finish(e, half):
                    n = 4 * i + e
                    if half == 0:
                        pe.wait_ge(p_ready, after(s_base + n + 1))
                        turn_probs(bank[4], prob[:, 0, :])
                        turn_probs(bank[7], prob[:, 1, :])
                        for tt in range(2):
                            mm = pe.transpose(bank[6][0:NCMP, T + tt * P:T + (tt + 1) * P], prob_c[:, tt, :], ident)
                        mm.then_inc(pt_ready, 1)
                        return
                    pe.wait_ge(pt_used, after(s_base + 2 * n + 2))
                    pe.wait_ge(cur_kv, after(2 * i + 2))
                    pe.wait_ge(o_used, after(o_base + n))
                    o = bank[5][:, 0:T]
                    pe.matmul(o, vc_cur[0:NCMP, :], probT_c[0:NCMP, :], start=True, stop=False)
                    for b, v in enumerate((vN, vN2)):
                        pe.matmul(o, v[:, 0:P], probT[:, b, 0:T], start=False, stop=False)
                        mm = pe.matmul(o[:, P:T], v[:, P:T], probT[:, b, T:T + P], start=False, stop=b == 1)
                    mm.then_inc(o_ready, 1)

                pe.wait_ge(q_ready, after(q_base + 4 * i))
                product(nsa, i, 0, bank[0])
                pe.wait_ge(z_used, after(g_base + 4 * i))
                values(nsa, i, 1, bank[1])
                pe.wait_ge(nkv_ready, after(4 * i + 1))
                product(nsa, i, 2, bank[0])
                pe.wait_ge(nkv_ready, after(4 * i + 2))
                values(nsa, i, 3, bank[1])
                for e in range(HPG):
                    n = 4 * i + e
                    pe.wait_ge(q_ready, after(q_base + n))
                    pe.wait_ge(nkv_ready, after(4 * i + 3))
                    product(nsa, i, 4 + 2 * e, bank[0])
                    if e:
                        finish(e - 1, 0)
                    pe.wait_ge(z_used, after(g_base + n))
                    pe.wait_ge(nkv_ready, after(4 * i + 4))
                    product(nsa, i, 5 + 2 * e, bank[1], 0, 6)
                    if e:
                        finish(e - 1, 1)
                    pe.wait_ge(q_ready, after(q_base + n + 1))
                    pe.wait_ge(cur_kv, after(2 * i + 2))
                    causal_scores(bank[2], kT)
                    causal_scores(bank[3], kT2)
                    for tt in range(2):
                        mm = pe.matmul(bank[6][:, tt * NCMP:(tt + 1) * NCMP], qT[:, tt * P:(tt + 1) * P],
                                       kc_cur[:, 0:NCMP], start=True, stop=True)
                    mm.then_inc(s_ready, 1)
                    product(nsa, i, 5 + 2 * e, bank[1], 6, KT)
                finish(HPG - 1, 0)
                finish(HPG - 1, 1)
            pe.wait_ge(o_used, after(o_base + HEADS))
            pe.wait_ge(h_mixed, after(HEADS))
            out_proj(out3, 32, 32, 16)
            norm(4)
            pe.wait_ge(h_ready, after(5 * KT))
            with pe.Fori(0, RGB) as i:
                pe.wait_ge(xb_ready, after(2 * i))
                product(rg, i, 0, bank[0][:, 0:T])
                product(rg, i, 1, bank[1][:, 0:T])
                pe.wait_ge(rgg_used, after(i))
                product(rg, i, 2, bank[4][:, 0:T])
                pe.wait_ge(xc_ready, after(2 * i + 2))
                wait_load(pe, rg, i, 4)
                pe.wait_ge(rg_pre, after(i))
                for g in range(2):
                    for e in range(2):
                        for c in range(2):
                            mm = pe.matmul(bank[2 + g][:, e * T:(e + 1) * T], tile(rg, 4, 4 * g + 2 * e + c),
                                           w2[:, c, :], start=c == 0, stop=c == 1)
                mm.then_inc(used, 1)
                product(rg, i, 3, bank[5][:, 0:T])
            pe.wait_ge(rg_mixed, after(RGB))
            out_proj(out4, 20, 48, 4)
            norm(5)

        @block.scalar
        def _(s):
            st = Steps(s, step_sem["act"])

            def norm(n):
                s.wait_ge(sum_ready, after(n + 1))
                st.mark(s.activation(rstd[:, :], bank[7][:, 0:T], ACT.Ln, bias=ccol("eps"), scale=1.0 / D))
                st.settle()
                s.activation(rstd[:, :], rstd[:, :], ACT.Exp, scale=-0.5).then_inc(rms_guess, 1)

            def out_squares(first_block):
                with s.Fori(0, 4) as i:
                    for b in range(4):
                        s.wait_ge(x_added, after(first_block + 4 * i + b + 1))
                        s.activation(sq[:, b % 2, :], x[:, ds(4 * i + b, 1), :].rearrange("p a t -> p (a t)"),
                                     ACT.Square).then_inc(sq_ready, 1)

            def exps(src, dst, neg, sums):
                for tt, cols in ((0, slice(0, P)), (1, slice(P, 384))):
                    ins = s.activation(dst[:, cols], src[:, cols], ACT.Exp, bias=neg[tt], accum_out=sums[tt])
                return ins

            s.wait_ge(par_in, 16)
            s.activation(s5t[:, 0, :], pcol("log_dt"), ACT.Exp).then_inc(s5_act, 1)
            s.wait_ge(s5_mid, after(1))
            s.activation(s5[:, 0, :], s5t[:, 1, :], ACT.Exp).then_inc(s5_act, 1)
            s.wait_ge(sp_in, after(1))
            st.mark(s.activation(rgt[:, 1, :], rgt[:, 0, :], ACT.Exp, scale=-1.0))
            s.activation(lbt[:, 1, :], lbt[:, 0, :], ACT.Exp).then_inc(sp_exp, 1)
            s.wait_ge(s5_mid, after(2))
            st.mark(s.activation(s5t[:, 5, :], s5t[:, 3, :], ACT.Sin))
            s.activation(s5t[:, 6, :], s5t[:, 4, :], ACT.Sin).then_inc(s5_act, 1)
            s.wait_ge(x_in, 64)
            s.activation(mix[:, 0:KT, :], x[:, :, :], ACT.Square).then_inc(squares, 1)
            s.wait_ge(con_in, 16)
            norm(0)
            turns = wide_a[:, :, :].rearrange("p (t c) n -> p t c n", c=2)
            trig = wide_c[:, :, :].rearrange("p (t c) n -> p t c n", c=2)
            with s.Fori(0, PAIRS) as i:
                s.wait_ge(used, done(even1, i, 1))
                s.wait_ge(y_used, after(i))
                s.activation(uT[:, :], bank[0][:, 0:T], ACT.Copy).then_inc(u_ready, 1)
                s.wait_ge(used, done(even1, i, 2))
                s.activation(qT[:, :], bank[1][:, 0:T], ACT.Copy, scale=64 ** -0.5).then_inc(q_ready, 1)
                s.wait_ge(phase_ready, after(i + 1))
                s.wait_ge(rot_used, after(4 * i))
                st.enter(i, 1)
                st.mark(s.activation(trig[:, :, 0, :], turns[:, :, 0, :], ACT.Sin, scale=-TURN))
                s.activation(trig[:, :, 1, :], turns[:, :, 1, :], ACT.Sin, scale=TURN).then_inc(trig_ready, 1)
                st.leave(PAIRS)
                s.wait_ge(used, done(even1, i, 3))
                s.activation(kT[:, :], bank[0][:, 0:T], ACT.Copy).then_inc(k_ready, 1)
                s.wait_ge(used, done(even1, i, 4))
                s.activation(vN[:, :], bank[1][:, 0:T], ACT.Copy).then_inc(v_ready, 1)
                for e in range(2):
                    s.wait_ge(m_ready, after(2 * i + e + 1))
                    exps(bank[2 + e], prob[:, e, :], [nmax[:, e, t:t + 1] for t in range(2)],
                         [psums[:, e, t:t + 1] for t in range(2)]).then_inc(e_ready, 1)
                s.wait_ge(used, done(even1, i, 5))
                s.activation(gate[:, :], bank[0][:, 0:T], ACT.Tanh, scale=0.5).then_inc(za_tanh, 1)
                for e in range(2):
                    s.wait_ge(pt_ready, after(2 * i + e + 1))
                    s.activation(probT[:, e, :], bank[4][:, 0:384], ACT.Copy).then_inc(pt_used, 1)
                s.wait_ge(used, done(even1, i, 6))
                s.activation(sq[:, 0, :], bank[1][:, 0:T], ACT.Tanh, scale=0.5).then_inc(zb_tanh, 1)
                s.wait_ge(gelu_in, after(i + 1))
                s.activation(sq[:, 1, :], w4[:, 1, :], ACT.Tanh, scale=GELU_S).then_inc(gelu_t, 1)
            with s.Fori(0, 2) as i:
                for b in range(4):
                    s.wait_ge(used, done(glu, i, b + 1))
                    s.wait_ge(glu_mixed, after(4 * i + b - 1))
                    s.activation(sq[:, b % 2, :], bank[b % 2][:, 0:T], ACT.Tanh, bias=bgh[:, ds(4 * i + b, 1)],
                                 scale=0.5).then_inc(glu_t, 1)
            out_squares(0)
            norm(1)
            s.wait_ge(f_in, after(1))
            st.mark(s.activation(fl[:, 2, :], fl[:, 1, :], ACT.Exp, scale=-1.0))
            st.settle()
            s.activation(fl[:, 3, :], fl[:, 2, :], ACT.Ln, bias=ccol("ones", 0, 1)[0:16, :]).then_inc(f_ln, 1)
            with s.Fori(0, HEADS) as i:
                s.wait_ge(used, done(odd1, i, 1))
                s.activation(qT[:, :], bank[0][:, 0:T], ACT.Copy, scale=P ** -0.5).then_inc(q_ready, 1)
                s.wait_ge(used, done(odd1, i, 2))
                s.activation(kT[:, :], bank[1][:, 0:T], ACT.Copy).then_inc(k_ready, 1)
                s.wait_ge(used, done(odd1, i, 3))
                s.activation(vN[:, :], bank[0][:, 0:T], ACT.Copy).then_inc(v_ready, 1)
                s.wait_ge(m_ready, after(2 * PAIRS + i + 1))
                exps(score[:, 0, :], prob[:, 0, :], [nmax[:, 0, t:t + 1] for t in range(2)],
                     [psums[:, 0, t:t + 1] for t in range(2)]).then_inc(e_ready, 1)
                s.wait_ge(pt_ready, after(2 * PAIRS + i + 1))
                s.activation(probT[:, 0, :], bank[4][:, 0:384], ACT.Copy).then_inc(pt_used, 1)
                s.wait_ge(used, done(odd1, i, 4))
                s.activation(gate[:, :], bank[1][:, 0:T], ACT.Tanh, scale=0.5).then_inc(z_tanh, 1)
            out_squares(16)
            norm(2)
            s.wait_ge(h_ready, after(3 * KT))
            s.activation(mix[:, 0:KT, :], x[:, :, :], ACT.Square).then_inc(squares, 1)
            norm(3)
            with s.Fori(0, HEADS) as i:
                st.enter(i, 4)
                s.wait_ge(hf_in, after(i + 1))
                s.activation(w2[:, 1, :], w2[:, 0, :], ACT.Exp, scale=-1.0).then_inc(hf_exp, 1)
                s.wait_ge(hf_split, after(i + 1))
                st.mark(s.activation(w8[:, 0, :], w4[:, 0, :], ACT.Ln))
                s.activation(w8[:, 1, :], w4[:, 1, :], ACT.Ln, scale=1.0 / SPLIT).then_inc(hf_ln, 1)
                s.wait_ge(used, done(hgrn, i, 2))
                s.activation(gate[:, :], bank[1][:, 0:T], ACT.Tanh, scale=0.5).then_inc(hq_tanh, 1)
                s.wait_ge(span_ready, after(20 * i + 20))
                s.activation(wide_b[:, :, :], wide_a[:, :, :], ACT.Exp).then_inc(decay_ready, 1)
                s.wait_ge(used, done(hgrn, i, 3))
                s.activation(vN[:, :], bank[0][:, 0:T], ACT.Copy).then_inc(hv_ready, 1)
                s.wait_ge(att_far, after(i + 1))
                s.activation(near[:, 0:P], bank[4][:, 0:P], ACT.Copy).then_inc(att_ready, 1)
                s.wait_ge(ho_ready, after(i + 1))
                for tt in range(2):
                    st.mark(s.activation(w6[:, 1, 0, tt * P:(tt + 1) * P], bank[5][:, tt * P:(tt + 1) * P], ACT.Square,
                                         accum_out=stat[:, 0, tt, 0:1]))
                st.settle()
                st.mark(s.activation(stat[:, 1, :, 0], stat[:, 0, :, 0], ACT.Ln, bias=ccol("eps"), scale=1.0 / P))
                st.settle()
                s.activation(stat[:, 2, :, 0], stat[:, 1, :, 0], ACT.Exp, scale=-0.5).then_inc(ho_guess, 1)
                s.wait_ge(used, done(hgrn, i, 4))
                s.wait_ge(hq_used, after(i + 1))
                s.activation(gate[:, :], bank[1][:, 0:T], ACT.Tanh, scale=0.5).then_inc(hg_tanh, 1)
                st.leave(HEADS)
            s.wait_ge(used, done(gates, 0, 1))
            s.activation(w2[:, 0, 0:96], bank[6][:, 0:96], ACT.Exp, scale=-1.0).then_inc(gate_exp, 1)
            with s.Fori(0, GROUPS) as i:
                for n in range(2):
                    s.wait_ge(used, done(cmp_in, i, n + 1))
                    s.activation(wide_b[:, ds(i + 4 * n, 1), :].rearrange("p a t -> p (a t)"), bank[n][:, 0:T],
                                 ACT.Copy).then_inc(ckv_ready, 1)
            for n in range(2):
                s.wait_ge(used, done(cmp_w1, 0, 2 * n + 2))
                s.activation(w3[:, n, 0:GROUPS * NCMP], bank[2 + n][:, 0:GROUPS * NCMP], ACT.Tanh, scale=0.5)\
                    .then_inc(c_tanh, 1)
            s.wait_ge(c_out, after(1))
            s.activation(Kc[:, :], bank[4][:, 0:GROUPS * NCMP], ACT.Copy).then_inc(c_kept, 1)
            s.wait_ge(used, done(cmp_w1, 0, 5))
            s.activation(Vc[0:NCMP, :, :], bank[5][0:NCMP, :].rearrange("p (g d) -> p g d", g=GROUPS), ACT.Copy)\
                .then_inc(c_kept, 1)
            s_base = 2 * PAIRS + HEADS
            with s.Fori(0, GROUPS) as i:
                for n, (dst, b) in enumerate(((kT, 0), (vN, 1), (kT2, 0), (vN2, 1))):
                    s.wait_ge(used, done(nsa, i, n + 1))
                    s.activation(dst[:, :], bank[b][:, 0:T], ACT.Copy).then_inc(nkv_ready, 1)

                def keep_turned(e):
                    s.wait_ge(pt_ready, after(s_base + 4 * i + e + 1))
                    s.activation(probT_c[0:NCMP, :], bank[6][0:NCMP, T:2 * T], ACT.Copy)
                    s.activation(probT[:, 0, :], bank[4][:, 0:384], ACT.Copy).then_inc(pt_used, 1)
                    s.activation(probT[:, 1, :], bank[7][:, 0:384], ACT.Copy).then_inc(pt_used, 1)

                for e in range(HPG):
                    s.wait_ge(used, done(nsa, i, 5 + 2 * e))
                    s.activation(qT[:, :], bank[0][:, 0:T], ACT.Copy, scale=P ** -0.5).then_inc(q_ready, 1)
                    if e:
                        keep_turned(e - 1)
                    s.wait_ge(m_ready, after(s_base + 4 * i + e + 1))
                    for tt in range(2):
                        s.activation(prob_c[:, tt, :], score_c[:, tt, :], ACT.Exp, bias=stat[:, 1, tt, 0:1],
                                     accum_out=stat[:, 2, tt, 0:1])
                    exps(score[:, 0, :], prob[:, 0, :], [stat[:, 1, t, 1:2] for t in range(2)],
                         [stat[:, 2, t, 1:2] for t in range(2)])
                    exps(score[:, 1, :], prob[:, 1, :], [stat[:, 1, t, 2:3] for t in range(2)],
                         [stat[:, 2, t, 2:3] for t in range(2)]).then_inc(e_ready, 1)
                    s.wait_ge(used, done(nsa, i, 6 + 2 * e))
                    s.activation(gate[:, :], bank[1][:, 0:T], ACT.Tanh, scale=0.5).then_inc(z_tanh, 1)
                keep_turned(HPG - 1)
            out_squares(32)
            norm(4)
            with s.Fori(0, RGB) as i:
                for c in range(2):
                    s.wait_ge(used, done(rg, i, c + 1))
                    s.wait_ge(xc_ready, after(2 * i))
                    s.activation(xpad[:, c, 4:T + 4], bank[c][:, 0:T], ACT.Copy).then_inc(xb_ready, 1)
                s.wait_ge(used, done(rg, i, 4))
                for c in range(2):
                    s.activation(w3[:, c, :], bank[2][:, c * T:(c + 1) * T], ACT.Exp, scale=-1.0,
                                 bias=cur[:, 8 * c + RG_COLS["ba"]:8 * c + RG_COLS["ba"] + 1])
                for c in range(2):
                    ins = s.activation(w4[:, c, :], bank[3][:, c * T:(c + 1) * T], ACT.Tanh, scale=0.5,
                                       bias=cur[:, 8 * c + RG_COLS["bi"]:8 * c + RG_COLS["bi"] + 1])
                ins.then_inc(rg_pre, 1)
                s.wait_ge(rg_r, after(i + 1))
                for func, dst in ((ACT.Exp, w8), (ACT.Tanh, w9)):
                    for c in range(2):
                        ins = s.activation(dst[:, c, :], w5[:, c, :], func,
                                           scale=cur[:, 8 * c + RG_COLS["lam"]:8 * c + RG_COLS["lam"] + 1])
                ins.then_inc(rg_a, 1)
                s.wait_ge(rg_v, after(i + 1))
                s.activation(w6[:, 0, :, :], w3[:, :, :], ACT.Sqrt, scale=0.25).then_inc(rg_s, 1)
                s.wait_ge(used, done(rg, i, 5))
                s.activation(wide_a[:, 0:2, :], psum[:, 4:6, 0:T], ACT.Tanh, scale=0.5)\
                    .then_inc(rgg_tanh, 1)
            out_squares(48)
            norm(5)

        @block.gpsimd
        def _(g):
            for sem in signals:
                g.sem_inc(sem, CREDIT)
            st = Steps(g, step_sem["pool"])
            g.wait_ge(con_in, 16)
            g.wait_ge(s5_par, after(1))
            turns = wide_a[:, :, :]
            trig = wide_c[:, :, :].rearrange("p (t c) n -> p t c n", c=2)
            tmp = wide_b[:, :, :].rearrange("p (t c) n -> p t c n", c=2)
            table = mix[:, 8:16, :].rearrange("p (t c) n -> p t c n", c=2)
            with g.Fori(0, PAIRS) as i:
                st.enter(i, 27)
                st.mark(g.tensor_copy(s5_pool[:, :, :], s5[:, :, ds(4 * i, 4)]))
                st.settle()
                g.wait_ge(trig_ready, after(i))
                apart(g)
                for t in range(4):
                    st.mark(g.tensor_scalar(turns[:, 2 * t, :], ccol("time"), s5_pool[:, 1, t:t + 1], None, ALU.mult))
                    st.mark(g.tensor_scalar(turns[:, 2 * t + 1, :], ccol("time"), s5_pool[:, 1, t:t + 1], 0.25,
                                            ALU.mult, ALU.add))
                st.settle()
                apart(g)
                st.mark(g.tensor_scalar(wide_b[:, :, :], turns, ROUND, -ROUND, ALU.add, ALU.add))
                st.settle()
                g.tensor_tensor(turns, turns, wide_b[:, :, :], ALU.subtract).then_inc(phase_ready, 1)
                g.wait_ge(trig_ready, after(i + 1))
                g.wait_ge(bu_used, after(4 * i))
                apart(g)
                for half, (cos_by, sin_by, op) in enumerate(((2, 3, ALU.subtract), (3, 2, ALU.add))):
                    for t in range(4):
                        st.mark(g.tensor_scalar(tmp[:, t, 0, :], trig[:, t, 1, :], s5_pool[:, cos_by, t:t + 1], None,
                                                ALU.mult))
                        st.mark(g.tensor_scalar(tmp[:, t, 1, :], trig[:, t, 0, :], s5_pool[:, sin_by, t:t + 1], None,
                                                ALU.mult))
                    st.settle()
                    ins = g.tensor_tensor(table[:, :, half, :], tmp[:, :, 0, :], tmp[:, :, 1, :], op)
                    if half:
                        ins.then_inc(rot_ready, 1)
                    else:
                        st.mark(ins)
                        st.settle()
                        apart(g)
                for t in range(4):
                    g.wait_ge(rot_used, after(4 * i + t + 1))
                    g.wait_ge(y_ready, after(4 * i + max(t - 1, 0)))
                    g.tensor_tensor(w6[:, t % 2, 0, :], w8[:, 0, :], w9[:, 1, :], ALU.add).then_inc(state_ready, 1)
                    g.tensor_tensor(w6[:, t % 2, 1, :], w9[:, 0, :], w8[:, 1, :], ALU.subtract).then_inc(state_ready, 1)
                st.leave(PAIRS)
            with g.Fori(0, HEADS) as i:
                b = w5[:, 1, :]
                g.wait_ge(hb_ready, after(i + 1))
                g.wait_ge(decay_ready, after(i))
                for lv in range(LEVELS - 1):
                    m = 1 << lv
                    bv = b.rearrange("p (n c m) -> p n c m", c=2, m=m)
                    dv = wide_a[:, lv, :].rearrange("p (n c m) -> p n c m", c=2, m=m)
                    ref = bv[:, :, 0, m - 1:m].to_broadcast([P, P // m, m])
                    g.tensor_tensor(dv[:, :, 0, :], ref, bv[:, :, 0, :], ALU.subtract).then_inc(span_ready, 1)
                    g.tensor_tensor(dv[:, :, 1, :], bv[:, :, 1, :], ref, ALU.subtract).then_inc(span_ready, 1)
                bv = b.rearrange("p (n c m) -> p n c m", c=2, m=CHUNK)
                dv = wide_a[:, LEVELS - 1, :].rearrange("p (n c m) -> p n c m", c=2, m=CHUNK)
                last = bv[:, :, 0, CHUNK - 1:CHUNK].to_broadcast([P, 2, CHUNK])
                g.tensor_tensor(dv[:, :, 0, :], last, bv[:, :, 0, :], ALU.subtract).then_inc(span_ready, 1)
                g.tensor_copy(dv[:, :, 1, :], bv[:, :, 1, :]).then_inc(span_ready, 1)
                far = wide_a[:, LEVELS, :]
                c64 = [slice(CHUNK * n, CHUNK * (n + 1)) for n in range(4)]
                end = [b[:, CHUNK * n + CHUNK - 1:CHUNK * (n + 1)] for n in range(4)]
                g.tensor_scalar(far[:, c64[0]], b[:, c64[0]], -1.0, end[0], ALU.mult, ALU.add).then_inc(span_ready, 1)
                g.tensor_scalar(far[:, c64[1]], b[:, c64[1]], -1.0, end[1], ALU.mult, ALU.add).then_inc(span_ready, 1)
                g.tensor_copy(far[:, c64[2]], b[:, c64[2]]).then_inc(span_ready, 1)
                g.wait_ge(span_ready, after(20 * i + 17))
                apart(g)
                g.tensor_scalar(far[:, c64[0]], far[:, c64[0]], end[1], None, ALU.add).then_inc(span_ready, 1)
                g.tensor_scalar(far[:, c64[3]], b[:, c64[3]], end[2], None, ALU.add).then_inc(span_ready, 2)
                kk, qs = w9[:, 0, :], w9[:, 1, :]
                g.wait_ge(decay_ready, after(i + 1))
                g.wait_ge(hq_used, after(i + 1))
                for lv in range(4, LEVELS + 1):
                    m = 1 << lv
                    for c, src in ((0, kk), (1, qs)):
                        dv = wide_b[:, lv, :].rearrange("p (n c m) -> p n c m", c=2, m=m)[:, :, c, :]
                        sv = src.rearrange("p (n c m) -> p n c m", c=2, m=m)[:, :, c, :]
                        g.tensor_tensor(dv, dv, sv, ALU.mult).then_inc(w_high, 1)
            g.wait_ge(c_kept, after(2))
            g.wait_ge(ho_ready, after(HEADS))
            o_base, s_base = PAIRS + HEADS, 2 * PAIRS + HEADS
            with g.Fori(0, GROUPS) as i:
                st.enter(i, 1)
                g.wait_ge(near_ready, after(2 * HPG * i))
                st.mark(g.tensor_copy(s5_pool[:, 0, :], ccol("slopes")[:, ds(HPG * i, HPG)]))
                g.wait_ge(o_ready, after(o_base + 4 * i))
                g.tensor_copy(kc_cur[:, 0:NCMP], Kc[:, ds(NCMP * i, NCMP)]).then_inc(cur_kv, 1)
                g.tensor_copy(vc_cur[0:NCMP, :], Vc[0:NCMP, ds(i, 1), :].rearrange("p a d -> p (a d)"))\
                    .then_inc(cur_kv, 1)
                st.settle()
                for e in range(HPG):
                    g.wait_ge(m_ready, after(s_base + 4 * i + e))
                    apart(g)
                    g.tensor_scalar(near[:, :], ccol("alibi"), s5_pool[:, 0, e:e + 1], None, ALU.mult)\
                        .then_inc(near_ready, 1)
                    g.tensor_scalar(near_c[:, :, :].rearrange("p a n -> p (a n)"), ccol("alibi_c"),
                                    s5_pool[:, 0, e:e + 1], None, ALU.mult).then_inc(near_ready, 1)
                st.leave(GROUPS)

        @block.vector
        def _(v):
            st = Steps(v, step_sem["dve"])

            def then(instruction):
                st.mark(instruction)
                st.settle()

            def norm(n, gname, dst, ready):
                v.wait_ge(sum_ready, after(n + 1))
                v.wait_ge(rms_guess, after(n + 1))
                st.mark(v.tensor_scalar(nv[:, :], bank[7][:, 0:T], 1.0 / D, EPS, ALU.mult, ALU.add))
                then(v.tensor_tensor(nt[:, :], rstd[:, :], rstd[:, :], ALU.mult))
                then(v.tensor_tensor(nt[:, :], nt[:, :], nv[:, :], ALU.mult))
                then(v.tensor_scalar(nt[:, :], nt[:, :], -0.5, 1.5, ALU.mult, ALU.add))
                then(v.tensor_tensor(rstd[:, :], rstd[:, :], nt[:, :], ALU.mult))
                for k in range(KT):
                    v.scalar_tensor_tensor(dst[:, k, :], x[:, k, :], pcol(gname, k, 1), rstd[:, :], ALU.mult,
                                           ALU.mult).then_inc(ready, 1)

            def sum_squares(n):
                v.wait_ge(squares, after(n + 1))
                v.tensor_reduce(ssq[:, :], mix[:, 0:KT, :].rearrange("p k t -> p t k"), AX_X, ALU.add)\
                    .then_inc(ssq_ready, 1)

            def add_out(ph, ktiles, unit, first_block):
                st.mark(v.memset(ssq[:, :], 0.0))
                with v.Fori(0, 4) as i:
                    st.enter(i, 4)
                    for b in range(4):
                        v.wait_ge(used, done(ph, i, (b + 1) * ktiles // unit))
                        xb = x[:, ds(4 * i + b, 1), :].rearrange("p a t -> p (a t)")
                        v.tensor_tensor(xb, xb, bank[b % 2][:, 0:T], ALU.add).then_inc(x_added, 1)
                        st.settle()
                        v.wait_ge(sq_ready, after(first_block + 4 * i + b + 1))
                        st.mark(v.tensor_tensor(ssq[:, :], ssq[:, :], sq[:, b % 2, :], ALU.add))
                    st.leave(4)
                st.settle()
                v.tensor_copy(nt[:, 0:1], ssq[:, 0:1]).then_inc(ssq_ready, 1)

            def masked_max(src, mask, dst, out_max):
                for tt, cols in ((0, slice(0, P)), (1, slice(P, 384))):
                    st.mark(v.tensor_tensor_reduce(dst[:, cols], src[:, cols], mask[:, cols], 1.0, -3e38, ALU.add,
                                                   ALU.max, out_max[tt]))

            def normalise(dst, factor):
                for tt, cols in ((0, slice(0, P)), (1, slice(P, 384))):
                    ins = v.tensor_scalar(dst[:, cols], dst[:, cols], factor[tt], None, ALU.mult)
                return ins

            v.wait_ge(par_in, 16)
            lr, li = pcol("lam_re"), pcol("lam_im")
            st.mark(v.tensor_scalar(bgh[:, :], pcol("b_glu"), 0.5, None, ALU.mult))
            v.wait_ge(s5_act, after(1))
            st.mark(v.tensor_tensor(s5t[:, 1, :], lr, s5t[:, 0, :], ALU.mult))
            then(v.tensor_tensor(s5t[:, 2, :], li, s5t[:, 0, :], ALU.mult))
            then(v.tensor_scalar(s5t[:, 7, :], s5t[:, 2, :], 1.0 / TWO_PI, ROUND, ALU.mult, ALU.add))
            v.tensor_scalar(s5t[:, 7, :], s5t[:, 7, :], -ROUND, None, ALU.add).then_inc(s5_mid, 1)
            v.wait_ge(s5_mid, after(1))
            then(v.scalar_tensor_tensor(s5t[:, 3, :], s5t[:, 7, :], -TWO_PI_HI, s5t[:, 2, :], ALU.mult, ALU.add))
            then(v.scalar_tensor_tensor(s5t[:, 3, :], s5t[:, 7, :], -TWO_PI_LO, s5t[:, 3, :], ALU.mult, ALU.add))
            then(v.tensor_scalar(s5t[:, 3, :], s5t[:, 3, :], PI_IN, -PI_IN, ALU.min, ALU.max))
            then(v.scalar_tensor_tensor(s5t[:, 4, :], s5t[:, 3, :], -1.0, s5t[:, 3, :], ALU.mult, ALU.max))
            v.tensor_scalar(s5t[:, 4, :], s5t[:, 4, :], -1.0, math.pi / 2, ALU.mult, ALU.add).then_inc(s5_mid, 1)
            rgv = pcol("rg").rearrange("p (n f) -> p n f", f=8)
            lam = rgv[:, :, RG_COLS["lam"]]
            st.mark(v.scalar_tensor_tensor(rgt[:, 0, :], lam, -1.0, lam, ALU.mult, ALU.max))
            v.tensor_tensor(lbt[:, 0, :], pcol("lb"), pcol("lb"), ALU.subtract).then_inc(sp_in, 1)
            st.mark(v.tensor_scalar(rgt[:, 5, :], lam, -1.0, 0.0, ALU.mult, ALU.max))
            st.mark(v.tensor_scalar(rgv[:, :, RG_COLS["ba"]], rgv[:, :, RG_COLS["ba"]], -1.0, None, ALU.mult))
            st.mark(v.tensor_scalar(rgv[:, :, RG_COLS["bi"]], rgv[:, :, RG_COLS["bi"]], 0.5, None, ALU.mult))
            v.wait_ge(s5_act, after(3))
            decay = s5[:, 0, :]
            st.mark(v.tensor_scalar(s5[:, 1, :], s5t[:, 3, :], 1.0 / TWO_PI, None, ALU.mult))
            st.mark(v.tensor_tensor(s5t[:, 8, :], decay, s5t[:, 6, :], ALU.mult))
            st.mark(v.tensor_tensor(s5t[:, 9, :], decay, s5t[:, 5, :], ALU.mult))
            st.mark(v.tensor_tensor(s5t[:, 10, :], lr, lr, ALU.mult))
            then(v.tensor_tensor(s5t[:, 11, :], li, li, ALU.mult))
            st.mark(v.tensor_scalar(s5t[:, 8, :], s5t[:, 8, :], -1.0, None, ALU.add))
            then(v.tensor_tensor(s5t[:, 10, :], s5t[:, 10, :], s5t[:, 11, :], ALU.add))
            then(v.reciprocal(s5t[:, 10, :], s5t[:, 10, :]))
            for n, (first, second, op) in enumerate(((8, 9, ALU.add), (9, 8, ALU.subtract))):
                st.mark(v.tensor_tensor(s5t[:, 11, :], s5t[:, first, :], lr, ALU.mult))
                then(v.tensor_tensor(s5t[:, 7, :], s5t[:, second, :], li, ALU.mult))
                then(v.tensor_tensor(s5t[:, 11, :], s5t[:, 11, :], s5t[:, 7, :], op))
                then(v.tensor_tensor(s5[:, 2 + n, :], s5t[:, 11, :], s5t[:, 10, :], ALU.mult))
            v.tensor_copy(cur[:, 30:31], s5[:, 3, 0:1]).then_inc(s5_par, 1)
            sum_squares(0)
            v.wait_ge(sp_exp, after(1))
            then(v.tensor_scalar(rgt[:, 2, :], rgt[:, 1, :], 2.0, None, ALU.add))
            then(v.reciprocal(rgt[:, 2, :], rgt[:, 2, :]))
            then(v.tensor_tensor(rgt[:, 2, :], rgt[:, 2, :], rgt[:, 1, :], ALU.mult))
            then(v.tensor_tensor(rgt[:, 3, :], rgt[:, 2, :], rgt[:, 2, :], ALU.mult))
            then(v.tensor_scalar(rgt[:, 4, :], rgt[:, 3, :], 1.0 / 17, None, ALU.mult))
            for odd in (15, 13, 11, 9, 7, 5, 3):
                then(v.scalar_tensor_tensor(rgt[:, 4, :], rgt[:, 4, :], 1.0 / odd, rgt[:, 3, :], ALU.add, ALU.mult))
            then(v.scalar_tensor_tensor(rgt[:, 4, :], rgt[:, 4, :], 1.0, rgt[:, 2, :], ALU.add, ALU.mult))
            then(v.scalar_tensor_tensor(rgt[:, 4, :], rgt[:, 4, :], 2.0, rgt[:, 5, :], ALU.mult, ALU.add))
            st.mark(v.tensor_scalar(lam, rgt[:, 4, :], -8.0, None, ALU.mult))
            then(v.reciprocal(lbt[:, 2, :], lbt[:, 1, :]))
            then(v.tensor_tensor(lbt[:, 1, :], lbt[:, 1, :], lbt[:, 2, :], ALU.mult))
            then(v.tensor_tensor(lbt[:, 0, :], lbt[:, 1, :], lbt[:, 1, :], ALU.subtract))
            st.mark(v.tensor_scalar(lbt[:, 2, :], lbt[:, 0, :], -0.5, 0.5, ALU.mult, ALU.add))
            st.mark(v.tensor_scalar(lbt[:, 3, :], pcol("gain"), 0.5, None, ALU.mult))
            then(v.tensor_scalar(lbt[:, 1, :], lbt[:, 0, :], -1.0, 1.0, ALU.mult, ALU.add))
            v.wait_ge(con_in, 16)
            norm(0, "g_even", h, h_ready)
            with v.Fori(0, PAIRS) as i:
                st.enter(i, 34)
                st.mark(v.tensor_copy(cur[:, 0:4], s5[:, 0, ds(4 * i, 4)]))
                then(v.tensor_copy(cur[:, 4:5], pcol("d_skip")[:, ds(i, 1)]))
                v.wait_ge(landed[6], even1.loads[4].land0 + i * even1.loads[4].land_per)
                st.mark(v.memset(ring[64:P, 6, 512 + 192:768], NEG))
                v.memset(ring[64:P, 6, 768 + 192:1024], NEG).then_inc(bias_masked, 1)
                v.wait_ge(rot_ready, after(i + 1))

                def states(t):
                    v.wait_ge(bu_ready, after(4 * i + t + 1))
                    bu = bank[6][:, :].rearrange("p (c n) -> p c n", c=2)
                    st.mark(v.tensor_tensor(w2[:, :, :], bu, mix[:, 8 + 2 * t:9 + 2 * t, :].to_broadcast([P, 2, T]),
                                            ALU.mult))
                    v.tensor_tensor(w3[:, :, :], bu, mix[:, 9 + 2 * t:10 + 2 * t, :].to_broadcast([P, 2, T]),
                                    ALU.mult).then_inc(bu_used, 1)
                    st.settle()
                    v.wait_ge(bu_used, after(4 * i + t + 1))
                    st.mark(v.tensor_tensor(w4[:, 0, :], w2[:, 0, :], w3[:, 1, :], ALU.subtract))
                    then(v.tensor_tensor(w4[:, 1, :], w2[:, 1, :], w3[:, 0, :], ALU.add))
                    for c in range(2):
                        st.mark(v.tensor_tensor_scan(w5[:, c, :], cur[:, t:t + 1].to_broadcast([P, T]), w4[:, c, :],
                                                     0.0, ALU.mult, ALU.add))
                    st.settle()
                    v.wait_ge(state_ready, after(8 * i + 2 * t))
                    st.mark(v.tensor_tensor(w8[:, :, :], w5[:, :, :],
                                            wide_c[:, 2 * t + 1:2 * t + 2, :].to_broadcast([P, 2, T]), ALU.mult))
                    v.tensor_tensor(w9[:, :, :], w5[:, :, :],
                                    wide_c[:, 2 * t:2 * t + 1, :].to_broadcast([P, 2, T]), ALU.mult)\
                        .then_inc(rot_used, 1)

                states(0)
                states(1)
                for e in range(2):
                    v.wait_ge(s_ready, after(2 * i + e + 1))
                    st.mark(v.tensor_reduce(nmax[:, e, 0:1], bank[2 + e][:, 0:P], AX_X, ALU.max, negate=True))
                    v.tensor_reduce(nmax[:, e, 1:2], bank[2 + e][:, P:384], AX_X, ALU.max, negate=True)\
                        .then_inc(m_ready, 1)
                for e in range(2):
                    v.wait_ge(e_ready, after(2 * i + e + 1))
                    then(v.reciprocal(pinv[:, e, :], psums[:, e, :]))
                    normalise(prob[:, e, :], [pinv[:, e, t:t + 1] for t in range(2)]).then_inc(p_ready, 1)
                v.wait_ge(za_tanh, after(i + 1))
                v.scalar_tensor_tensor(gz[:, :], gate[:, :], 1.0, bank[0][:, 0:T], ALU.add, ALU.mult)\
                    .then_inc(za_used, 1)
                states(2)
                v.wait_ge(zb_tanh, after(i + 1))
                v.scalar_tensor_tensor(mix[:, ds(24 + i, 1), :].rearrange("p a t -> p (a t)"), sq[:, 0, :], 1.0,
                                       bank[1][:, 0:T], ALU.add, ALU.mult).then_inc(zb_used, 1)
                states(3)
                v.wait_ge(za_used, after(i + 1))
                v.wait_ge(o_ready, after(i + 1))
                v.scalar_tensor_tensor(mix[:, ds(i, 1), :].rearrange("p a t -> p (a t)"), bank[5][:, 0:T], 0.5,
                                       gz[:, :], ALU.mult, ALU.mult).then_inc(o_used, 1)
                v.wait_ge(y_ready, after(4 * i + 4))
                v.scalar_tensor_tensor(w4[:, 0, :], uT[:, :], cur[:, 4:5], bank[7][:, 0:T], ALU.mult, ALU.add)\
                    .then_inc(y_used, 1)
                v.wait_ge(y_used, after(i + 1))
                then(v.tensor_tensor(w4[:, 1, :], w4[:, 0, :], w4[:, 0, :], ALU.mult))
                then(v.tensor_scalar(w4[:, 1, :], w4[:, 1, :], GELU_C, 1.0, ALU.mult, ALU.add))
                v.tensor_tensor(w4[:, 1, :], w4[:, 1, :], w4[:, 0, :], ALU.mult).then_inc(gelu_in, 1)
                st.mark(v.tensor_scalar(w5[:, 0, :], w4[:, 0, :], 0.5, None, ALU.mult))
                v.wait_ge(gelu_t, after(i + 1))
                st.settle()
                v.scalar_tensor_tensor(mix[:, ds(16 + i, 1), :].rearrange("p a t -> p (a t)"), sq[:, 1, :], 1.0,
                                       w5[:, 0, :], ALU.add, ALU.mult).then_inc(y_mixed, 1)
                st.leave(PAIRS)
            v.wait_ge(y_mixed, after(PAIRS))
            v.wait_ge(zb_used, after(PAIRS))
            with v.Fori(0, 2) as i:
                st.enter(i, 4)
                for b in range(4):
                    v.wait_ge(glu_t, after(4 * i + b + 1))
                    then(v.scalar_tensor_tensor(w4[:, b % 2, :], sq[:, b % 2, :], 1.0,
                                                mix[:, ds(16 + 4 * i + b, 1), :].rearrange("p a t -> p (a t)"),
                                                ALU.add, ALU.mult))
                    v.scalar_tensor_tensor(mix[:, ds(8 + 4 * i + b, 1), :].rearrange("p a t -> p (a t)"),
                                           w4[:, b % 2, :], 0.25, mix[:, ds(24 + 4 * i + b, 1), :].rearrange("p a t -> p (a t)"),
                                           ALU.mult, ALU.mult).then_inc(glu_mixed, 1)
                st.leave(2)
            add_out(out1, 16, 16, 0)
            norm(1, "g_odd", h, h_ready)
            v.wait_ge(used, done(forget, 0, 1))
            then(v.tensor_scalar(fl[:, 0, :], bank[6][0:HEADS, 0:T], pcol("b_forget")[0:16, :], None, ALU.add))
            v.scalar_tensor_tensor(fl[:, 1, :], fl[:, 0, :], -1.0, fl[:, 0, :], ALU.mult, ALU.max).then_inc(f_in, 1)
            v.wait_ge(f_ln, after(1))
            then(v.tensor_scalar(fl[:, 1, :], fl[:, 0, :], 0.0, None, ALU.min))
            then(v.tensor_tensor(fl[:, 2, :], fl[:, 3, :], fl[:, 1, :], ALU.subtract))
            then(v.tensor_tensor_scan(nc_[:, :], ccol("ones", 0, 1)[0:16, :].to_broadcast([16, T]), fl[:, 2, :], 0.0,
                                      ALU.mult, ALU.add))
            with v.Fori(0, HEADS) as i:
                st.enter(i, 2)
                v.wait_ge(s_ready, after(2 * PAIRS + i))
                v.tensor_scalar(ck[:, :], nc_[:, :], ident[0:16, ds(i, 1)], None, ALU.mult).then_inc(ck_ready, 1)
                v.wait_ge(s_ready, after(2 * PAIRS + i + 1))
                apart(v)
                masked_max(bank[2], ccol("causal"), score[:, 0, :], [stat[:, 0, t, 0:1] for t in range(2)])
                st.settle()
                v.tensor_scalar(nmax[:, 0, :], stat[:, 0, :, 0], -1.0, None, ALU.mult).then_inc(m_ready, 1)
                v.wait_ge(e_ready, after(2 * PAIRS + i + 1))
                v.wait_ge(m_ready, after(2 * PAIRS + i + 1))
                v.reciprocal(pinv[:, 0, :], psums[:, 0, :]).then_inc(f_cum, 1)
                v.wait_ge(f_cum, after(i + 1))
                normalise(prob[:, 0, :], [pinv[:, 0, t:t + 1] for t in range(2)]).then_inc(p_ready, 1)
                v.wait_ge(z_tanh, after(i + 1))
                v.scalar_tensor_tensor(gz[:, :], gate[:, :], 1.0, bank[1][:, 0:T], ALU.add, ALU.mult)\
                    .then_inc(z_used, 1)
                v.wait_ge(z_used, after(i + 1))
                v.wait_ge(o_ready, after(PAIRS + i + 1))
                v.scalar_tensor_tensor(mix[:, ds(i, 1), :].rearrange("p a t -> p (a t)"), bank[5][:, 0:T], 0.5,
                                       gz[:, :], ALU.mult, ALU.mult).then_inc(o_used, 1)
                st.leave(HEADS)
            add_out(out2, 16, 16, 16)
            norm(2, "g_final", x, h_ready)
            sum_squares(1)
            norm(3, "g_even2", h, h_ready)
            with v.Fori(0, HEADS) as i:
                kk, qs = w9[:, 0, :], w9[:, 1, :]
                st.enter(i, 20)
                v.wait_ge(used, done(hgrn, i, 1))
                v.tensor_scalar(w2[:, 0, :], bank[0][:, 0:T], -80.0, None, ALU.max).then_inc(hf_in, 1)
                v.wait_ge(h_mixed, after(i))
                st.mark(v.tensor_copy(cur[:, 0:4].unsqueeze(2), lbt[:, :, ds(i, 1)]))
                v.wait_ge(hf_exp, after(i + 1))
                then(v.tensor_scalar(w3[:, 0, :], w2[:, 1, :], 1.0, None, ALU.add))
                then(v.reciprocal(w3[:, 1, :], w3[:, 0, :]))
                st.mark(v.scalar_tensor_tensor(kk, w2[:, 1, :], cur[:, 2:3], w3[:, 1, :], ALU.mult, ALU.mult))
                then(v.tensor_scalar(w5[:, 0, :], w3[:, 1, :], cur[:, 1:2], cur[:, 0:1], ALU.mult, ALU.add))
                st.mark(v.tensor_scalar(w4[:, 0, :], w5[:, 0, :], SPLIT, None, ALU.max))
                v.tensor_scalar(w4[:, 1, :], w5[:, 0, :], SPLIT, TINY, ALU.min, ALU.max).then_inc(hf_split, 1)
                v.wait_ge(hf_ln, after(i + 1))
                then(v.tensor_tensor(w5[:, 0, :], w8[:, 0, :], w8[:, 1, :], ALU.add))
                v.tensor_tensor_scan(w5[:, 1, :], ccol("chunk"), w5[:, 0, :], 0.0, ALU.mult, ALU.add)\
                    .then_inc(hb_ready, 1)
                v.wait_ge(hq_tanh, after(i + 1))
                v.scalar_tensor_tensor(qs, gate[:, :], 1.0, bank[1][:, 0:T], ALU.add, ALU.mult).then_inc(hq_used, 1)
                att = small[:, :].rearrange("p (b t) -> p b t", b=2)
                st.mark(v.memset(small[:, :], 0.0))
                st.settle()
                v.wait_ge(hq_used, after(i + 1))
                v.wait_ge(decay_ready, after(i + 1))
                for lv in range(4):
                    m = 1 << lv
                    for c, src in ((0, kk), (1, qs)):
                        dv = wide_b[:, lv, :].rearrange("p (n c m) -> p n c m", c=2, m=m)[:, :, c, :]
                        sv = src.rearrange("p (n c m) -> p n c m", c=2, m=m)[:, :, c, :]
                        ins = v.tensor_tensor(dv, dv, sv, ALU.mult)
                        if (lv, c) != (3, 1):
                            st.mark(ins)
                        else:
                            ins.then_inc(w_low, 1)
                for pos, lv in enumerate(LEVEL_ORDER):
                    v.wait_ge(lv_used, after(8 * i + pos))
                    v.wait_ge(lv_ready, after(8 * i + pos + 1))
                    apart(v)
                    src = bank[LEVEL_BANKS[pos % 4]][:, 0:T].rearrange("p (b t) -> p b t", b=2)
                    mask = ccol("level", lv * P, P).bitcast(U32).unsqueeze(1).to_broadcast([P, 2, P])
                    v.copy_predicated(att, mask, src).then_inc(lv_used, 1)
                v.wait_ge(ho_guess, after(i + 1))
                y, r = stat[:, 2, :, 0], stat[:, 3, :, 0]
                st.mark(v.tensor_scalar(stat[:, 1, :, 1], stat[:, 0, :, 0], 1.0 / P, EPS, ALU.mult, ALU.add))
                then(v.tensor_tensor(r, y, y, ALU.mult))
                then(v.tensor_tensor(r, r, stat[:, 1, :, 1], ALU.mult))
                then(v.tensor_scalar(r, r, -0.5, 1.5, ALU.mult, ALU.add))
                then(v.tensor_tensor(r, r, y, ALU.mult))
                for tt in range(2):
                    ins = v.tensor_scalar(w6[:, 0, 0, tt * P:(tt + 1) * P], bank[5][:, tt * P:(tt + 1) * P],
                                          stat[:, 3, tt, 0:1], None, ALU.mult)
                ins.then_inc(ho_norm, 1)
                v.wait_ge(hg_tanh, after(i + 1))
                v.scalar_tensor_tensor(gz[:, :], gate[:, :], 1.0, bank[1][:, 0:T], ALU.add, ALU.mult)\
                    .then_inc(hg_used, 1)
                v.wait_ge(hg_used, after(i + 1))
                v.wait_ge(ht_ready, after(i + 1))
                v.scalar_tensor_tensor(mix[:, ds(i, 1), :].rearrange("p a t -> p (a t)"), bank[4][:, 0:T],
                                       cur[:, 3:4], gz[:, :], ALU.mult, ALU.mult).then_inc(h_mixed, 1)
                st.leave(HEADS)
            v.wait_ge(gate_exp, after(1))
            then(v.tensor_scalar(w2[:, 0, 0:96], w2[:, 0, 0:96], 1.0, None, ALU.add))
            then(v.reciprocal(gates_sb[:, :, :].rearrange("p a n -> p (a n)"), w2[:, 0, 0:96]))
            v.wait_ge(ckv_ready, after(2 * GROUPS))
            for n, (dst, pe_name) in enumerate(((wide_a, "pe_k"), (wide_c, "pe_v"))):
                base = wide_b[:, 4 * n, 0:1]
                windows = bass.AP(base.tensor, base.offset, [base.ap[0], [1, CMP_LEN], [T, GROUPS],
                                                             [CMP_STRIDE, NCMP]])
                blocks = dst[:, :, :].rearrange("p k t -> p (k t)")[:, 0:CMP_LEN * GROUPS * NCMP]\
                    .rearrange("p (l g n) -> p l g n", l=CMP_LEN, g=GROUPS)
                v.tensor_tensor(blocks, windows,
                                pcol(pe_name).unsqueeze(2).unsqueeze(3).to_broadcast([P, CMP_LEN, GROUPS, NCMP]),
                                ALU.add).then_inc(cblk_ready, 1)
            for n in range(2):
                v.wait_ge(c_tanh, after(n + 1))
                then(v.scalar_tensor_tensor(w4[:, n, 0:60], w3[:, n, 0:60], 1.0, bank[2 + n][:, 0:60], ALU.add,
                                            ALU.mult))
                v.tensor_scalar(w2[:, n, 0:60], w4[:, n, 0:60], 0.5, None, ALU.mult).then_inc(c_silu, 1)
            s_base, g_base, o_base = 2 * PAIRS + HEADS, HEADS, PAIRS + HEADS
            with v.Fori(0, GROUPS) as i:
                st.enter(i, 45)
                st.mark(v.tensor_copy(gcur[:, :, :], gates_sb[:, :, ds(3 * HPG * i, 3 * HPG)]))
                for e in range(HPG):
                    n = 4 * i + e
                    v.wait_ge(near_ready, after(2 * n + 2))
                    v.wait_ge(s_ready, after(s_base + n + 1))
                    apart(v)
                    for tt in range(2):
                        st.mark(v.tensor_tensor_reduce(score_c[:, tt, :], bank[6][:, tt * NCMP:(tt + 1) * NCMP],
                                                       near_c[:, tt, :], 1.0, -3e38, ALU.add, ALU.max,
                                                       stat[:, 0, tt, 0:1]))
                    masked_max(bank[2], near, score[:, 0, :], [stat[:, 0, t, 1:2] for t in range(2)])
                    masked_max(bank[3], near, score[:, 1, :], [stat[:, 0, t, 2:3] for t in range(2)])
                    st.settle()
                    v.tensor_scalar(stat[:, 1, :, :], stat[:, 0, :, :], -1.0, None, ALU.mult).then_inc(m_ready, 1)
                    v.wait_ge(e_ready, after(s_base + n + 1))
                    then(v.reciprocal(stat[:, 3, :, :], stat[:, 2, :, :]))
                    then(v.tensor_tensor(stat[:, 3, :, :], stat[:, 3, :, :], gcur[:, :, 3 * e:3 * e + 3], ALU.mult))
                    for tt in range(2):
                        st.mark(v.scalar_tensor_tensor(prob_c[:, tt, :], prob_c[:, tt, :], stat[:, 3, tt, 0:1],
                                                       ccol("seen_c", tt * NCMP, NCMP), ALU.mult, ALU.mult))
                    st.mark(normalise(prob[:, 0, :], [stat[:, 3, t, 1:2] for t in range(2)]))
                    normalise(prob[:, 1, :], [stat[:, 3, t, 2:3] for t in range(2)]).then_inc(p_ready, 1)
                    if e:
                        pass
                    v.wait_ge(z_tanh, after(g_base + n + 1))
                    st.settle()
                    v.scalar_tensor_tensor(gz[:, :], gate[:, :], 1.0, bank[1][:, 0:T], ALU.add, ALU.mult)\
                        .then_inc(z_used, 1)
                    v.wait_ge(z_used, after(g_base + n + 1))
                    v.wait_ge(o_ready, after(o_base + n + 1))
                    v.scalar_tensor_tensor(mix[:, ds(16 + n, 1), :].rearrange("p a t -> p (a t)"), bank[5][:, 0:T], 0.5,
                                           gz[:, :], ALU.mult, ALU.mult).then_inc(o_used, 1)
                st.leave(GROUPS)
            add_out(out3, 32, 16, 32)
            norm(4, "g_odd2", h, h_ready)
            st.mark(v.memset(xpad[:, :, 0:4], 0.0))
            with v.Fori(0, RGB) as i:
                st.enter(i, 14)
                v.wait_ge(rg_mixed, after(i))
                then(v.tensor_copy(cur[:, 0:16], pcol("rg")[:, ds(16 * i, 16)]))
                for c in range(2):
                    v.wait_ge(xb_ready, after(2 * i + c + 1))
                    f = 8 * c
                    then(v.tensor_scalar(w2[:, c, :], xpad[:, c, 4:T + 4], cur[:, f + 3:f + 4],
                                         cur[:, f + RG_COLS["b"]:f + RG_COLS["b"] + 1], ALU.mult, ALU.add))
                    for j in (2, 1, 0):
                        ins = v.scalar_tensor_tensor(w2[:, c, :], xpad[:, c, j + 1:j + 1 + T], cur[:, f + j:f + j + 1],
                                                     w2[:, c, :], ALU.mult, ALU.add)
                        if j:
                            then(ins)
                        else:
                            ins.then_inc(xc_ready, 1)
                v.wait_ge(rg_pre, after(i + 1))
                then(v.tensor_scalar(w3[:, :, :], w3[:, :, :], 1.0, None, ALU.add))
                v.reciprocal(w5[:, :, :], w3[:, :, :]).then_inc(rg_r, 1)
                v.wait_ge(xc_ready, after(2 * i + 2))
                st.mark(v.scalar_tensor_tensor(w4[:, :, :], w4[:, :, :], 1.0, w2[:, :, :], ALU.add, ALU.mult))
                v.wait_ge(rg_a, after(i + 1))
                v.wait_ge(rg_r, after(i + 1))
                then(v.tensor_tensor(w3[:, :, :], w8[:, :, :], w8[:, :, :], ALU.mult))
                then(v.scalar_tensor_tensor(w3[:, :, :], w3[:, :, :], 1.0, w9[:, :, :], ALU.add, ALU.mult))
                v.tensor_scalar(w3[:, :, :], w3[:, :, :], -1.0, 0.0, ALU.mult, ALU.max).then_inc(rg_v, 1)
                v.wait_ge(rg_s, after(i + 1))
                then(v.tensor_tensor(w4[:, :, :], w4[:, :, :], w6[:, 0, :, :], ALU.mult))
                for c in range(2):
                    st.mark(v.tensor_tensor_scan(wide_b[:, c, :], w8[:, c, :], w4[:, c, :], 0.0, ALU.mult, ALU.add))
                v.wait_ge(rgg_tanh, after(i + 1))
                v.scalar_tensor_tensor(wide_c[:, 0:2, :], wide_a[:, 0:2, :], 1.0,
                                       psum[:, 4:6, 0:T], ALU.add, ALU.mult)\
                    .then_inc(rgg_used, 1)
                st.settle()
                v.wait_ge(rgg_used, after(i + 1))
                v.scalar_tensor_tensor(mix[:, ds(2 * i, 2), :], wide_b[:, 0:2, :], 0.5, wide_c[:, 0:2, :], ALU.mult,
                                       ALU.mult).then_inc(rg_mixed, 1)
                st.leave(RGB)
            add_out(out4, 20, 4, 48)
            norm(5, "g_final2", x, x_final)


INPUTS = ("xT", "params", "consts", "rel", "s5_bc", "w_even1", "w_glu", "w_out1", "w_forget", "w_odd1", "w_out2",
          "w_hgrn", "w_gates", "w_cmp_in", "w_cmp1", "w_cmp2", "w_nsa", "w_out3", "w_rg", "w_rgg", "w_out4")


def shape_constants():
    c = np.zeros((P, N_CONSTS), np.float32)

    def put(name, value):
        at, width = CONSTS[name]
        c[:, at:at + width] = value

    put("ident", np.eye(P))
    put("flip", np.eye(P)[::-1])
    put("ones", 1.0)
    q = np.arange(P)[:, None]
    far = np.concatenate([q - np.arange(P)[None, :], P + q - np.arange(T)[None, :]], 1)
    put("alibi", np.where(far >= 0, -far, FAR))
    put("causal", np.where(far >= 0, 0.0, NEG))
    last = CMP_STRIDE * np.arange(NCMP)[None, :] + CMP_LEN - 1
    far = np.concatenate([q - last, P + q - last], 1)
    put("alibi_c", np.where(far >= 0, -far, FAR))
    put("seen_c", far >= 0)
    put("slopes", 2.0 ** (-8.0 * np.arange(1, HEADS + 1) / HEADS))
    put("time", np.arange(T))
    key, query = np.arange(P)[:, None], np.arange(P)[None, :]
    levels = []
    for lv in range(LEVELS):
        m = 1 << lv
        levels.append((key // (2 * m) == query // (2 * m)) & (key // m % 2 == 0) & (query // m % 2 == 1))
    levels.append(key == query)
    put("level", np.concatenate(levels, 1))
    put("chunk", np.arange(T) % CHUNK != 0)
    put("eps", EPS)
    return c


def lay_out(i):
    def col(v, width):
        return np.reshape(v, (width, P)).T

    def cut(w, first, width=P):
        b = w[:, first:first + width]
        return b.reshape(-1, P, width).transpose(1, 0, 2).reshape(P, -1)

    def series(w, firsts):
        return np.stack([np.stack([cut(w, f) for f in turn]) for turn in firsts])

    def packed(w, blocks, ktiles, turns):
        b = np.stack([cut(w, P * n) for n in range(blocks)])
        b = b.reshape(turns, blocks // turns, P, ktiles, P).transpose(0, 1, 3, 2, 4)
        b = b.reshape(turns, -1, TILES, P, P).transpose(0, 1, 3, 2, 4)
        return np.ascontiguousarray(b.reshape(turns, -1, P, TILES * P))

    par = np.zeros((P, N_PARAMS), np.float32)

    def put(name, value):
        at, width = PARAMS[name]
        par[:, at:at + width] = value

    put("g_even", col(i["norm_even_g"][0], KT))
    put("g_odd", col(i["norm_odd_g"][0], KT))
    put("g_final", col(i["final_norm_g"], KT))
    put("g_even2", col(i["norm_w_2"][0], KT))
    put("g_odd2", col(i["norm_w_2"][1], KT))
    put("g_final2", col(i["final_norm_w_2"], KT))
    put("lam_re", col(i["s5_lambda_re"][0], 32))
    put("lam_im", col(i["s5_lambda_im"][0], 32))
    put("log_dt", col(np.repeat(i["s5_log_dt"][0], 64), 32))
    put("d_skip", col(i["s5_d"][0], PAIRS))
    put("b_glu", col(i["b_glu"][0], PAIRS))
    par[0:HEADS, PARAMS["b_forget"][0]] = i["b_forget"][0]
    put("lb", col(i["hgrn_lb_logits_2"][0], HEADS))
    put("gain", col(i["hgrn_norm_w_2"][0], HEADS))
    put("pe_k", i["cmp_pe_k_2"][0].T)
    put("pe_v", i["cmp_pe_v_2"][0].T)
    rgp = np.stack([*i["rg_conv_w_2"][0], i["rg_conv_b_2"][0], i["rg_b_a_2"][0], i["rg_b_i_2"][0],
                    i["rg_lambda_2"][0]])
    put("rg", rgp.reshape(8, RGB * 2, P).transpose(2, 1, 0).reshape(P, -1))

    rb = i["rel_bias"][0][:, ::-1]
    reach = rb.shape[1] // 2
    rev = np.concatenate([np.repeat(rb[:, :1], T - 1 - reach, 1), rb, np.repeat(rb[:, -1:], T - 1 - reach, 1)], 1)
    rel = np.stack([rev[:, p:p + T] for p in range(P)], 1)

    bc = np.zeros((PAIRS, P, 4, P), np.float32)
    for turn in range(PAIRS):
        for gl in range(8):
            g, t, e = 8 * turn + gl, gl // 2, gl % 2
            rows, states, chans = slice(16 * gl, 16 * gl + 16), slice(64 * e, 64 * e + 64), slice(16 * gl, 16 * gl + 16)
            bc[turn, rows, 0, states] = i["s5_b_re"][0, g].T
            bc[turn, rows, 1, states] = i["s5_b_im"][0, g].T
            bc[turn, states, 2, chans] = i["s5_c_re"][0, g].T
            bc[turn, states, 3, chans] = i["s5_c_im"][0, g].T

    we, wo, w2 = i["w_in_even"][0], i["w_in_odd"][0], i["even_w_in_2"][0]
    out = dict(
        xT=np.ascontiguousarray(i["x"][0].T).reshape(KT, P, T), params=par, consts=shape_constants(),
        rel=np.ascontiguousarray(rel), s5_bc=bc.reshape(PAIRS, P, 4 * P),
        w_even1=series(we, [[3072 + P * n, P * n, 1024 + P * n, 2048 + P * n, 4096 + P * n, 5120 + P * n]
                            for n in range(PAIRS)]),
        w_glu=packed(i["w_glu"][0], 8, 8, 2),
        w_out1=packed(i["w_out_even"][0], 16, 16, 4),
        w_forget=cut(wo, 8192, HEADS)[None, None],
        w_odd1=series(wo, [[D * m + P * n for m in range(4)] for n in range(HEADS)]),
        w_out2=packed(i["w_out_odd"][0], 16, 16, 4),
        w_hgrn=series(w2, [[2048 + P * n, P * n, 4096 + P * n, 6144 + P * n] for n in range(HEADS)]),
        w_gates=cut(w2, 13312, 48)[None, None],
        w_cmp_in=series(w2, [[10240 + P * n, 10752 + P * n] for n in range(GROUPS)]),
        w_cmp1=np.stack([i[f"cmp_w1_{c}_2"][0].reshape(2, TILES, P, P)[half].transpose(1, 0, 2).reshape(P, -1)
                         for c in "kv" for half in range(2)])[None],
        w_cmp2=np.concatenate([i["cmp_w2_k_2"][0], i["cmp_w2_v_2"][0]], 1)[None, None],
        w_nsa=series(w2, [[11264 + P * n, 11776 + P * n, 12288 + P * n, 12800 + P * n] +
                          [f + P * (HPG * n + e) for e in range(HPG) for f in (8192, 13360)]
                          for n in range(GROUPS)]),
        w_out3=packed(i["even_w_out_2"][0], 16, 32, 4),
        w_rg=series(i["odd_w_in_2"][0], [[256 * n, 256 * n + P, 2560 + 256 * n, 2560 + 256 * n + P]
                                         for n in range(RGB)]),
        w_rgg=np.stack([i["rg_w_a_2"][0], i["rg_w_i_2"][0]], 1)
        .reshape(RGB, 2, 2, P, 2, P).transpose(0, 3, 1, 4, 2, 5).reshape(RGB, 1, P, 8 * P),
        w_out4=packed(i["odd_w_out_2"][0], 16, 20, 4),
    )
    return {k: np.ascontiguousarray(v) for k, v in out.items()}


def kernel(**inputs):
    import concourse.bacc as bacc
    from concourse.bass_utils import run_bass_kernel_spmd

    nc = bacc.Bacc("TRN2", target_bir_lowering=False, num_devices=1)
    arrays = lay_out({k: np.asarray(v) for k, v in inputs.items()})
    a = {n: nc.dram_tensor(n, arrays[n].shape, F32, kind="ExternalInput").ap() for n in INPUTS}
    out = nc.dram_tensor("yT", (KT, P, T), F32, kind="ExternalOutput").ap()
    program(nc, a, out)
    r = run_bass_kernel_spmd(nc, [arrays], core_ids=[0])
    return np.ascontiguousarray(r.results[0]["yT"].reshape(D, T).T)[None]
```

```python
from contextlib import ExitStack
import math

import numpy as np
import concourse.bass as bass
from concourse import mybir

F32 = mybir.dt.float32
U32 = mybir.dt.uint32
ALU = mybir.AluOpType
ACT = mybir.ActivationFunctionType
AX_X = mybir.AxisListType.X

P = 128
T = 256
D = 2048
KT = D // P
HALF = P
SLOTS = 7
TILES = 16
SLOT = TILES * P
CREDIT = 2

PAIRS = 8
HEADS = 16
GROUPS = 4
HPG = 4
NCMP = 15
CMP_LEN, CMP_STRIDE = 32, 16
RGB = 10
CHUNK = 64
LEVELS = 7
LEVEL_BANKS = (2, 3, 6, 7)
LEVEL_ORDER = (LEVELS,) + tuple(range(LEVELS))
EPS = 1e-6
NEG = -1e30
FAR = -1e34
TINY = 1e-30
SPLIT = 2.0 ** -30
ROUND = 1.5 * 2.0 ** 23
TWO_PI = 2 * math.pi
TURN = 6.283185
TWO_PI_HI = 6.28125
TWO_PI_LO = TWO_PI - TWO_PI_HI
PI_IN = 3.1415925
GELU_C = 0.044715
GELU_S = math.sqrt(2.0 / math.pi)
ds = bass.ds


def columns(spec):
    out, at = {}, 0
    for name, width in spec:
        out[name] = (at, width)
        at += width
    return out, at


PARAMS, N_PARAMS = columns([
    ("g_even", KT), ("g_odd", KT), ("g_final", KT), ("g_even2", KT), ("g_odd2", KT), ("g_final2", KT),
    ("lam_re", 32), ("lam_im", 32), ("log_dt", 32), ("d_skip", PAIRS), ("b_glu", PAIRS),
    ("b_forget", 1), ("lb", HEADS), ("gain", HEADS), ("pe_k", CMP_LEN), ("pe_v", CMP_LEN),
    ("rg", RGB * 16)])
RG_COLS = dict(w=0, b=4, ba=5, bi=6, lam=7)
CONSTS, N_CONSTS = columns([
    ("half_pi", 1), ("ident", P), ("flip", P), ("ones", P), ("alibi", 384), ("causal", 384), ("alibi_c", 2 * NCMP),
    ("seen_c", 2 * NCMP), ("slopes", HEADS), ("time", T), ("level", (LEVELS + 1) * P),
    ("chunk", T), ("eps", 1)])


class Steps:

    def __init__(self, eng, sem):
        self.eng, self.sem = eng, sem
        self.base, self.n, self.i, self.per = 0, 0, 0, 0

    def mark(self, instruction):
        instruction.then_inc(self.sem, 1)
        self.n += 1
        return instruction

    def settle(self):
        self.eng.wait_ge(self.sem, self.base + self.i * self.per + self.n)

    def enter(self, i, per):
        self.base, self.n, self.i, self.per = self.base + self.n, 0, i, per

    def leave(self, times):
        assert self.n == self.per, f"{self.sem}: {self.n} steps per turn, not {self.per}"
        self.base, self.n, self.i, self.per = self.base + times * self.per, 0, 0, 0


class Load:

    def __init__(self, slot, src, width, freed, others=0):
        self.slot, self.src, self.width, self.freed, self.others = slot, src, width, freed, others


class Phase:

    def __init__(self, turns, units, loads):
        self.turns, self.units, self.loads = turns, units, loads


def plan(phases):
    units = 0
    landed = [0] * SLOTS
    last = [0] * SLOTS
    for ph in phases:
        ph.base = units
        per = [0] * SLOTS
        for ld in ph.loads:
            per[ld.slot] += 16 * (1 + ld.others)
        so_far = [0] * SLOTS
        prev = {}
        for ld in ph.loads:
            so_far[ld.slot] += 16 * (1 + ld.others)
            ld.land0 = landed[ld.slot] + so_far[ld.slot]
            ld.land_per = per[ld.slot]
            ld.free0 = ph.base + prev[ld.slot] if ld.slot in prev else last[ld.slot]
            final = [x for x in ph.loads if x.slot == ld.slot][-1].freed
            ld.free_later = (0, prev[ld.slot]) if ld.slot in prev else (-1, final)
            prev[ld.slot] = ld.freed
        for s in range(SLOTS):
            landed[s] += per[s] * ph.turns
            if s in prev:
                last[s] = ph.base + (ph.turns - 1) * ph.units + prev[s]
        units += ph.units * ph.turns
    return phases


def program(nc, a, out):
    with ExitStack() as ctx:
        def sb(name, shape, dt=F32):
            return ctx.enter_context(nc.sbuf_tensor(name, shape, dt))

        def signal(name):
            s = ctx.enter_context(nc.semaphore(name))
            signals.append(s)
            return s

        signals = []
        psum = ctx.enter_context(nc.psum_tensor("psum", [P, 8, 512], F32))
        bank = [psum[:, n, :] for n in range(8)]
        ring = sb("ring", [P, SLOTS, SLOT])
        x = sb("x", [P, KT, T])
        h = sb("h", [P, KT, T])
        mix = sb("mix", [P, 32, T])
        par = sb("par", [P, N_PARAMS])
        con = sb("con", [P, N_CONSTS])

        def pcol(name, a0=0, width=None):
            c, w = PARAMS[name]
            return par[:, c + a0:c + a0 + (w - a0 if width is None else width)]

        def ccol(name, a0=0, width=None):
            c, w = CONSTS[name]
            return con[:, c + a0:c + a0 + (w - a0 if width is None else width)]

        ident, flip, ones = ccol("ident"), ccol("flip"), ccol("ones")
        ssq = sb("ssq", [P, T])
        rstd = sb("rstd", [P, T])
        sq = sb("sq", [P, 2, T])
        unused = sb("unused", [P, 1])
        uT = sb("uT", [P, T])
        qT = sb("qT", [P, T])
        kT = sb("kT", [P, T])
        kT2 = sb("kT2", [P, T])
        vN = sb("vN", [P, T])
        vN2 = sb("vN2", [P, T])
        prob = sb("prob", [P, 2, 384])
        probT = sb("probT", [P, 2, 384])
        score = sb("score", [P, 2, 384])
        near = sb("near", [P, 384])
        nmax = sb("nmax", [P, 2, 2])
        psums = sb("psums", [P, 2, 2])
        pinv = sb("pinv", [P, 2, 2])
        gate = sb("gate", [P, T])
        gz = sb("gz", [P, T])
        wide_a = sb("wide_a", [P, 8, T])
        wide_b = sb("wide_b", [P, 8, T])
        wide_c = sb("wide_c", [P, 8, T])
        w2 = sb("w2", [P, 2, T])
        w3 = sb("w3", [P, 2, T])
        w4 = sb("w4", [P, 2, T])
        w5 = sb("w5", [P, 2, T])
        w8 = sb("w8", [P, 2, T])
        w9 = sb("w9", [P, 2, T])
        nv, nt = w9[:, 0, :], w9[:, 1, :]
        w6 = sb("w6", [P, 2, 2, T])
        small = sb("small", [P, 256])
        cur = sb("cur", [P, 32])

        def tiles(name, n):
            return lambda i: a[name][ds(i, 1), n].rearrange("a p n -> (a p) n")

        even1 = Phase(PAIRS, 6, [Load(n, tiles("w_even1", n), SLOT, n + 1) for n in range(4)] +
                      [Load(6, None, 0, 6, 2)] +
                      [Load(n, tiles("w_even1", n), SLOT, n + 1) for n in range(4, 6)])
        glu = Phase(2, 4, [Load(n, tiles("w_glu", n), SLOT, 2 * n + 2) for n in range(2)])
        out1 = Phase(4, 4, [Load(2 + n, tiles("w_out1", n), SLOT, n + 1) for n in range(4)])
        forget = Phase(1, 1, [Load(6, tiles("w_forget", 0), KT * HEADS, 1)])
        odd1 = Phase(HEADS, 4, [Load(n, tiles("w_odd1", n), SLOT, n + 1) for n in range(4)])
        out2 = Phase(4, 4, [Load((4, 5, 6, 3)[n], tiles("w_out2", n), SLOT, n + 1) for n in range(4)])
        hgrn = Phase(HEADS, 4, [Load(n, tiles("w_hgrn", n), SLOT, n + 1) for n in range(4)])
        gates = Phase(1, 1, [Load(4, tiles("w_gates", 0), KT * 3 * HEADS, 1)])
        cmp_in = Phase(GROUPS, 2, [Load(5 + n, tiles("w_cmp_in", n), SLOT, n + 1) for n in range(2)])
        cmp_w1 = Phase(1, 5, [Load(n, tiles("w_cmp1", n), SLOT, n + 1) for n in range(4)] +
                       [Load(4, tiles("w_cmp2", 0), 2 * P, 5)])
        nsa = Phase(GROUPS, 12, [Load(n % 6, tiles("w_nsa", n), SLOT, n + 1) for n in range(12)])
        out3 = Phase(4, 8, [Load(n if n < 7 else 3, tiles("w_out3", n), SLOT, n + 1) for n in range(8)])
        rg = Phase(RGB, 5, [Load(n, tiles("w_rg", n), SLOT, (1, 2, 3, 5)[n]) for n in range(4)] +
                   [Load(4, tiles("w_rgg", 0), 8 * P, 4)])
        out4 = Phase(4, 20, [Load((5 + n) % 7, tiles("w_out4", n), SLOT, 4 * n + 4) for n in range(5)])
        phases = plan([even1, glu, out1, forget, odd1, out2, hgrn, gates, cmp_in, cmp_w1, nsa, out3,
                       rg, out4])

        landed = [ctx.enter_context(nc.semaphore(f"landed{s}")) for s in range(SLOTS)]
        used = ctx.enter_context(nc.semaphore("used"))
        x_in = [ctx.enter_context(nc.semaphore(f"x_in{c}")) for c in range(4)]
        par_in = ctx.enter_context(nc.semaphore("par_in"))
        ones_in = ctx.enter_context(nc.semaphore("ones_in"))
        con_in = ctx.enter_context(nc.semaphore("con_in"))
        stored = ctx.enter_context(nc.semaphore("stored"))

        def done(ph, i, unit):
            return ph.base + i * ph.units + unit

        def wait_load(pe, ph, i, n):
            ld = ph.loads[n]
            pe.wait_ge(landed[ld.slot], ld.land0 + i * ld.land_per)

        def tile(ph, n, t):
            return ring[:, ph.loads[n].slot, t * P:(t + 1) * P]

        squares = signal("squares")
        ssq_ready = signal("ssq_ready")
        sum_ready = signal("sum_ready")
        rms_guess = signal("rms_guess")
        h_ready = signal("h_ready")
        x_added = signal("x_added")
        sq_ready = signal("sq_ready")
        x_final = signal("x_final")
        q_ready, k_ready, v_ready = signal("q_ready"), signal("k_ready"), signal("v_ready")
        s_ready = signal("s_ready")
        m_ready = signal("m_ready")
        e_ready = signal("e_ready")
        p_ready = signal("p_ready")
        pt_ready = signal("pt_ready")
        pt_used = signal("pt_used")
        o_ready, o_used = signal("o_ready"), signal("o_used")
        u_ready = signal("u_ready")
        za_tanh, za_used, zb_tanh, zb_used = (signal(n) for n in ("za_tanh", "za_used", "zb_tanh", "zb_used"))
        bias_masked = signal("bias_masked")
        s5_mid = signal("s5_mid")
        s5_act = signal("s5_act")
        phase_ready, trig_ready, c_in_ready = signal("phase_ready"), signal("trig_ready"), signal("c_in_ready")
        rot_used = signal("rot_used")
        bu_ready, bu_used = signal("bu_ready"), signal("bu_used")
        state_ready = signal("state_ready")
        y_ready, y_used, gelu_in, gelu_t, y_mixed = (signal(n) for n in (
            "y_ready", "y_used", "gelu_in", "gelu_t", "y_mixed"))
        glu_t, glu_mixed = signal("glu_t"), signal("glu_mixed")
        f_in, f_ln, f_cum, ck_ready = (signal(n) for n in ("f_in", "f_ln", "f_cum", "ck_ready"))
        z_tanh, z_used = signal("z_tanh"), signal("z_used")
        hf_in, hf_exp, hf_split, hf_ln, hb_ready = (signal(n) for n in (
            "hf_in", "hf_exp", "hf_split", "hf_ln", "hb_ready"))
        hq_tanh, hq_used, hv_ready, hg_tanh, hg_used = (signal(n) for n in (
            "hq_tanh", "hq_used", "hv_ready", "hg_tanh", "hg_used"))
        span_ready, decay_ready, w_low, w_high = (signal(n) for n in (
            "span_ready", "decay_ready", "w_low", "w_high"))
        span_low, decay_low = signal("span_low"), signal("decay_low")
        lv_ready, lv_used, att_far, att_ready = (signal(n) for n in ("lv_ready", "lv_used", "att_far", "att_ready"))
        ho_ready, ho_guess, ho_norm, ht_ready, h_mixed = (signal(n) for n in (
            "ho_ready", "ho_guess", "ho_norm", "ht_ready", "h_mixed"))
        gate_exp = signal("gate_exp")
        ckv_ready, cblk_ready, c_tanh, c_silu, c_out, c_kept = (signal(n) for n in (
            "ckv_ready", "cblk_ready", "c_tanh", "c_silu", "c_out", "c_kept"))
        nkv_ready, near_ready, cur_kv = signal("nkv_ready"), signal("near_ready"), signal("cur_kv")
        xb_ready, xc_ready, rg_pre, rg_r, rg_a, rg_v, rg_s, rgg_tanh, rgg_used, rg_mixed = (signal(n) for n in (
            "xb_ready", "xc_ready", "rg_pre", "rg_r", "rg_a", "rg_v", "rg_s", "rgg_tanh", "rgg_used",
            "rg_mixed"))
        sp_in, sp_exp = signal("sp_in"), signal("sp_exp")

        s5 = sb("s5", [P, 4, 36])
        c_in = sb("c_in", [P, 2, P])
        c_tmp = sb("c_tmp", [P, 4, P])
        s5t = prob[:, :, :].rearrange("p a n -> p (a n)")[:, 0:384].rearrange("p (a n) -> p a n", a=12)
        slope = sb("slope", [P, HPG])
        bgh = sb("bgh", [P, PAIRS])
        rgt = sb("rgt", [P, 6, 2 * RGB])
        nc_ = sb("neg_cum", [16, T])
        fl = wide_a[0:16, 0:4, :]
        ck = sb("ck", [16, T])
        lbt = sb("lbt", [P, 4, HEADS])
        gates_sb = sb("gates_sb", [P, 2, 3 * HEADS])
        gcur = sb("gcur", [P, 2, 3 * HPG])
        Kc = sb("Kc", [P, GROUPS * NCMP])
        Vc = sb("Vc", [16, GROUPS, P])
        kc_cur = sb("kc_cur", [P, 16])
        vc_cur = sb("vc_cur", [16, P])
        near_c = sb("near_c", [P, 2, NCMP])
        score_c = sb("score_c", [P, 2, NCMP])
        prob_c = sb("prob_c", [P, 2, NCMP])
        probT_c = sb("probT_c", [16, T])
        stat = sb("stat", [P, 4, 2, 3])
        xpad = score[:, :, 0:T + 4]

        apart_sem = ctx.enter_context(nc.semaphore("apart"))

        def apart(eng):
            eng.sem_inc(apart_sem, 1)

        step_sem = {n: ctx.enter_context(nc.semaphore(f"{n}_step")) for n in ("dve", "pool", "act")}
        block = ctx.enter_context(nc.Block())

        def after(n):
            return n + CREDIT

        def spans(eng, lv):
            m = 1 << lv
            bv = w5[:, 1, :].rearrange("p (n c m) -> p n c m", c=2, m=m)
            dv = wide_a[:, lv, :].rearrange("p (n c m) -> p n c m", c=2, m=m)
            ref = bv[:, :, 0, m - 1:m].to_broadcast([P, P // m, m])
            yield eng.tensor_tensor(dv[:, :, 0, :], ref, bv[:, :, 0, :], ALU.subtract)
            yield eng.tensor_tensor(dv[:, :, 1, :], bv[:, :, 1, :], ref, ALU.subtract)
        @block.sync
        def _(sp):
            def fill(ph, ld, i, first):
                if ld.src is None:
                    sp.wait_ge(c_in_ready, after(i))
                    sp.wait_ge(bu_ready, after(4 * i))
                    sp.dma_start(ring[:, ld.slot, 0:512], a["s5_bc"][ds(i, 1)].rearrange("a p n -> (a p) n"))\
                        .then_inc(landed[ld.slot], 16)
                    for e in range(2):
                        rows = a["rel"][ds(2 * i + e, 1)].rearrange("a p n -> (a p) n")
                        sp.dma_start(ring[:, ld.slot, 512 + e * T:768 + e * T], rows)\
                            .then_inc(landed[ld.slot], 16)
                    return
                if first:
                    if ld.free0:
                        sp.wait_ge(used, ld.free0)
                else:
                    back, unit = ld.free_later
                    sp.wait_ge(used, ph.base + (i + back) * ph.units + unit)
                sp.dma_start(ring[:, ld.slot, 0:ld.width], ld.src(i)).then_inc(landed[ld.slot], 16)

            sp.dma_start(par[:, :], a["params"]).then_inc(par_in, 16)
            square_mats = CONSTS["ones"][0] + P
            sp.dma_start(con[:, 0:square_mats], a["consts"][:, 0:square_mats]).then_inc(ones_in, 16)
            for c in range(4):
                sp.dma_start(x[:, 4 * c:4 * c + 4, :], a["xT"][4 * c:4 * c + 4].rearrange("k p t -> p k t"))\
                    .then_inc(x_in[c], 16)
            sp.dma_start(con[:, square_mats:], a["consts"][:, square_mats:]).then_inc(con_in, 16)
            for ph in phases:
                if ph is forget:
                    sp.wait_ge(bu_ready, after(4 * PAIRS))
                for ld in ph.loads:
                    fill(ph, ld, 0, True)
                if ph.turns > 1:
                    with sp.Fori(1, ph.turns) as i:
                        for ld in ph.loads:
                            fill(ph, ld, i, False)
            for c in range(4):
                sp.wait_ge(x_final, after(4 * c + 4))
                sp.dma_start(out[4 * c:4 * c + 4].rearrange("k p t -> p k t"), x[:, 4 * c:4 * c + 4, :])\
                    .then_inc(stored, 16)
            sp.wait_ge(stored, 64)

        @block.tensor
        def _(pe):
            def product(ph, i, n, dst, k0=0, k1=KT, h_from=None):
                if k0 == 0:
                    wait_load(pe, ph, i, n)
                for k in range(k0, k1):
                    if h_from is not None:
                        pe.wait_ge(h_ready, after(h_from + k + 1))
                    mm = pe.matmul(dst[:, 0:T], tile(ph, n, k), h[:, k, :], start=k == 0, stop=k == KT - 1)
                if k1 == KT:
                    mm.then_inc(used, 1)

            def values(ph, i, n, dst):
                wait_load(pe, ph, i, n)
                for tt in range(2):
                    for k in range(KT):
                        mm = pe.matmul(dst[:, tt * P:(tt + 1) * P], h[:, k, tt * P:(tt + 1) * P], tile(ph, n, k),
                                       start=k == 0, stop=k == KT - 1)
                mm.then_inc(used, 1)

            def norm(out_n):
                pe.wait_ge(ssq_ready, after(out_n + 1))
                pe.matmul(bank[7][:, 0:T], ones, ssq[:, :], start=True, stop=True).then_inc(sum_ready, 1)

            def norm_of_squares(n):
                for k in range(KT):
                    if k % 4 == 0:
                        pe.wait_ge(squares, after(4 * n + k // 4 + 1))
                    mm = pe.matmul(bank[7][:, 0:T], ones, mix[:, k, :], start=k == 0, stop=k == KT - 1)
                mm.then_inc(sum_ready, 1)

            def out_proj(ph, ktiles, first_block, unit, last_tiles):
                with pe.Fori(0, 4) as i:
                    at = 0
                    for b in range(4):
                        pe.wait_ge(x_added, after(first_block + 4 * i + b - 1))
                        for k in range(ktiles):
                            if at % TILES == 0:
                                wait_load(pe, ph, i, at // TILES)
                            if b == 0 and k == last_tiles[0]:
                                pe.wait_ge(*last_tiles[1:])
                            mm = pe.matmul(bank[b % 2][:, 0:T], tile(ph, at // TILES, at % TILES), mix[:, k, :],
                                           start=k == 0, stop=k == ktiles - 1)
                            at += 1
                            if at % unit == 0:
                                mm.then_inc(used, 1)

            def causal_scores(dst, keys, queries=qT):
                for c0, width, q0 in ((0, P, 0), (P, T, P)):
                    mm = pe.matmul(dst[:, c0:c0 + width], queries[:, q0:q0 + P], keys[:, 0:width],
                                   start=True, stop=True)
                return mm

            def turn_probs(dst, src):
                for c in range(3):
                    mm = pe.transpose(dst[:, c * P:(c + 1) * P], src[:, c * P:(c + 1) * P], ident)
                return mm

            pe.wait_ge(ones_in, 16)
            norm_of_squares(0)
            def pair(i, last):
                misc = ring[:, 6, :]

                def drive(t):
                    pe.wait_ge(bu_used, after(4 * i + t))
                    for c in range(2):
                        mm = pe.matmul(bank[6][:, c * T:(c + 1) * T], misc[32 * t:32 * t + 32, c * P:(c + 1) * P],
                                       uT[32 * t:32 * t + 32, :], start=True, stop=True)
                    mm.then_inc(bu_ready, 1)

                def read_out(t):
                    pe.wait_ge(state_ready, after(8 * i + 2 * t + 2))
                    if t == 0:
                        pe.wait_ge(c_in_ready, after(i + 1))
                        pe.wait_ge(y_used, after(i))
                    for c in range(2):
                        mm = pe.matmul(bank[7][32 * t:32 * t + 32, 0:T], c_in[:, c, 32 * t:32 * t + 32],
                                       w6[:, t % 2, c, :], start=c == 0, stop=c == 1)
                    mm.then_inc(y_ready, 1)

                def turn_head(e):
                    pe.wait_ge(p_ready, after(2 * i + e + 1))
                    pe.wait_ge(pt_used, after(2 * i + e))
                    turn_probs(bank[4], prob[:, e, :]).then_inc(pt_ready, 1)

                pe.wait_ge(zb_used, after(i))
                product(even1, i, 1, bank[1])
                pe.wait_ge(u_ready, after(i + 1))
                wait_load(pe, even1, i, 4)
                drive(0)
                product(even1, i, 2, bank[0])
                drive(1)
                pe.wait_ge(q_ready, after(i + 1))
                values(even1, i, 3, bank[1])
                pe.wait_ge(k_ready, after(i + 1))
                pe.wait_ge(bias_masked, after(i + 1))
                for e in range(2):
                    qk = slice(64 * e, 64 * e + 64)
                    bias = misc[:, 512 + e * T:768 + e * T]
                    for c0, width, q0 in ((0, P, 0), (P, T, P)):
                        dst = bank[2 + e][:, c0:c0 + width]
                        pe.matmul(dst, qT[qk, q0:q0 + P], kT[qk, 0:width], start=True, stop=False)
                        mm = pe.matmul(dst, flip, bias[:, T - width:T], start=False, stop=True)
                    mm.then_inc(s_ready, 1)
                drive(2)
                product(even1, i, 5, bank[0])
                read_out(0)
                pe.wait_ge(v_ready, after(i + 1))
                product(even1, i, 6, bank[1], 0, 9)
                drive(3)
                turn_head(0)
                read_out(1)
                product(even1, i, 6, bank[1], 9, 13)
                turn_head(1)
                product(even1, i, 6, bank[1], 13, KT)
                pe.wait_ge(o_used, after(i))
                for e in range(2):
                    pe.wait_ge(pt_used, after(2 * i + e + 1))
                    dst = bank[5][64 * e:64 * e + 64, 0:T]
                    pe.matmul(dst, vN[:, 64 * e:64 * e + 64], probT[:, e, 0:T], start=True, stop=False)
                    mm = pe.matmul(dst[:, P:T], vN[:, P + 64 * e:P + 64 * e + 64], probT[:, e, T:T + P],
                                   start=False, stop=True)
                mm.then_inc(o_ready, 1)
                if not last:
                    pe.wait_ge(za_used, after(i + 1))
                    product(even1, i + 1, 0, bank[0])
                read_out(2)
                read_out(3)

            product(even1, 0, 0, bank[0], h_from=0)
            with pe.Fori(0, PAIRS - 1) as i:
                pair(i, False)
            pair(PAIRS - 1, True)
            pe.wait_ge(y_mixed, after(PAIRS - 1))
            pe.wait_ge(za_used, after(PAIRS))
            pe.wait_ge(zb_used, after(PAIRS))
            with pe.Fori(0, 2) as i:
                for b in range(4):
                    pe.wait_ge(glu_t, after(4 * i + b - 1))
                    if b % 2 == 0:
                        wait_load(pe, glu, i, b // 2)
                    for k in range(8):
                        if (b, k) == (0, 7):
                            pe.wait_ge(y_mixed, after(PAIRS))
                        mm = pe.matmul(bank[b % 2][:, 0:T], tile(glu, b // 2, 8 * (b % 2) + k), mix[:, 16 + k, :],
                                       start=k == 0, stop=k == 7)
                    mm.then_inc(used, 1)
            pe.wait_ge(o_used, after(PAIRS))
            pe.wait_ge(glu_t, after(7))
            pe.wait_ge(glu_mixed, after(6))
            out_proj(out1, 16, 0, 16, (14, glu_mixed, after(8)))
            norm(0)
            wait_load(pe, forget, 0, 0)
            for k in range(KT):
                pe.wait_ge(h_ready, after(KT + k + 1))
                mm = pe.matmul(bank[6][0:HEADS, 0:T], ring[:, 6, k * HEADS:(k + 1) * HEADS], h[:, k, :],
                               start=k == 0, stop=k == KT - 1)
            mm.then_inc(used, 1)
            with pe.Fori(0, HEADS) as i:
                pe.wait_ge(q_ready, after(PAIRS + i))
                pe.wait_ge(v_ready, after(PAIRS + i))
                product(odd1, i, 0, bank[0])
                pe.wait_ge(z_used, after(i))
                product(odd1, i, 1, bank[1])
                pe.wait_ge(q_ready, after(PAIRS + i + 1))
                values(odd1, i, 2, bank[0])
                pe.wait_ge(k_ready, after(PAIRS + i + 1))
                pe.wait_ge(ck_ready, after(i + 1))
                for c0, width, q0 in ((0, P, 0), (P, T, P)):
                    dst = bank[2][:, c0:c0 + width]
                    pe.matmul(dst, qT[:, q0:q0 + P], kT[:, 0:width], start=True, stop=False)
                    mm = pe.matmul(dst, ones[0:16, :], ck[:, 0:width], start=False, stop=True)
                mm.then_inc(s_ready, 1)
                product(odd1, i, 3, bank[1], 0, 9)
                pe.wait_ge(p_ready, after(2 * PAIRS + i + 1))
                turn_probs(bank[4], prob[:, 0, :]).then_inc(pt_ready, 1)
                product(odd1, i, 3, bank[1], 9, KT)
                pe.wait_ge(pt_used, after(2 * PAIRS + i + 1))
                pe.wait_ge(v_ready, after(PAIRS + i + 1))
                pe.wait_ge(o_used, after(PAIRS + i))
                pe.matmul(bank[5][:, 0:T], vN[:, 0:P], probT[:, 0, 0:T], start=True, stop=False)
                pe.matmul(bank[5][:, P:T], vN[:, P:T], probT[:, 0, T:T + P], start=False, stop=True)\
                    .then_inc(o_ready, 1)
            out_proj(out2, 16, 16, 16, (15, o_used, after(PAIRS + HEADS)))
            norm(1)
            norm_of_squares(1)
            def head(i, last):
                kk, qs = w9[:, 0, :], w9[:, 1, :]

                def level(pos, lv):
                    pe.wait_ge(lv_used, after(8 * i + max(pos - 3, 0)))
                    dst = bank[LEVEL_BANKS[pos % 4]][:, 0:T]
                    for b in range(2):
                        cols = slice(b * P, (b + 1) * P)
                        if lv < LEVELS:
                            mm = pe.matmul(dst[:, cols], wide_b[:, lv, cols], wide_b[:, lv, cols],
                                           start=True, stop=True)
                        else:
                            mm = pe.matmul(dst[:, cols], kk[:, cols], qs[:, cols], start=True, stop=True)
                    mm.then_inc(lv_ready, 1)

                pe.wait_ge(hg_used, after(i))
                product(hgrn, i, 1, bank[1])
                pe.wait_ge(hf_in, after(i + 1))
                values(hgrn, i, 2, bank[0])
                pe.wait_ge(hq_used, after(i + 1))
                product(hgrn, i, 3, bank[1], 0, 4)
                pe.wait_ge(w_low, after(i + 1))
                for pos, lv in enumerate(LEVEL_ORDER[0:5]):
                    level(pos, lv)
                product(hgrn, i, 3, bank[1], 4, 7)
                pe.wait_ge(w_high, after(8 * i + 8))
                for pos in range(5, 8):
                    level(pos, LEVEL_ORDER[pos])
                pe.wait_ge(h_mixed, after(i))
                pe.matmul(bank[4][:, 0:P], wide_b[:, 7, 0:P], wide_b[:, 7, P:T], start=True, stop=True)\
                    .then_inc(att_far, 1)
                product(hgrn, i, 3, bank[1], 7, 9)
                pe.wait_ge(lv_used, after(8 * i + 8))
                pe.wait_ge(att_ready, after(i + 1))
                pe.wait_ge(hv_ready, after(i + 1))
                pe.matmul(bank[5][:, 0:P], small[:, 0:P], vN[:, 0:P], start=True, stop=True)
                pe.matmul(bank[5][:, P:T], small[:, P:T], vN[:, P:T], start=True, stop=False)
                pe.matmul(bank[5][:, P:T], near[:, 0:P], vN[:, 0:P], start=False, stop=True).then_inc(ho_ready, 1)
                product(hgrn, i, 3, bank[1], 9, KT)
                if not last:
                    pe.wait_ge(hv_ready, after(i + 1))
                    product(hgrn, i + 1, 0, bank[0])
                pe.wait_ge(ho_norm, after(i + 1))
                for tt in range(2):
                    mm = pe.transpose(bank[4][:, tt * P:(tt + 1) * P], w6[:, 0, 0, tt * P:(tt + 1) * P], ident)
                mm.then_inc(ht_ready, 1)

            product(hgrn, 0, 0, bank[0], h_from=3 * KT)
            with pe.Fori(0, HEADS - 1) as i:
                head(i, False)
            head(HEADS - 1, True)
            pe.wait_ge(hg_used, after(HEADS))
            pe.wait_ge(h_mixed, after(HEADS))
            wait_load(pe, gates, 0, 0)
            for tt in range(2):
                for k in range(KT):
                    mm = pe.matmul(bank[6][:, tt * 48:(tt + 1) * 48], h[:, k, tt * P:(tt + 1) * P],
                                   ring[:, 4, k * 48:(k + 1) * 48], start=k == 0, stop=k == KT - 1)
            mm.then_inc(used, 1)
            with pe.Fori(0, GROUPS) as i:
                for n in range(2):
                    pe.wait_ge(ckv_ready, after(2 * i + n - 1))
                    product(cmp_in, i, n, bank[n])
            for n in range(2):
                pe.wait_ge(cblk_ready, after(n + 1))
                blk = (wide_a, wide_c)[n].rearrange("p k t -> p (k t)")
                for l in range(CMP_LEN):
                    if l % TILES == 0:
                        wait_load(pe, cmp_w1, 0, 2 * n + l // TILES)
                    mm = pe.matmul(bank[2 + n][:, 0:GROUPS * NCMP], tile(cmp_w1, 2 * n + l // TILES, l % TILES),
                                   blk[:, l * GROUPS * NCMP:(l + 1) * GROUPS * NCMP], start=l == 0,
                                   stop=l == CMP_LEN - 1)
                    if l % TILES == TILES - 1:
                        mm.then_inc(used, 1)
            wait_load(pe, cmp_w1, 0, 4)
            pe.wait_ge(c_silu, after(1))
            pe.matmul(bank[4][:, 0:GROUPS * NCMP], ring[:, 4, 0:P], w2[:, 0, 0:GROUPS * NCMP], start=True, stop=True)\
                .then_inc(c_out, 1)
            pe.wait_ge(c_silu, after(2))
            for g in range(GROUPS):
                mm = pe.matmul(bank[5][0:NCMP, g * P:(g + 1) * P], w2[:, 1, g * NCMP:(g + 1) * NCMP],
                               ring[:, 4, P:2 * P], start=True, stop=True)
            mm.then_inc(used, 1)
            pe.wait_ge(c_kept, after(2))
            pe.wait_ge(ckv_ready, after(2 * GROUPS))
            q_base, o_base, g_base = PAIRS + HEADS, PAIRS + HEADS, HEADS
            s_base = 2 * PAIRS + HEADS
            def group(i, last):
                def finish(e, half):
                    n = 4 * i + e
                    if half == 0:
                        pe.wait_ge(p_ready, after(s_base + n + 1))
                        turn_probs(bank[4], prob[:, 0, :])
                        turn_probs(bank[7], prob[:, 1, :])
                        for tt in range(2):
                            mm = pe.transpose(bank[6][0:NCMP, T + tt * P:T + (tt + 1) * P], prob_c[:, tt, :], ident)
                        mm.then_inc(pt_ready, 1)
                        return
                    pe.wait_ge(pt_used, after(s_base + 2 * n + 2))
                    pe.wait_ge(cur_kv, after(2 * i + 2))
                    pe.wait_ge(o_used, after(o_base + n))
                    o = bank[5][:, 0:T]
                    pe.matmul(o, vc_cur[0:NCMP, :], probT_c[0:NCMP, :], start=True, stop=False)
                    for b, v in enumerate((vN, vN2)):
                        pe.matmul(o, v[:, 0:P], probT[:, b, 0:T], start=False, stop=False)
                        mm = pe.matmul(o[:, P:T], v[:, P:T], probT[:, b, T:T + P], start=False, stop=b == 1)
                    mm.then_inc(o_ready, 1)

                pe.wait_ge(z_used, after(g_base + 4 * i))
                values(nsa, i, 1, bank[1])
                pe.wait_ge(nkv_ready, after(4 * i + 1))
                product(nsa, i, 2, bank[0])
                pe.wait_ge(nkv_ready, after(4 * i + 2))
                values(nsa, i, 3, bank[1])
                for e in range(HPG):
                    n = 4 * i + e
                    pe.wait_ge(q_ready, after(q_base + n))
                    pe.wait_ge(nkv_ready, after(4 * i + 3))
                    product(nsa, i, 4 + 2 * e, bank[0])
                    if e:
                        finish(e - 1, 0)
                    pe.wait_ge(z_used, after(g_base + n))
                    pe.wait_ge(nkv_ready, after(4 * i + 4))
                    product(nsa, i, 5 + 2 * e, bank[1], 0, 4)
                    if e:
                        finish(e - 1, 1)
                    pe.wait_ge(q_ready, after(q_base + n + 1))
                    pe.wait_ge(cur_kv, after(2 * i + 2))
                    causal_scores(bank[2], kT)
                    causal_scores(bank[3], kT2)
                    for tt in range(2):
                        mm = pe.matmul(bank[6][:, tt * NCMP:(tt + 1) * NCMP], qT[:, tt * P:(tt + 1) * P],
                                       kc_cur[:, 0:NCMP], start=True, stop=True)
                    mm.then_inc(s_ready, 1)
                    product(nsa, i, 5 + 2 * e, bank[1], 4, KT)
                finish(HPG - 1, 0)
                if not last:
                    pe.wait_ge(q_ready, after(q_base + 4 * i + 4))
                    product(nsa, i + 1, 0, bank[0])
                finish(HPG - 1, 1)

            product(nsa, 0, 0, bank[0])
            with pe.Fori(0, GROUPS - 1) as i:
                group(i, False)
            group(GROUPS - 1, True)
            out_proj(out3, 32, 32, 16, (31, o_used, after(o_base + HEADS)))
            norm(2)
            with pe.Fori(0, RGB) as i:
                pe.wait_ge(xb_ready, after(2 * i))
                product(rg, i, 0, bank[0][:, 0:T], h_from=4 * KT)
                product(rg, i, 1, bank[1][:, 0:T])
                pe.wait_ge(rgg_used, after(i))
                product(rg, i, 2, bank[4][:, 0:T])
                pe.wait_ge(xc_ready, after(2 * i + 2))
                wait_load(pe, rg, i, 4)
                pe.wait_ge(rg_pre, after(i))
                for g in range(2):
                    for e in range(2):
                        for c in range(2):
                            mm = pe.matmul(bank[2 + g][:, e * T:(e + 1) * T], tile(rg, 4, 4 * g + 2 * e + c),
                                           w2[:, c, :], start=c == 0, stop=c == 1)
                mm.then_inc(used, 1)
                product(rg, i, 3, bank[5][:, 0:T])
            pe.wait_ge(rg_mixed, after(RGB - 1))
            out_proj(out4, 20, 48, 4, (18, rg_mixed, after(RGB)))
            norm(3)

        @block.scalar
        def _(s):
            st = Steps(s, step_sem["act"])

            def norm(n):
                st.mark(s.activation(unused[:, :], ccol("eps"), ACT.Ln))
                st.settle()
                s.wait_ge(sum_ready, after(n + 1))
                st.mark(s.activation(rstd[:, :], bank[7][:, 0:T], ACT.Ln, bias=ccol("eps"), scale=1.0 / D))
                st.settle()
                s.activation(rstd[:, :], rstd[:, :], ACT.Exp, scale=-0.5).then_inc(rms_guess, 1)

            def out_squares(first_block):
                with s.Fori(0, 4) as i:
                    for b in range(4):
                        s.wait_ge(x_added, after(first_block + 4 * i + b + 1))
                        s.activation(sq[:, b % 2, :], x[:, ds(4 * i + b, 1), :].rearrange("p a t -> p (a t)"),
                                     ACT.Square).then_inc(sq_ready, 1)

            def exps(src, dst, neg, sums):
                for tt, cols in ((0, slice(0, P)), (1, slice(P, 384))):
                    ins = s.activation(dst[:, cols], src[:, cols], ACT.Exp, bias=neg[tt], accum_out=sums[tt])
                return ins

            s.wait_ge(par_in, 16)
            s.activation(s5t[:, 0, :], pcol("log_dt"), ACT.Exp).then_inc(s5_act, 1)
            s.wait_ge(s5_mid, after(1))
            s.activation(s5[:, 0, 0:32], s5t[:, 1, :], ACT.Exp).then_inc(s5_act, 1)
            s.wait_ge(sp_in, after(1))
            st.mark(s.activation(rgt[:, 1, :], rgt[:, 0, :], ACT.Exp, scale=-1.0))
            s.activation(lbt[:, 1, :], lbt[:, 0, :], ACT.Exp).then_inc(sp_exp, 1)
            s.wait_ge(s5_mid, after(2))
            st.mark(s.activation(s5t[:, 5, :], s5t[:, 3, :], ACT.Sin))
            s.activation(s5t[:, 6, :], s5t[:, 4, :], ACT.Sin).then_inc(s5_act, 1)
            for c in range(4):
                s.wait_ge(x_in[c], 16)
                s.activation(mix[:, 4 * c:4 * c + 4, :], x[:, 4 * c:4 * c + 4, :], ACT.Square).then_inc(squares, 1)
            s.wait_ge(con_in, 16)
            norm(0)
            turns = wide_a[:, :, :].rearrange("p (t c) n -> p t c n", c=2)
            trig = wide_c[:, :, :].rearrange("p (t c) n -> p t c n", c=2)
            with s.Fori(0, PAIRS) as i:
                s.wait_ge(used, done(even1, i, 1))
                s.wait_ge(y_used, after(i))
                s.activation(uT[:, :], bank[0][:, 0:T], ACT.Copy).then_inc(u_ready, 1)
                s.wait_ge(used, done(even1, i, 2))
                s.activation(qT[:, :], bank[1][:, 0:T], ACT.Copy, scale=64 ** -0.5).then_inc(q_ready, 1)
                s.wait_ge(phase_ready, after(i + 1))
                s.wait_ge(rot_used, after(4 * i))
                st.enter(i, 1)
                st.mark(s.activation(trig[:, :, 0, :], turns[:, :, 0, :], ACT.Sin, scale=-TURN))
                s.activation(trig[:, :, 1, :], turns[:, :, 1, :], ACT.Sin, scale=-TURN, bias=ccol("half_pi"))\
                    .then_inc(trig_ready, 1)
                st.leave(PAIRS)
                s.wait_ge(used, done(even1, i, 3))
                s.activation(kT[:, :], bank[0][:, 0:T], ACT.Copy).then_inc(k_ready, 1)
                s.wait_ge(used, done(even1, i, 4))
                s.activation(vN[:, :], bank[1][:, 0:T], ACT.Copy).then_inc(v_ready, 1)
                for e in range(2):
                    s.wait_ge(m_ready, after(2 * i + e + 1))
                    exps(bank[2 + e], prob[:, e, :], [nmax[:, e, t:t + 1] for t in range(2)],
                         [psums[:, e, t:t + 1] for t in range(2)]).then_inc(e_ready, 1)
                s.wait_ge(used, done(even1, i, 5))
                s.activation(gate[:, :], bank[0][:, 0:T], ACT.Tanh, scale=0.5).then_inc(za_tanh, 1)
                for e in range(2):
                    s.wait_ge(pt_ready, after(2 * i + e + 1))
                    s.activation(probT[:, e, :], bank[4][:, 0:384], ACT.Copy).then_inc(pt_used, 1)
                s.wait_ge(used, done(even1, i, 6))
                s.activation(sq[:, 0, :], bank[1][:, 0:T], ACT.Tanh, scale=0.5).then_inc(zb_tanh, 1)
                s.wait_ge(gelu_in, after(i + 1))
                s.activation(sq[:, 1, :], w4[:, 1, :], ACT.Tanh, scale=GELU_S).then_inc(gelu_t, 1)
            with s.Fori(0, 2) as i:
                for b in range(4):
                    s.wait_ge(used, done(glu, i, b + 1))
                    s.wait_ge(glu_mixed, after(4 * i + b - 1))
                    s.activation(sq[:, b % 2, :], bank[b % 2][:, 0:T], ACT.Tanh, bias=bgh[:, ds(4 * i + b, 1)],
                                 scale=0.5).then_inc(glu_t, 1)
            out_squares(0)
            norm(1)
            s.wait_ge(f_in, after(1))
            st.mark(s.activation(fl[:, 2, :], fl[:, 1, :], ACT.Exp, scale=-1.0))
            st.settle()
            s.activation(fl[:, 3, :], fl[:, 2, :], ACT.Ln, bias=ccol("ones", 0, 1)[0:16, :]).then_inc(f_ln, 1)
            with s.Fori(0, HEADS) as i:
                s.wait_ge(used, done(odd1, i, 1))
                s.activation(qT[:, :], bank[0][:, 0:T], ACT.Copy, scale=P ** -0.5).then_inc(q_ready, 1)
                s.wait_ge(used, done(odd1, i, 2))
                s.activation(kT[:, :], bank[1][:, 0:T], ACT.Copy).then_inc(k_ready, 1)
                s.wait_ge(used, done(odd1, i, 3))
                s.activation(vN[:, :], bank[0][:, 0:T], ACT.Copy).then_inc(v_ready, 1)
                s.wait_ge(m_ready, after(2 * PAIRS + i + 1))
                exps(score[:, 0, :], prob[:, 0, :], [nmax[:, 0, t:t + 1] for t in range(2)],
                     [psums[:, 0, t:t + 1] for t in range(2)]).then_inc(e_ready, 1)
                s.wait_ge(pt_ready, after(2 * PAIRS + i + 1))
                s.activation(probT[:, 0, :], bank[4][:, 0:384], ACT.Copy).then_inc(pt_used, 1)
                s.wait_ge(used, done(odd1, i, 4))
                s.activation(gate[:, :], bank[1][:, 0:T], ACT.Tanh, scale=0.5).then_inc(z_tanh, 1)
            out_squares(16)
            norm(2)
            for c in range(4):
                s.wait_ge(h_ready, after(2 * KT + 4 * c + 4))
                s.activation(mix[:, 4 * c:4 * c + 4, :], x[:, 4 * c:4 * c + 4, :], ACT.Square).then_inc(squares, 1)
            norm(3)
            with s.Fori(0, HEADS) as i:
                st.enter(i, 4)
                s.wait_ge(hf_in, after(i + 1))
                s.activation(w2[:, 1, :], w2[:, 0, :], ACT.Exp, scale=-1.0).then_inc(hf_exp, 1)
                s.wait_ge(hf_split, after(i + 1))
                st.mark(s.activation(w8[:, 0, :], w4[:, 0, :], ACT.Ln))
                s.activation(w8[:, 1, :], w4[:, 1, :], ACT.Ln, scale=1.0 / SPLIT).then_inc(hf_ln, 1)
                s.wait_ge(used, done(hgrn, i, 2))
                s.activation(gate[:, :], bank[1][:, 0:T], ACT.Tanh, scale=0.5).then_inc(hq_tanh, 1)
                s.wait_ge(span_low, after(i + 1))
                s.activation(wide_b[:, 0:4, :], wide_a[:, 0:4, :], ACT.Exp).then_inc(decay_low, 1)
                s.wait_ge(span_ready, after(12 * i + 12))
                s.activation(wide_b[:, 4:8, :], wide_a[:, 4:8, :], ACT.Exp).then_inc(decay_ready, 1)
                s.wait_ge(used, done(hgrn, i, 3))
                s.activation(vN[:, :], bank[0][:, 0:T], ACT.Copy).then_inc(hv_ready, 1)
                s.wait_ge(att_far, after(i + 1))
                s.activation(near[:, 0:P], bank[4][:, 0:P], ACT.Copy).then_inc(att_ready, 1)
                s.wait_ge(ho_ready, after(i + 1))
                for tt in range(2):
                    st.mark(s.activation(w6[:, 1, 0, tt * P:(tt + 1) * P], bank[5][:, tt * P:(tt + 1) * P], ACT.Square,
                                         accum_out=stat[:, 0, tt, 0:1]))
                st.settle()
                st.mark(s.activation(stat[:, 1, :, 0], stat[:, 0, :, 0], ACT.Ln, bias=ccol("eps"), scale=1.0 / P))
                st.settle()
                s.activation(stat[:, 2, :, 0], stat[:, 1, :, 0], ACT.Exp, scale=-0.5).then_inc(ho_guess, 1)
                s.wait_ge(used, done(hgrn, i, 4))
                s.wait_ge(hq_used, after(i + 1))
                s.activation(gate[:, :], bank[1][:, 0:T], ACT.Tanh, scale=0.5).then_inc(hg_tanh, 1)
                st.leave(HEADS)
            s.wait_ge(used, done(gates, 0, 1))
            s.activation(w2[:, 0, 0:96], bank[6][:, 0:96], ACT.Exp, scale=-1.0).then_inc(gate_exp, 1)
            with s.Fori(0, GROUPS) as i:
                for n in range(2):
                    s.wait_ge(used, done(cmp_in, i, n + 1))
                    s.activation(wide_b[:, ds(i + 4 * n, 1), :].rearrange("p a t -> p (a t)"), bank[n][:, 0:T],
                                 ACT.Copy).then_inc(ckv_ready, 1)
            for n in range(2):
                s.wait_ge(used, done(cmp_w1, 0, 2 * n + 2))
                s.activation(w3[:, n, 0:GROUPS * NCMP], bank[2 + n][:, 0:GROUPS * NCMP], ACT.Tanh, scale=0.5)\
                    .then_inc(c_tanh, 1)
            s.wait_ge(c_out, after(1))
            s.activation(Kc[:, :], bank[4][:, 0:GROUPS * NCMP], ACT.Copy).then_inc(c_kept, 1)
            s.wait_ge(used, done(cmp_w1, 0, 5))
            s.activation(Vc[0:NCMP, :, :], bank[5][0:NCMP, :].rearrange("p (g d) -> p g d", g=GROUPS), ACT.Copy)\
                .then_inc(c_kept, 1)
            s_base = 2 * PAIRS + HEADS
            with s.Fori(0, GROUPS) as i:
                for n, (dst, b) in enumerate(((kT, 0), (vN, 1), (kT2, 0), (vN2, 1))):
                    s.wait_ge(used, done(nsa, i, n + 1))
                    s.activation(dst[:, :], bank[b][:, 0:T], ACT.Copy).then_inc(nkv_ready, 1)

                def keep_turned(e):
                    s.wait_ge(pt_ready, after(s_base + 4 * i + e + 1))
                    s.activation(probT_c[0:NCMP, :], bank[6][0:NCMP, T:2 * T], ACT.Copy)
                    s.activation(probT[:, 0, :], bank[4][:, 0:384], ACT.Copy).then_inc(pt_used, 1)
                    s.activation(probT[:, 1, :], bank[7][:, 0:384], ACT.Copy).then_inc(pt_used, 1)

                for e in range(HPG):
                    s.wait_ge(used, done(nsa, i, 5 + 2 * e))
                    s.activation(qT[:, :], bank[0][:, 0:T], ACT.Copy, scale=P ** -0.5).then_inc(q_ready, 1)
                    if e:
                        keep_turned(e - 1)
                    s.wait_ge(m_ready, after(s_base + 4 * i + e + 1))
                    for tt in range(2):
                        s.activation(prob_c[:, tt, :], score_c[:, tt, :], ACT.Exp, bias=stat[:, 1, tt, 0:1],
                                     accum_out=stat[:, 2, tt, 0:1])
                    exps(score[:, 0, :], prob[:, 0, :], [stat[:, 1, t, 1:2] for t in range(2)],
                         [stat[:, 2, t, 1:2] for t in range(2)])
                    exps(score[:, 1, :], prob[:, 1, :], [stat[:, 1, t, 2:3] for t in range(2)],
                         [stat[:, 2, t, 2:3] for t in range(2)]).then_inc(e_ready, 1)
                    s.wait_ge(used, done(nsa, i, 6 + 2 * e))
                    s.activation(gate[:, :], bank[1][:, 0:T], ACT.Tanh, scale=0.5).then_inc(z_tanh, 1)
                keep_turned(HPG - 1)
            out_squares(32)
            norm(4)
            with s.Fori(0, RGB) as i:
                for c in range(2):
                    s.wait_ge(used, done(rg, i, c + 1))
                    s.wait_ge(xc_ready, after(2 * i))
                    s.activation(xpad[:, c, 4:T + 4], bank[c][:, 0:T], ACT.Copy).then_inc(xb_ready, 1)
                s.wait_ge(used, done(rg, i, 4))
                for c in range(2):
                    s.activation(w3[:, c, :], bank[2][:, c * T:(c + 1) * T], ACT.Exp, scale=-1.0,
                                 bias=cur[:, 8 * c + RG_COLS["ba"]:8 * c + RG_COLS["ba"] + 1])
                for c in range(2):
                    ins = s.activation(w4[:, c, :], bank[3][:, c * T:(c + 1) * T], ACT.Tanh, scale=0.5,
                                       bias=cur[:, 8 * c + RG_COLS["bi"]:8 * c + RG_COLS["bi"] + 1])
                ins.then_inc(rg_pre, 1)
                s.wait_ge(rg_r, after(i + 1))
                for func, dst in ((ACT.Exp, w8), (ACT.Tanh, w9)):
                    for c in range(2):
                        ins = s.activation(dst[:, c, :], w5[:, c, :], func,
                                           scale=cur[:, 8 * c + RG_COLS["lam"]:8 * c + RG_COLS["lam"] + 1])
                ins.then_inc(rg_a, 1)
                s.wait_ge(rg_v, after(i + 1))
                s.activation(w6[:, 0, :, :], w3[:, :, :], ACT.Sqrt, scale=0.25).then_inc(rg_s, 1)
                s.wait_ge(used, done(rg, i, 5))
                s.activation(wide_a[:, 0:2, :], psum[:, 4:6, 0:T], ACT.Tanh, scale=0.5)\
                    .then_inc(rgg_tanh, 1)
            out_squares(48)
            norm(5)

        @block.gpsimd
        def _(g):
            for sem in signals:
                g.sem_inc(sem, CREDIT)
            st = Steps(g, step_sem["pool"])
            with g.Fori(0, PAIRS) as i:
                for t in range(4):
                    g.wait_ge(rot_used, after(4 * i + t + 1))
                    g.wait_ge(y_ready, after(4 * i + max(t - 1, 0)))
                    g.tensor_tensor(w6[:, t % 2, 0, :], w8[:, 0, :], w9[:, 1, :], ALU.add).then_inc(state_ready, 1)
                    g.tensor_tensor(w6[:, t % 2, 1, :], w9[:, 0, :], w8[:, 1, :], ALU.subtract).then_inc(state_ready, 1)
            g.wait_ge(con_in, 16)
            with g.Fori(0, HEADS) as i:
                b = w5[:, 1, :]
                g.wait_ge(hb_ready, after(i + 1))
                g.wait_ge(decay_ready, after(i))
                for lv in range(4, LEVELS - 1):
                    for ins in spans(g, lv):
                        ins.then_inc(span_ready, 1)
                bv = b.rearrange("p (n c m) -> p n c m", c=2, m=CHUNK)
                dv = wide_a[:, LEVELS - 1, :].rearrange("p (n c m) -> p n c m", c=2, m=CHUNK)
                last = bv[:, :, 0, CHUNK - 1:CHUNK].to_broadcast([P, 2, CHUNK])
                g.tensor_tensor(dv[:, :, 0, :], last, bv[:, :, 0, :], ALU.subtract).then_inc(span_ready, 1)
                g.tensor_copy(dv[:, :, 1, :], bv[:, :, 1, :]).then_inc(span_ready, 1)
                far = wide_a[:, LEVELS, :]
                c64 = [slice(CHUNK * n, CHUNK * (n + 1)) for n in range(4)]
                end = [b[:, CHUNK * n + CHUNK - 1:CHUNK * (n + 1)] for n in range(4)]
                g.tensor_scalar(far[:, c64[0]], b[:, c64[0]], -1.0, end[0], ALU.mult, ALU.add).then_inc(span_ready, 1)
                g.tensor_scalar(far[:, c64[1]], b[:, c64[1]], -1.0, end[1], ALU.mult, ALU.add).then_inc(span_ready, 1)
                g.tensor_copy(far[:, c64[2]], b[:, c64[2]]).then_inc(span_ready, 1)
                g.wait_ge(span_ready, after(12 * i + 9))
                apart(g)
                g.tensor_scalar(far[:, c64[0]], far[:, c64[0]], end[1], None, ALU.add).then_inc(span_ready, 1)
                g.tensor_scalar(far[:, c64[3]], b[:, c64[3]], end[2], None, ALU.add).then_inc(span_ready, 2)
                kk, qs = w9[:, 0, :], w9[:, 1, :]
                g.wait_ge(decay_ready, after(i + 1))
                g.wait_ge(hq_used, after(i + 1))
                for lv in range(4, LEVELS + 1):
                    m = 1 << lv
                    for c, src in ((0, kk), (1, qs)):
                        dv = wide_b[:, lv, :].rearrange("p (n c m) -> p n c m", c=2, m=m)[:, :, c, :]
                        sv = src.rearrange("p (n c m) -> p n c m", c=2, m=m)[:, :, c, :]
                        g.tensor_tensor(dv, dv, sv, ALU.mult).then_inc(w_high, 1)
            g.wait_ge(c_kept, after(2))
            g.wait_ge(ho_ready, after(HEADS))
            o_base, s_base = PAIRS + HEADS, 2 * PAIRS + HEADS
            with g.Fori(0, GROUPS) as i:
                st.enter(i, 1)
                g.wait_ge(near_ready, after(2 * HPG * i))
                st.mark(g.tensor_copy(slope[:, :], ccol("slopes")[:, ds(HPG * i, HPG)]))
                g.wait_ge(o_ready, after(o_base + 4 * i))
                g.tensor_copy(kc_cur[:, 0:NCMP], Kc[:, ds(NCMP * i, NCMP)]).then_inc(cur_kv, 1)
                g.tensor_copy(vc_cur[0:NCMP, :], Vc[0:NCMP, ds(i, 1), :].rearrange("p a d -> p (a d)"))\
                    .then_inc(cur_kv, 1)
                st.settle()
                for e in range(HPG):
                    g.wait_ge(m_ready, after(s_base + 4 * i + e))
                    apart(g)
                    g.tensor_scalar(near[:, :], ccol("alibi"), slope[:, e:e + 1], None, ALU.mult)\
                        .then_inc(near_ready, 1)
                    g.tensor_scalar(near_c[:, :, :].rearrange("p a n -> p (a n)"), ccol("alibi_c"),
                                    slope[:, e:e + 1], None, ALU.mult).then_inc(near_ready, 1)
                st.leave(GROUPS)

        @block.vector
        def _(v):
            st = Steps(v, step_sem["dve"])

            def then(instruction):
                st.mark(instruction)
                st.settle()

            def norm(n, gname, dst, ready):
                v.wait_ge(sum_ready, after(n + 1))
                v.wait_ge(rms_guess, after(n + 1))
                st.mark(v.tensor_scalar(nv[:, :], bank[7][:, 0:T], 1.0 / D, EPS, ALU.mult, ALU.add))
                then(v.tensor_tensor(nt[:, :], rstd[:, :], rstd[:, :], ALU.mult))
                then(v.scalar_tensor_tensor(nt[:, :], nt[:, :], -0.5, nv[:, :], ALU.mult, ALU.mult))
                then(v.scalar_tensor_tensor(rstd[:, :], nt[:, :], 1.5, rstd[:, :], ALU.add, ALU.mult))
                for k in range(KT):
                    v.scalar_tensor_tensor(dst[:, k, :], x[:, k, :], pcol(gname, k, 1), rstd[:, :], ALU.mult,
                                           ALU.mult).then_inc(ready, 1)

            def add_out(ph, ktiles, unit, first_block):
                st.mark(v.memset(ssq[:, :], 0.0))
                with v.Fori(0, 4) as i:
                    st.enter(i, 4)
                    for b in range(4):
                        v.wait_ge(used, done(ph, i, (b + 1) * ktiles // unit))
                        xb = x[:, ds(4 * i + b, 1), :].rearrange("p a t -> p (a t)")
                        v.tensor_tensor(xb, xb, bank[b % 2][:, 0:T], ALU.add).then_inc(x_added, 1)
                        st.settle()
                        v.wait_ge(sq_ready, after(first_block + 4 * i + b + 1))
                        st.mark(v.tensor_tensor(ssq[:, :], ssq[:, :], sq[:, b % 2, :], ALU.add))
                    st.leave(4)
                st.settle()
                v.tensor_copy(nt[:, 0:1], ssq[:, 0:1]).then_inc(ssq_ready, 1)

            def masked_max(src, mask, dst, out_max):
                for tt, cols in ((0, slice(0, P)), (1, slice(P, 384))):
                    st.mark(v.tensor_tensor_reduce(dst[:, cols], src[:, cols], mask[:, cols], 1.0, -3e38, ALU.add,
                                                   ALU.max, out_max[tt]))

            def normalise(dst, factor):
                for tt, cols in ((0, slice(0, P)), (1, slice(P, 384))):
                    ins = v.tensor_scalar(dst[:, cols], dst[:, cols], factor[tt], None, ALU.mult)
                return ins

            v.wait_ge(par_in, 16)
            lr, li = pcol("lam_re"), pcol("lam_im")
            st.mark(v.memset(s5[:, :, 32:36], 0.0))
            st.mark(v.tensor_scalar(bgh[:, :], pcol("b_glu"), 0.5, None, ALU.mult))
            v.wait_ge(s5_act, after(1))
            st.mark(v.tensor_tensor(s5t[:, 1, :], lr, s5t[:, 0, :], ALU.mult))
            then(v.tensor_tensor(s5t[:, 2, :], li, s5t[:, 0, :], ALU.mult))
            then(v.tensor_scalar(s5t[:, 7, :], s5t[:, 2, :], 1.0 / TWO_PI, ROUND, ALU.mult, ALU.add))
            v.tensor_scalar(s5t[:, 7, :], s5t[:, 7, :], -ROUND, None, ALU.add).then_inc(s5_mid, 1)
            v.wait_ge(s5_mid, after(1))
            then(v.scalar_tensor_tensor(s5t[:, 3, :], s5t[:, 7, :], -TWO_PI_HI, s5t[:, 2, :], ALU.mult, ALU.add))
            then(v.scalar_tensor_tensor(s5t[:, 3, :], s5t[:, 7, :], -TWO_PI_LO, s5t[:, 3, :], ALU.mult, ALU.add))
            then(v.tensor_scalar(s5t[:, 3, :], s5t[:, 3, :], PI_IN, -PI_IN, ALU.min, ALU.max))
            then(v.scalar_tensor_tensor(s5t[:, 4, :], s5t[:, 3, :], -1.0, s5t[:, 3, :], ALU.mult, ALU.max))
            v.tensor_scalar(s5t[:, 4, :], s5t[:, 4, :], -1.0, math.pi / 2, ALU.mult, ALU.add).then_inc(s5_mid, 1)
            rgv = pcol("rg").rearrange("p (n f) -> p n f", f=8)
            lam = rgv[:, :, RG_COLS["lam"]]
            st.mark(v.scalar_tensor_tensor(rgt[:, 0, :], lam, -1.0, lam, ALU.mult, ALU.max))
            v.tensor_tensor(lbt[:, 0, :], pcol("lb"), pcol("lb"), ALU.subtract).then_inc(sp_in, 1)
            st.mark(v.tensor_scalar(rgt[:, 5, :], lam, -1.0, 0.0, ALU.mult, ALU.max))
            st.mark(v.tensor_scalar(rgv[:, :, RG_COLS["ba"]], rgv[:, :, RG_COLS["ba"]], -1.0, None, ALU.mult))
            st.mark(v.tensor_scalar(rgv[:, :, RG_COLS["bi"]], rgv[:, :, RG_COLS["bi"]], 0.5, None, ALU.mult))
            v.wait_ge(s5_act, after(3))
            decay = s5[:, 0, 0:32]
            st.mark(v.tensor_scalar(s5[:, 1, 0:32], s5t[:, 3, :], 1.0 / TWO_PI, None, ALU.mult))
            st.mark(v.tensor_tensor(s5t[:, 8, :], decay, s5t[:, 6, :], ALU.mult))
            st.mark(v.tensor_tensor(s5t[:, 9, :], decay, s5t[:, 5, :], ALU.mult))
            st.mark(v.tensor_tensor(s5t[:, 10, :], lr, lr, ALU.mult))
            then(v.tensor_tensor(s5t[:, 11, :], li, li, ALU.mult))
            st.mark(v.tensor_scalar(s5t[:, 8, :], s5t[:, 8, :], -1.0, None, ALU.add))
            then(v.tensor_tensor(s5t[:, 10, :], s5t[:, 10, :], s5t[:, 11, :], ALU.add))
            then(v.reciprocal(s5t[:, 10, :], s5t[:, 10, :]))
            for n, (first, second, op) in enumerate(((8, 9, ALU.add), (9, 8, ALU.subtract))):
                st.mark(v.tensor_tensor(s5t[:, 11, :], s5t[:, first, :], lr, ALU.mult))
                then(v.tensor_tensor(s5t[:, 7, :], s5t[:, second, :], li, ALU.mult))
                then(v.tensor_tensor(s5t[:, 11, :], s5t[:, 11, :], s5t[:, 7, :], op))
                then(v.tensor_tensor(s5[:, 2 + n, 0:32], s5t[:, 11, :], s5t[:, 10, :], ALU.mult))
            v.wait_ge(sp_exp, after(1))
            then(v.tensor_scalar(rgt[:, 2, :], rgt[:, 1, :], 2.0, None, ALU.add))
            then(v.reciprocal(rgt[:, 2, :], rgt[:, 2, :]))
            then(v.tensor_tensor(rgt[:, 2, :], rgt[:, 2, :], rgt[:, 1, :], ALU.mult))
            then(v.tensor_tensor(rgt[:, 3, :], rgt[:, 2, :], rgt[:, 2, :], ALU.mult))
            then(v.tensor_scalar(rgt[:, 4, :], rgt[:, 3, :], 1.0 / 17, None, ALU.mult))
            for odd in (15, 13, 11, 9, 7, 5, 3):
                then(v.scalar_tensor_tensor(rgt[:, 4, :], rgt[:, 4, :], 1.0 / odd, rgt[:, 3, :], ALU.add, ALU.mult))
            then(v.scalar_tensor_tensor(rgt[:, 4, :], rgt[:, 4, :], 1.0, rgt[:, 2, :], ALU.add, ALU.mult))
            then(v.scalar_tensor_tensor(rgt[:, 4, :], rgt[:, 4, :], 2.0, rgt[:, 5, :], ALU.mult, ALU.add))
            st.mark(v.tensor_scalar(lam, rgt[:, 4, :], -8.0, None, ALU.mult))
            then(v.reciprocal(lbt[:, 2, :], lbt[:, 1, :]))
            then(v.tensor_tensor(lbt[:, 1, :], lbt[:, 1, :], lbt[:, 2, :], ALU.mult))
            then(v.tensor_tensor(lbt[:, 0, :], lbt[:, 1, :], lbt[:, 1, :], ALU.subtract))
            st.mark(v.tensor_scalar(lbt[:, 2, :], lbt[:, 0, :], -0.5, 0.5, ALU.mult, ALU.add))
            st.mark(v.tensor_scalar(lbt[:, 3, :], pcol("gain"), 0.5, None, ALU.mult))
            then(v.tensor_scalar(lbt[:, 1, :], lbt[:, 0, :], -1.0, 1.0, ALU.mult, ALU.add))
            v.wait_ge(con_in, 16)
            norm(0, "g_even", h, h_ready)

            def angles(turn, seen):
                y = wide_b[:, 0:4, :]
                arg = wide_a[:, :, :].rearrange("p (t c) n -> p t c n", c=2)
                then(v.tensor_copy(cur[:, 8:12], s5[:, 1, ds(4 * turn, 4)]))
                for t in range(4):
                    st.mark(v.tensor_scalar(y[:, t, :], ccol("time"), cur[:, 8 + t:9 + t], None, ALU.mult))
                v.wait_ge(trig_ready, after(seen))
                st.settle()
                st.mark(v.tensor_scalar(wide_b[:, 4:8, :], y, ROUND, -ROUND, ALU.add, ALU.add))
                then(v.tensor_scalar(arg[:, :, 1, :], y, 0.25, ROUND, ALU.add, ALU.add))
                st.mark(v.tensor_tensor(arg[:, :, 0, :], y, wide_b[:, 4:8, :], ALU.subtract))
                v.scalar_tensor_tensor(arg[:, :, 1, :], arg[:, :, 1, :], -ROUND, y, ALU.add, ALU.subtract)\
                    .then_inc(phase_ready, 1)

            angles(0, 0)
            with v.Fori(0, PAIRS) as i:
                st.enter(i, 48)
                st.mark(v.tensor_copy(cur[:, 0:4], s5[:, 0, ds(4 * i, 4)]))
                then(v.tensor_copy(cur[:, 4:5], pcol("d_skip")[:, ds(i, 1)]))
                v.wait_ge(landed[6], even1.loads[4].land0 + i * even1.loads[4].land_per)
                st.mark(v.memset(ring[64:P, 6, 512 + 192:768], NEG))
                v.memset(ring[64:P, 6, 768 + 192:1024], NEG).then_inc(bias_masked, 1)
                then(v.tensor_copy(cur[:, 12:20].rearrange("p (c t) -> p c t", c=2), s5[:, 2:4, ds(4 * i, 4)]))
                c_mat = ring[:, 6, T:2 * T].rearrange("p (c t n) -> p c t n", c=2, t=4)
                coef = cur[:, 12:20].rearrange("p (c t) -> p c t", c=2)
                for n, (part, by) in enumerate(((0, 0), (1, 1), (0, 1), (1, 0))):
                    st.mark(v.tensor_tensor(c_tmp[:, n, :].rearrange("p (t n) -> p t n", t=4), c_mat[:, part],
                                            coef[:, by, :].unsqueeze(2).to_broadcast([P, 4, 32]), ALU.mult))
                v.wait_ge(y_used, after(i))
                st.settle()
                st.mark(v.tensor_tensor(c_in[:, 0, :], c_tmp[:, 0, :], c_tmp[:, 1, :], ALU.subtract))
                v.tensor_tensor(c_in[:, 1, :], c_tmp[:, 2, :], c_tmp[:, 3, :], ALU.add).then_inc(c_in_ready, 1)
                v.wait_ge(trig_ready, after(i + 1))

                def states(t):
                    v.wait_ge(bu_ready, after(4 * i + t + 1))
                    bu = bank[6][:, :].rearrange("p (c n) -> p c n", c=2)
                    cos = wide_c[:, 2 * t + 1:2 * t + 2, :].to_broadcast([P, 2, T])
                    minus_sin = wide_c[:, 2 * t:2 * t + 1, :].to_broadcast([P, 2, T])
                    st.mark(v.tensor_tensor(w2[:, :, :], bu, cos, ALU.mult))
                    v.tensor_tensor(w3[:, :, :], bu, minus_sin, ALU.mult).then_inc(bu_used, 1)
                    st.settle()
                    v.wait_ge(bu_used, after(4 * i + t + 1))
                    st.mark(v.tensor_tensor(w4[:, 0, :], w2[:, 0, :], w3[:, 1, :], ALU.subtract))
                    then(v.tensor_tensor(w4[:, 1, :], w2[:, 1, :], w3[:, 0, :], ALU.add))
                    for c in range(2):
                        st.mark(v.tensor_tensor_scan(w5[:, c, :], cur[:, t:t + 1].to_broadcast([P, T]), w4[:, c, :],
                                                     0.0, ALU.mult, ALU.add))
                    st.settle()
                    v.wait_ge(state_ready, after(8 * i + 2 * t))
                    st.mark(v.tensor_tensor(w8[:, :, :], w5[:, :, :], cos, ALU.mult))
                    v.tensor_tensor(w9[:, :, :], w5[:, :, :], minus_sin, ALU.mult).then_inc(rot_used, 1)

                states(0)
                states(1)
                for e in range(2):
                    v.wait_ge(s_ready, after(2 * i + e + 1))
                    st.mark(v.tensor_reduce(nmax[:, e, 0:1], bank[2 + e][:, 0:P], AX_X, ALU.max, negate=True))
                    v.tensor_reduce(nmax[:, e, 1:2], bank[2 + e][:, P:384], AX_X, ALU.max, negate=True)\
                        .then_inc(m_ready, 1)
                for e in range(2):
                    v.wait_ge(e_ready, after(2 * i + e + 1))
                    then(v.reciprocal(pinv[:, e, :], psums[:, e, :]))
                    normalise(prob[:, e, :], [pinv[:, e, t:t + 1] for t in range(2)]).then_inc(p_ready, 1)
                v.wait_ge(za_tanh, after(i + 1))
                v.scalar_tensor_tensor(gz[:, :], gate[:, :], 1.0, bank[0][:, 0:T], ALU.add, ALU.mult)\
                    .then_inc(za_used, 1)
                states(2)
                angles(i + 1, i + 1)
                v.wait_ge(zb_tanh, after(i + 1))
                v.scalar_tensor_tensor(mix[:, ds(24 + i, 1), :].rearrange("p a t -> p (a t)"), sq[:, 0, :], 1.0,
                                       bank[1][:, 0:T], ALU.add, ALU.mult).then_inc(zb_used, 1)
                states(3)
                v.wait_ge(za_used, after(i + 1))
                v.wait_ge(o_ready, after(i + 1))
                v.scalar_tensor_tensor(mix[:, ds(i, 1), :].rearrange("p a t -> p (a t)"), bank[5][:, 0:T], 0.5,
                                       gz[:, :], ALU.mult, ALU.mult).then_inc(o_used, 1)
                v.wait_ge(y_ready, after(4 * i + 4))
                v.scalar_tensor_tensor(w4[:, 0, :], uT[:, :], cur[:, 4:5], bank[7][:, 0:T], ALU.mult, ALU.add)\
                    .then_inc(y_used, 1)
                v.wait_ge(y_used, after(i + 1))
                then(v.tensor_tensor(w4[:, 1, :], w4[:, 0, :], w4[:, 0, :], ALU.mult))
                then(v.tensor_scalar(w4[:, 1, :], w4[:, 1, :], GELU_C, 1.0, ALU.mult, ALU.add))
                v.tensor_tensor(w4[:, 1, :], w4[:, 1, :], w4[:, 0, :], ALU.mult).then_inc(gelu_in, 1)
                st.mark(v.tensor_scalar(w5[:, 0, :], w4[:, 0, :], 0.5, None, ALU.mult))
                v.wait_ge(gelu_t, after(i + 1))
                st.settle()
                v.scalar_tensor_tensor(mix[:, ds(16 + i, 1), :].rearrange("p a t -> p (a t)"), sq[:, 1, :], 1.0,
                                       w5[:, 0, :], ALU.add, ALU.mult).then_inc(y_mixed, 1)
                st.leave(PAIRS)
            v.wait_ge(y_mixed, after(PAIRS))
            v.wait_ge(zb_used, after(PAIRS))
            with v.Fori(0, 2) as i:
                st.enter(i, 4)
                for b in range(4):
                    v.wait_ge(glu_t, after(4 * i + b + 1))
                    then(v.scalar_tensor_tensor(w4[:, b % 2, :], sq[:, b % 2, :], 1.0,
                                                mix[:, ds(16 + 4 * i + b, 1), :].rearrange("p a t -> p (a t)"),
                                                ALU.add, ALU.mult))
                    v.scalar_tensor_tensor(mix[:, ds(8 + 4 * i + b, 1), :].rearrange("p a t -> p (a t)"),
                                           w4[:, b % 2, :], 0.25, mix[:, ds(24 + 4 * i + b, 1), :].rearrange("p a t -> p (a t)"),
                                           ALU.mult, ALU.mult).then_inc(glu_mixed, 1)
                st.leave(2)
            add_out(out1, 16, 16, 0)
            norm(1, "g_odd", h, h_ready)
            v.wait_ge(used, done(forget, 0, 1))
            then(v.tensor_scalar(fl[:, 0, :], bank[6][0:HEADS, 0:T], pcol("b_forget")[0:16, :], None, ALU.add))
            v.scalar_tensor_tensor(fl[:, 1, :], fl[:, 0, :], -1.0, fl[:, 0, :], ALU.mult, ALU.max).then_inc(f_in, 1)
            v.wait_ge(f_ln, after(1))
            then(v.tensor_scalar(fl[:, 1, :], fl[:, 0, :], 0.0, None, ALU.min))
            then(v.tensor_tensor(fl[:, 2, :], fl[:, 3, :], fl[:, 1, :], ALU.subtract))
            then(v.tensor_tensor_scan(nc_[:, :], ccol("ones", 0, 1)[0:16, :].to_broadcast([16, T]), fl[:, 2, :], 0.0,
                                      ALU.mult, ALU.add))
            with v.Fori(0, HEADS) as i:
                st.enter(i, 2)
                v.wait_ge(s_ready, after(2 * PAIRS + i))
                v.tensor_scalar(ck[:, :], nc_[:, :], ident[0:16, ds(i, 1)], None, ALU.mult).then_inc(ck_ready, 1)
                v.wait_ge(s_ready, after(2 * PAIRS + i + 1))
                apart(v)
                masked_max(bank[2], ccol("causal"), score[:, 0, :], [stat[:, 0, t, 0:1] for t in range(2)])
                st.settle()
                v.tensor_scalar(nmax[:, 0, :], stat[:, 0, :, 0], -1.0, None, ALU.mult).then_inc(m_ready, 1)
                v.wait_ge(e_ready, after(2 * PAIRS + i + 1))
                v.wait_ge(m_ready, after(2 * PAIRS + i + 1))
                v.reciprocal(pinv[:, 0, :], psums[:, 0, :]).then_inc(f_cum, 1)
                v.wait_ge(f_cum, after(i + 1))
                normalise(prob[:, 0, :], [pinv[:, 0, t:t + 1] for t in range(2)]).then_inc(p_ready, 1)
                v.wait_ge(z_tanh, after(i + 1))
                v.scalar_tensor_tensor(gz[:, :], gate[:, :], 1.0, bank[1][:, 0:T], ALU.add, ALU.mult)\
                    .then_inc(z_used, 1)
                v.wait_ge(z_used, after(i + 1))
                v.wait_ge(o_ready, after(PAIRS + i + 1))
                v.scalar_tensor_tensor(mix[:, ds(i, 1), :].rearrange("p a t -> p (a t)"), bank[5][:, 0:T], 0.5,
                                       gz[:, :], ALU.mult, ALU.mult).then_inc(o_used, 1)
                st.leave(HEADS)
            add_out(out2, 16, 16, 16)
            norm(2, "g_final", x, h_ready)
            norm(3, "g_even2", h, h_ready)
            with v.Fori(0, HEADS) as i:
                kk, qs = w9[:, 0, :], w9[:, 1, :]
                st.enter(i, 27)
                v.wait_ge(used, done(hgrn, i, 1))
                v.tensor_scalar(w2[:, 0, :], bank[0][:, 0:T], -80.0, None, ALU.max).then_inc(hf_in, 1)
                v.wait_ge(h_mixed, after(i))
                st.mark(v.tensor_copy(cur[:, 0:4].unsqueeze(2), lbt[:, :, ds(i, 1)]))
                v.wait_ge(hf_exp, after(i + 1))
                then(v.tensor_scalar(w3[:, 0, :], w2[:, 1, :], 1.0, None, ALU.add))
                then(v.reciprocal(w3[:, 1, :], w3[:, 0, :]))
                st.mark(v.scalar_tensor_tensor(kk, w2[:, 1, :], cur[:, 2:3], w3[:, 1, :], ALU.mult, ALU.mult))
                then(v.tensor_scalar(w5[:, 0, :], w3[:, 1, :], cur[:, 1:2], cur[:, 0:1], ALU.mult, ALU.add))
                st.mark(v.tensor_scalar(w4[:, 0, :], w5[:, 0, :], SPLIT, None, ALU.max))
                v.tensor_scalar(w4[:, 1, :], w5[:, 0, :], SPLIT, TINY, ALU.min, ALU.max).then_inc(hf_split, 1)
                v.wait_ge(hf_ln, after(i + 1))
                then(v.tensor_tensor(w5[:, 0, :], w8[:, 0, :], w8[:, 1, :], ALU.add))
                v.tensor_tensor_scan(w5[:, 1, :], ccol("chunk"), w5[:, 0, :], 0.0, ALU.mult, ALU.add)\
                    .then_inc(hb_ready, 1)
                v.wait_ge(hb_ready, after(i + 1))
                for lv in range(4):
                    for n, ins in enumerate(spans(v, lv)):
                        if (lv, n) != (3, 1):
                            st.mark(ins)
                        else:
                            ins.then_inc(span_low, 1)
                v.wait_ge(hq_tanh, after(i + 1))
                v.scalar_tensor_tensor(qs, gate[:, :], 1.0, bank[1][:, 0:T], ALU.add, ALU.mult).then_inc(hq_used, 1)
                att = small[:, :].rearrange("p (b t) -> p b t", b=2)
                st.mark(v.memset(small[:, :], 0.0))
                st.settle()
                v.wait_ge(hq_used, after(i + 1))
                v.wait_ge(decay_low, after(i + 1))
                for lv in range(4):
                    m = 1 << lv
                    for c, src in ((0, kk), (1, qs)):
                        dv = wide_b[:, lv, :].rearrange("p (n c m) -> p n c m", c=2, m=m)[:, :, c, :]
                        sv = src.rearrange("p (n c m) -> p n c m", c=2, m=m)[:, :, c, :]
                        ins = v.tensor_tensor(dv, dv, sv, ALU.mult)
                        if (lv, c) != (3, 1):
                            st.mark(ins)
                        else:
                            ins.then_inc(w_low, 1)
                for pos, lv in enumerate(LEVEL_ORDER):
                    v.wait_ge(lv_used, after(8 * i + pos))
                    v.wait_ge(lv_ready, after(8 * i + pos + 1))
                    apart(v)
                    src = bank[LEVEL_BANKS[pos % 4]][:, 0:T].rearrange("p (b t) -> p b t", b=2)
                    mask = ccol("level", lv * P, P).bitcast(U32).unsqueeze(1).to_broadcast([P, 2, P])
                    v.copy_predicated(att, mask, src).then_inc(lv_used, 1)
                v.wait_ge(ho_guess, after(i + 1))
                y, r = stat[:, 2, :, 0], stat[:, 3, :, 0]
                st.mark(v.tensor_scalar(stat[:, 1, :, 1], stat[:, 0, :, 0], 1.0 / P, EPS, ALU.mult, ALU.add))
                then(v.tensor_tensor(r, y, y, ALU.mult))
                then(v.tensor_tensor(r, r, stat[:, 1, :, 1], ALU.mult))
                then(v.tensor_scalar(r, r, -0.5, 1.5, ALU.mult, ALU.add))
                then(v.tensor_tensor(r, r, y, ALU.mult))
                for tt in range(2):
                    ins = v.tensor_scalar(w6[:, 0, 0, tt * P:(tt + 1) * P], bank[5][:, tt * P:(tt + 1) * P],
                                          stat[:, 3, tt, 0:1], None, ALU.mult)
                ins.then_inc(ho_norm, 1)
                v.wait_ge(hg_tanh, after(i + 1))
                v.scalar_tensor_tensor(gz[:, :], gate[:, :], 1.0, bank[1][:, 0:T], ALU.add, ALU.mult)\
                    .then_inc(hg_used, 1)
                v.wait_ge(hg_used, after(i + 1))
                v.wait_ge(ht_ready, after(i + 1))
                v.scalar_tensor_tensor(mix[:, ds(i, 1), :].rearrange("p a t -> p (a t)"), bank[4][:, 0:T],
                                       cur[:, 3:4], gz[:, :], ALU.mult, ALU.mult).then_inc(h_mixed, 1)
                st.leave(HEADS)
            v.wait_ge(gate_exp, after(1))
            then(v.tensor_scalar(w2[:, 0, 0:96], w2[:, 0, 0:96], 1.0, None, ALU.add))
            then(v.reciprocal(gates_sb[:, :, :].rearrange("p a n -> p (a n)"), w2[:, 0, 0:96]))
            v.wait_ge(ckv_ready, after(2 * GROUPS))
            for n, (dst, pe_name) in enumerate(((wide_a, "pe_k"), (wide_c, "pe_v"))):
                base = wide_b[:, 4 * n, 0:1]
                windows = bass.AP(base.tensor, base.offset, [base.ap[0], [1, CMP_LEN], [T, GROUPS],
                                                             [CMP_STRIDE, NCMP]])
                blocks = dst[:, :, :].rearrange("p k t -> p (k t)")[:, 0:CMP_LEN * GROUPS * NCMP]\
                    .rearrange("p (l g n) -> p l g n", l=CMP_LEN, g=GROUPS)
                v.tensor_tensor(blocks, windows,
                                pcol(pe_name).unsqueeze(2).unsqueeze(3).to_broadcast([P, CMP_LEN, GROUPS, NCMP]),
                                ALU.add).then_inc(cblk_ready, 1)
            for n in range(2):
                v.wait_ge(c_tanh, after(n + 1))
                then(v.scalar_tensor_tensor(w4[:, n, 0:60], w3[:, n, 0:60], 1.0, bank[2 + n][:, 0:60], ALU.add,
                                            ALU.mult))
                v.tensor_scalar(w2[:, n, 0:60], w4[:, n, 0:60], 0.5, None, ALU.mult).then_inc(c_silu, 1)
            s_base, g_base, o_base = 2 * PAIRS + HEADS, HEADS, PAIRS + HEADS
            with v.Fori(0, GROUPS) as i:
                st.enter(i, 45)
                st.mark(v.tensor_copy(gcur[:, :, :], gates_sb[:, :, ds(3 * HPG * i, 3 * HPG)]))
                for e in range(HPG):
                    n = 4 * i + e
                    v.wait_ge(near_ready, after(2 * n + 2))
                    v.wait_ge(s_ready, after(s_base + n + 1))
                    apart(v)
                    for tt in range(2):
                        st.mark(v.tensor_tensor_reduce(score_c[:, tt, :], bank[6][:, tt * NCMP:(tt + 1) * NCMP],
                                                       near_c[:, tt, :], 1.0, -3e38, ALU.add, ALU.max,
                                                       stat[:, 0, tt, 0:1]))
                    masked_max(bank[2], near, score[:, 0, :], [stat[:, 0, t, 1:2] for t in range(2)])
                    masked_max(bank[3], near, score[:, 1, :], [stat[:, 0, t, 2:3] for t in range(2)])
                    st.settle()
                    v.tensor_scalar(stat[:, 1, :, :], stat[:, 0, :, :], -1.0, None, ALU.mult).then_inc(m_ready, 1)
                    v.wait_ge(e_ready, after(s_base + n + 1))
                    then(v.reciprocal(stat[:, 3, :, :], stat[:, 2, :, :]))
                    then(v.tensor_tensor(stat[:, 3, :, :], stat[:, 3, :, :], gcur[:, :, 3 * e:3 * e + 3], ALU.mult))
                    for tt in range(2):
                        st.mark(v.scalar_tensor_tensor(prob_c[:, tt, :], prob_c[:, tt, :], stat[:, 3, tt, 0:1],
                                                       ccol("seen_c", tt * NCMP, NCMP), ALU.mult, ALU.mult))
                    st.mark(normalise(prob[:, 0, :], [stat[:, 3, t, 1:2] for t in range(2)]))
                    normalise(prob[:, 1, :], [stat[:, 3, t, 2:3] for t in range(2)]).then_inc(p_ready, 1)
                    v.wait_ge(z_tanh, after(g_base + n + 1))
                    st.settle()
                    v.scalar_tensor_tensor(gz[:, :], gate[:, :], 1.0, bank[1][:, 0:T], ALU.add, ALU.mult)\
                        .then_inc(z_used, 1)
                    v.wait_ge(z_used, after(g_base + n + 1))
                    v.wait_ge(o_ready, after(o_base + n + 1))
                    v.scalar_tensor_tensor(mix[:, ds(16 + n, 1), :].rearrange("p a t -> p (a t)"), bank[5][:, 0:T], 0.5,
                                           gz[:, :], ALU.mult, ALU.mult).then_inc(o_used, 1)
                st.leave(GROUPS)
            add_out(out3, 32, 16, 32)
            norm(4, "g_odd2", h, h_ready)
            st.mark(v.memset(xpad[:, :, 0:4], 0.0))
            with v.Fori(0, RGB) as i:
                st.enter(i, 14)
                v.wait_ge(rg_mixed, after(i))
                then(v.tensor_copy(cur[:, 0:16], pcol("rg")[:, ds(16 * i, 16)]))
                for c in range(2):
                    v.wait_ge(xb_ready, after(2 * i + c + 1))
                    f = 8 * c
                    then(v.tensor_scalar(w2[:, c, :], xpad[:, c, 4:T + 4], cur[:, f + 3:f + 4],
                                         cur[:, f + RG_COLS["b"]:f + RG_COLS["b"] + 1], ALU.mult, ALU.add))
                    for j in (2, 1, 0):
                        ins = v.scalar_tensor_tensor(w2[:, c, :], xpad[:, c, j + 1:j + 1 + T], cur[:, f + j:f + j + 1],
                                                     w2[:, c, :], ALU.mult, ALU.add)
                        if j:
                            then(ins)
                        else:
                            ins.then_inc(xc_ready, 1)
                v.wait_ge(rg_pre, after(i + 1))
                then(v.tensor_scalar(w3[:, :, :], w3[:, :, :], 1.0, None, ALU.add))
                v.reciprocal(w5[:, :, :], w3[:, :, :]).then_inc(rg_r, 1)
                v.wait_ge(xc_ready, after(2 * i + 2))
                st.mark(v.scalar_tensor_tensor(w4[:, :, :], w4[:, :, :], 1.0, w2[:, :, :], ALU.add, ALU.mult))
                v.wait_ge(rg_a, after(i + 1))
                v.wait_ge(rg_r, after(i + 1))
                then(v.tensor_tensor(w3[:, :, :], w8[:, :, :], w8[:, :, :], ALU.mult))
                then(v.scalar_tensor_tensor(w3[:, :, :], w3[:, :, :], 1.0, w9[:, :, :], ALU.add, ALU.mult))
                v.tensor_scalar(w3[:, :, :], w3[:, :, :], -1.0, 0.0, ALU.mult, ALU.max).then_inc(rg_v, 1)
                v.wait_ge(rg_s, after(i + 1))
                then(v.tensor_tensor(w4[:, :, :], w4[:, :, :], w6[:, 0, :, :], ALU.mult))
                for c in range(2):
                    st.mark(v.tensor_tensor_scan(wide_b[:, c, :], w8[:, c, :], w4[:, c, :], 0.0, ALU.mult, ALU.add))
                v.wait_ge(rgg_tanh, after(i + 1))
                v.scalar_tensor_tensor(wide_c[:, 0:2, :], wide_a[:, 0:2, :], 1.0,
                                       psum[:, 4:6, 0:T], ALU.add, ALU.mult)\
                    .then_inc(rgg_used, 1)
                st.settle()
                v.wait_ge(rgg_used, after(i + 1))
                v.scalar_tensor_tensor(mix[:, ds(2 * i, 2), :], wide_b[:, 0:2, :], 0.5, wide_c[:, 0:2, :], ALU.mult,
                                       ALU.mult).then_inc(rg_mixed, 1)
                st.leave(RGB)
            add_out(out4, 20, 4, 48)
            norm(5, "g_final2", x, x_final)


INPUTS = ("xT", "params", "consts", "rel", "s5_bc", "w_even1", "w_glu", "w_out1", "w_forget", "w_odd1", "w_out2",
          "w_hgrn", "w_gates", "w_cmp_in", "w_cmp1", "w_cmp2", "w_nsa", "w_out3", "w_rg", "w_rgg", "w_out4")


def shape_constants():
    c = np.zeros((P, N_CONSTS), np.float32)

    def put(name, value):
        at, width = CONSTS[name]
        c[:, at:at + width] = value

    put("half_pi", math.pi / 2)
    put("ident", np.eye(P))
    put("flip", np.eye(P)[::-1])
    put("ones", 1.0)
    q = np.arange(P)[:, None]
    far = np.concatenate([q - np.arange(P)[None, :], P + q - np.arange(T)[None, :]], 1)
    put("alibi", np.where(far >= 0, -far, FAR))
    put("causal", np.where(far >= 0, 0.0, NEG))
    last = CMP_STRIDE * np.arange(NCMP)[None, :] + CMP_LEN - 1
    far = np.concatenate([q - last, P + q - last], 1)
    put("alibi_c", np.where(far >= 0, -far, FAR))
    put("seen_c", far >= 0)
    put("slopes", 2.0 ** (-8.0 * np.arange(1, HEADS + 1) / HEADS))
    put("time", np.arange(T))
    key, query = np.arange(P)[:, None], np.arange(P)[None, :]
    levels = []
    for lv in range(LEVELS):
        m = 1 << lv
        levels.append((key // (2 * m) == query // (2 * m)) & (key // m % 2 == 0) & (query // m % 2 == 1))
    levels.append(key == query)
    put("level", np.concatenate(levels, 1))
    put("chunk", np.arange(T) % CHUNK != 0)
    put("eps", EPS)
    return c


def lay_out(i):
    def col(v, width):
        return np.reshape(v, (width, P)).T

    def cut(w, first, width=P):
        b = w[:, first:first + width]
        return b.reshape(-1, P, width).transpose(1, 0, 2).reshape(P, -1)

    def series(w, firsts):
        return np.stack([np.stack([cut(w, f) for f in turn]) for turn in firsts])

    def packed(w, blocks, ktiles, turns):
        b = np.stack([cut(w, P * n) for n in range(blocks)])
        b = b.reshape(turns, blocks // turns, P, ktiles, P).transpose(0, 1, 3, 2, 4)
        b = b.reshape(turns, -1, TILES, P, P).transpose(0, 1, 3, 2, 4)
        return np.ascontiguousarray(b.reshape(turns, -1, P, TILES * P))

    par = np.zeros((P, N_PARAMS), np.float32)

    def put(name, value):
        at, width = PARAMS[name]
        par[:, at:at + width] = value

    put("g_even", col(i["norm_even_g"][0], KT))
    put("g_odd", col(i["norm_odd_g"][0], KT))
    put("g_final", col(i["final_norm_g"], KT))
    put("g_even2", col(i["norm_w_2"][0], KT))
    put("g_odd2", col(i["norm_w_2"][1], KT))
    put("g_final2", col(i["final_norm_w_2"], KT))
    put("lam_re", col(i["s5_lambda_re"][0], 32))
    put("lam_im", col(i["s5_lambda_im"][0], 32))
    put("log_dt", col(np.repeat(i["s5_log_dt"][0], 64), 32))
    put("d_skip", col(i["s5_d"][0], PAIRS))
    put("b_glu", col(i["b_glu"][0], PAIRS))
    par[0:HEADS, PARAMS["b_forget"][0]] = i["b_forget"][0]
    put("lb", col(i["hgrn_lb_logits_2"][0], HEADS))
    put("gain", col(i["hgrn_norm_w_2"][0], HEADS))
    put("pe_k", i["cmp_pe_k_2"][0].T)
    put("pe_v", i["cmp_pe_v_2"][0].T)
    rgp = np.stack([*i["rg_conv_w_2"][0], i["rg_conv_b_2"][0], i["rg_b_a_2"][0], i["rg_b_i_2"][0],
                    i["rg_lambda_2"][0]])
    put("rg", rgp.reshape(8, RGB * 2, P).transpose(2, 1, 0).reshape(P, -1))

    rb = i["rel_bias"][0][:, ::-1]
    reach = rb.shape[1] // 2
    rev = np.concatenate([np.repeat(rb[:, :1], T - 1 - reach, 1), rb, np.repeat(rb[:, -1:], T - 1 - reach, 1)], 1)
    rel = np.stack([rev[:, p:p + T] for p in range(P)], 1)

    bc = np.zeros((PAIRS, P, 4, P), np.float32)
    for turn in range(PAIRS):
        for gl in range(8):
            g, t, e = 8 * turn + gl, gl // 2, gl % 2
            rows, states, chans = slice(16 * gl, 16 * gl + 16), slice(64 * e, 64 * e + 64), slice(16 * gl, 16 * gl + 16)
            bc[turn, rows, 0, states] = i["s5_b_re"][0, g].T
            bc[turn, rows, 1, states] = i["s5_b_im"][0, g].T
            bc[turn, states, 2, chans] = i["s5_c_re"][0, g].T
            bc[turn, states, 3, chans] = i["s5_c_im"][0, g].T

    we, wo, w2 = i["w_in_even"][0], i["w_in_odd"][0], i["even_w_in_2"][0]
    out = dict(
        xT=np.ascontiguousarray(i["x"][0].T).reshape(KT, P, T), params=par, consts=shape_constants(),
        rel=np.ascontiguousarray(rel), s5_bc=bc.reshape(PAIRS, P, 4 * P),
        w_even1=series(we, [[3072 + P * n, P * n, 1024 + P * n, 2048 + P * n, 4096 + P * n, 5120 + P * n]
                            for n in range(PAIRS)]),
        w_glu=packed(i["w_glu"][0], 8, 8, 2),
        w_out1=packed(i["w_out_even"][0], 16, 16, 4),
        w_forget=cut(wo, 8192, HEADS)[None, None],
        w_odd1=series(wo, [[D * m + P * n for m in range(4)] for n in range(HEADS)]),
        w_out2=packed(i["w_out_odd"][0], 16, 16, 4),
        w_hgrn=series(w2, [[2048 + P * n, P * n, 4096 + P * n, 6144 + P * n] for n in range(HEADS)]),
        w_gates=cut(w2, 13312, 48)[None, None],
        w_cmp_in=series(w2, [[10240 + P * n, 10752 + P * n] for n in range(GROUPS)]),
        w_cmp1=np.stack([i[f"cmp_w1_{c}_2"][0].reshape(2, TILES, P, P)[half].transpose(1, 0, 2).reshape(P, -1)
                         for c in "kv" for half in range(2)])[None],
        w_cmp2=np.concatenate([i["cmp_w2_k_2"][0], i["cmp_w2_v_2"][0]], 1)[None, None],
        w_nsa=series(w2, [[11264 + P * n, 11776 + P * n, 12288 + P * n, 12800 + P * n] +
                          [f + P * (HPG * n + e) for e in range(HPG) for f in (8192, 13360)]
                          for n in range(GROUPS)]),
        w_out3=packed(i["even_w_out_2"][0], 16, 32, 4),
        w_rg=series(i["odd_w_in_2"][0], [[256 * n, 256 * n + P, 2560 + 256 * n, 2560 + 256 * n + P]
                                         for n in range(RGB)]),
        w_rgg=np.stack([i["rg_w_a_2"][0], i["rg_w_i_2"][0]], 1)
        .reshape(RGB, 2, 2, P, 2, P).transpose(0, 3, 1, 4, 2, 5).reshape(RGB, 1, P, 8 * P),
        w_out4=packed(i["odd_w_out_2"][0], 16, 20, 4),
    )
    return {k: np.ascontiguousarray(v) for k, v in out.items()}


def kernel(**inputs):
    import concourse.bacc as bacc
    from concourse.bass_utils import run_bass_kernel_spmd

    nc = bacc.Bacc("TRN2", target_bir_lowering=False, num_devices=1)
    arrays = lay_out({k: np.asarray(v) for k, v in inputs.items()})
    a = {n: nc.dram_tensor(n, arrays[n].shape, F32, kind="ExternalInput").ap() for n in INPUTS}
    out = nc.dram_tensor("yT", (KT, P, T), F32, kind="ExternalOutput").ap()
    program(nc, a, out)
    r = run_bass_kernel_spmd(nc, [arrays], core_ids=[0])
    return np.ascontiguousarray(r.results[0]["yT"].reshape(D, T).T)[None]
```
